# Optimizing a Trainium2 kernel written in Bass

```python
import math
import jax, jax.numpy as jnp
from jax import lax
import numpy as np

D_MODEL = 2048
BATCH = 1
SEQ = 256
DEPTH = 1

CHUNK = 64
D_MIX = D_MODEL
HEAD_DIM = 128
LRU_HEADS = 6
D_LRU = LRU_HEADS * HEAD_DIM
CONV_A = 4
LRU_C = 8.0
CONV_GROUPS = 4
D_CONV = CONV_GROUPS * HEAD_DIM
CONV_B = 3
SB_HEADS = 6
D_SB = SB_HEADS * HEAD_DIM
Q_BLOCK = 128
IN_SPLIT_SIZES = (D_LRU, D_LRU, D_CONV, D_CONV, D_CONV, D_SB, D_SB, D_SB)
D_IN = 2 * D_LRU + 3 * D_CONV + 3 * D_SB
N_GROUPS = 4
EXPERTS_PER_GROUP = 8
N_EXPERTS = N_GROUPS * EXPERTS_PER_GROUP
TOP_K = 2
D_EXPERT = 512
ROW_BLOCK = 128
EPS = 1e-6

kernel_name = 'hymba_style_rglru_shortconv_stickbreak_hiermoe'

def rmsnorm(x, g):
    xf = x.astype(jnp.float32)
    y = xf * lax.rsqrt(jnp.mean(xf * xf, axis=-1, keepdims=True) + EPS)
    return (y * g.astype(jnp.float32)).astype(x.dtype)

def causal_depthwise_conv(x, w):
    k = w.shape[0]
    return lax.conv_general_dilated(x, w[:, None, :].astype(x.dtype), window_strides=(1,),
                                    padding=[(k - 1, 0)],
                                    dimension_numbers=('NWC', 'WIO', 'NWC'),
                                    feature_group_count=x.shape[-1])

def _linear_combine(c1, c2):
    a1, b1 = c1
    a2, b2 = c2
    return a1 * a2, a2 * b1 + b2

def rg_lru(x, w_a, b_a, w_x, b_x, lam):
    bsz, s, _ = x.shape
    xf = x.astype(jnp.float32)
    xh = xf.reshape(bsz, s, LRU_HEADS, HEAD_DIM)
    r = jax.nn.sigmoid(jnp.einsum('bshi,hij->bshj', xh, w_a.astype(jnp.float32)).reshape(bsz, s, D_LRU)
                       + b_a.astype(jnp.float32))
    i = jax.nn.sigmoid(jnp.einsum('bshi,hij->bshj', xh, w_x.astype(jnp.float32)).reshape(bsz, s, D_LRU)
                       + b_x.astype(jnp.float32))
    log_a = -LRU_C * r * jax.nn.softplus(-lam.astype(jnp.float32))
    a = jnp.exp(log_a)
    u = jnp.sqrt(-jnp.expm1(2.0 * log_a)) * (i * xf)
    _, h = lax.associative_scan(_linear_combine, (a, u), axis=1)
    return h.astype(x.dtype)

def stick_breaking_attention(q, k, v):
    s_len = q.shape[2]
    scale = 1.0 / math.sqrt(HEAD_DIM)
    outs = []
    for blk in range(s_len // Q_BLOCK):
        start = blk * Q_BLOCK
        end = start + Q_BLOCK
        qb = q[:, :, start:end]
        kb = k[:, :, :end]
        vb = v[:, :, :end]
        z = jnp.einsum('bhqd,bhkd->bhqk', qb, kb) * scale
        t_pos = start + jnp.arange(Q_BLOCK)[:, None]
        s_pos = jnp.arange(end)[None, :]
        mask = s_pos < t_pos
        log_keep = jnp.where(mask, jax.nn.log_sigmoid(-z), 0.0)
        suffix = lax.cumsum(log_keep, axis=3, reverse=True) - log_keep
        w = jnp.where(mask, jnp.exp(jax.nn.log_sigmoid(z) + suffix), 0.0)
        outs.append(jnp.einsum('bhqk,bhkd->bhqd', w, vb))
    return jnp.concatenate(outs, axis=2)

def hierarchical_moe(h, w_rg, b_rg, w_re, b_re, w_gate, w_up, w_down):
    bsz, s, d = h.shape
    t = bsz * s
    xt = h.reshape(t, d)
    grp_logits = (xt @ w_rg).astype(jnp.float32) + b_rg.astype(jnp.float32)
    grp_prob = jax.nn.softmax(grp_logits, axis=-1)
    g_idx = jnp.argmax(grp_logits, axis=-1)
    p_g = jnp.take_along_axis(grp_prob, g_idx[:, None], axis=-1)[:, 0]
    exp_logits = ((xt @ w_re).astype(jnp.float32) + b_re.astype(jnp.float32)).reshape(t, N_GROUPS, EXPERTS_PER_GROUP)
    in_grp = jnp.take_along_axis(exp_logits, g_idx[:, None, None], axis=1)[:, 0]
    top_p, top_i = lax.top_k(jax.nn.softmax(in_grp, axis=-1), TOP_K)
    top_p = top_p / jnp.sum(top_p, axis=-1, keepdims=True)
    gates = p_g[:, None] * top_p
    expert_ids = g_idx[:, None] * EXPERTS_PER_GROUP + top_i

    tk = t * TOP_K
    flat_e = expert_ids.reshape(tk).astype(jnp.int32)
    flat_g = gates.reshape(tk)
    flat_tok = jnp.repeat(jnp.arange(t, dtype=jnp.int32), TOP_K)
    order = jnp.argsort(flat_e)
    e_sorted = flat_e[order]
    tok_sorted = flat_tok[order]
    g_sorted = flat_g[order]
    counts = jnp.zeros((N_EXPERTS,), jnp.int32).at[flat_e].add(1)
    padded = (counts + ROW_BLOCK - 1) // ROW_BLOCK * ROW_BLOCK
    starts = jnp.cumsum(counts) - counts
    pends = jnp.cumsum(padded)
    pstarts = pends - padded
    dest = pstarts[e_sorted] + (jnp.arange(tk, dtype=jnp.int32) - starts[e_sorted])
    n_blocks = -(-tk // ROW_BLOCK) + N_EXPERTS
    rows = n_blocks * ROW_BLOCK
    x_pad = jnp.zeros((rows, d), xt.dtype).at[dest].set(xt[tok_sorted])
    tok_pad = jnp.full((rows,), t, jnp.int32).at[dest].set(tok_sorted)
    gate_pad = jnp.zeros((rows,), jnp.float32).at[dest].set(g_sorted)
    block_start = jnp.arange(n_blocks, dtype=jnp.int32) * ROW_BLOCK
    block_expert = jnp.minimum(jnp.searchsorted(pends, block_start, side='right'), N_EXPERTS - 1)

    def expert_block(args):
        xb, e = args
        hid = jax.nn.silu(xb @ w_gate[e]) * (xb @ w_up[e])
        return hid @ w_down[e]

    y_pad = lax.map(expert_block, (x_pad.reshape(n_blocks, ROW_BLOCK, d), block_expert))
    y_pad = y_pad.reshape(rows, d) * gate_pad[:, None].astype(y_pad.dtype)
    out = jax.ops.segment_sum(y_pad, tok_pad, num_segments=t + 1)[:t]
    return out.reshape(bsz, s, d)

def setup_inputs(seed: int = 0) -> dict:
    key = jax.random.key(seed)
    ks = jax.random.split(key, 24)
    f32 = jnp.float32
    nrm = lambda k, shape, sc: jax.random.normal(k, shape, f32) * sc
    u = jax.random.uniform(ks[9], (DEPTH, D_LRU), f32, minval=0.9, maxval=0.999)
    sig = u ** (1.0 / LRU_C)
    lam = jnp.log(sig) - jnp.log1p(-sig)
    return {
        'x': jax.random.normal(ks[0], (BATCH, SEQ, D_MODEL), f32),
        'norm_mix': 1.0 + nrm(ks[1], (DEPTH, D_MODEL), 0.1),
        'w_in': nrm(ks[2], (DEPTH, D_MODEL, D_IN), D_MODEL ** -0.5),
        'conv_a_w': nrm(ks[3], (DEPTH, CONV_A, D_LRU), CONV_A ** -0.5),
        'conv_a_b': nrm(ks[4], (DEPTH, D_LRU), 0.02),
        'lru_wa': nrm(ks[5], (DEPTH, LRU_HEADS, HEAD_DIM, HEAD_DIM), HEAD_DIM ** -0.5),
        'lru_ba': nrm(ks[6], (DEPTH, D_LRU), 0.02),
        'lru_wx': nrm(ks[7], (DEPTH, LRU_HEADS, HEAD_DIM, HEAD_DIM), HEAD_DIM ** -0.5),
        'lru_bx': nrm(ks[8], (DEPTH, D_LRU), 0.02),
        'lru_lam': lam,
        'conv_b_w': nrm(ks[10], (DEPTH, CONV_B, D_CONV), CONV_B ** -0.5),
        'q_norm': 1.0 + nrm(ks[11], (DEPTH, HEAD_DIM), 0.1),
        'k_norm': 1.0 + nrm(ks[12], (DEPTH, HEAD_DIM), 0.1),
        'mix_norm': 1.0 + nrm(ks[13], (DEPTH, D_MIX), 0.1),
        'w_out': nrm(ks[14], (DEPTH, D_MIX, D_MODEL), D_MIX ** -0.5),
        'norm_ffn': 1.0 + nrm(ks[15], (DEPTH, D_MODEL), 0.1),
        'w_router_group': nrm(ks[16], (DEPTH, D_MODEL, N_GROUPS), D_MODEL ** -0.5),
        'b_router_group': nrm(ks[17], (DEPTH, N_GROUPS), 0.01),
        'w_router_expert': nrm(ks[18], (DEPTH, D_MODEL, N_EXPERTS), D_MODEL ** -0.5),
        'b_router_expert': nrm(ks[19], (DEPTH, N_EXPERTS), 0.01),
        'w_gate': nrm(ks[20], (DEPTH, N_EXPERTS, D_MODEL, D_EXPERT), D_MODEL ** -0.5),
        'w_up': nrm(ks[21], (DEPTH, N_EXPERTS, D_MODEL, D_EXPERT), D_MODEL ** -0.5),
        'w_down': nrm(ks[22], (DEPTH, N_EXPERTS, D_EXPERT, D_MODEL), D_EXPERT ** -0.5),
    }

def reference(x, norm_mix, w_in, conv_a_w, conv_a_b, lru_wa, lru_ba, lru_wx, lru_bx, lru_lam,
              conv_b_w, q_norm, k_norm, mix_norm, w_out, norm_ffn, w_router_group, b_router_group,
              w_router_expert, b_router_expert, w_gate, w_up, w_down):
    bsz, s, _ = x.shape
    split_idx = [int(c) for c in np.cumsum(IN_SPLIT_SIZES)[:-1]]
    for l in range(DEPTH):
        h = rmsnorm(x, norm_mix[l])
        proj = h @ w_in[l]
        xa, ga, bg, cg, xb, q, k, v = jnp.split(proj, split_idx, axis=-1)
        xa = causal_depthwise_conv(xa, conv_a_w[l]) + conv_a_b[l].astype(xa.dtype)
        ya = rg_lru(xa, lru_wa[l], lru_ba[l], lru_wx[l], lru_bx[l], lru_lam[l]) * jax.nn.gelu(ga)
        yb = bg * causal_depthwise_conv(cg * xb, conv_b_w[l])
        to_heads = lambda z: z.reshape(bsz, s, SB_HEADS, HEAD_DIM).transpose(0, 2, 1, 3).astype(jnp.float32)
        qh = to_heads(rmsnorm(q.reshape(bsz, s, SB_HEADS, HEAD_DIM), q_norm[l]))
        kh = to_heads(rmsnorm(k.reshape(bsz, s, SB_HEADS, HEAD_DIM), k_norm[l]))
        vh = to_heads(v)
        yc = stick_breaking_attention(qh, kh, vh).transpose(0, 2, 1, 3).reshape(bsz, s, D_SB).astype(x.dtype)
        y = jnp.concatenate([ya, yb, yc], axis=-1)
        y = rmsnorm(y.reshape(bsz, s, D_MIX // HEAD_DIM, HEAD_DIM), jnp.ones((HEAD_DIM,), jnp.float32))
        y = y.reshape(bsz, s, D_MIX) * mix_norm[l].astype(y.dtype)
        x = x + y @ w_out[l]
        h2 = rmsnorm(x, norm_ffn[l])
        x = x + hierarchical_moe(h2, w_router_group[l], b_router_group[l], w_router_expert[l],
                                 b_router_expert[l], w_gate[l], w_up[l], w_down[l])
    return x


_drawn_inputs = setup_inputs


def setup_inputs(seed=0):
    import zlib

    import numpy as np

    out = dict(_drawn_inputs(seed))
    spreads = {}
    factors = {'lru_ba': 8.0, 'lru_bx': 8.0, 'b_router_group': 8.0, 'b_router_expert': 4.225}
    for name, (base, spread) in spreads.items():
        noise = np.random.default_rng([zlib.crc32(name.encode()), seed]).standard_normal(out[name].shape)
        drawn = base * np.exp(spread * noise) if base else spread * noise
        out[name] = __import__('jax').numpy.asarray(drawn.astype(out[name].dtype))
    for name, factor in factors.items():
        out[name] = (out[name] * factor).astype(out[name].dtype)
    return out
```

```python
from contextlib import ExitStack

import numpy as np

import concourse.bass as bass
from concourse import mybir

F32 = mybir.dt.float32
F32R = mybir.dt.float32r
BF16 = mybir.dt.bfloat16
I32 = mybir.dt.int32
ALU = mybir.AluOpType
ACT = mybir.ActivationFunctionType
AX = mybir.AxisListType.X

P = 128
EPS = 1e-6
MASKED = -1e30
LRU_C = 8.0
POLY_BELOW = 0.25


def hymba_layer(nc, x, norm_mix, w_in, conv_a_w, conv_a_b, lru_wa, lru_ba, lru_wx, lru_bx, lru_lam,
                conv_b_w, q_norm, k_norm, mix_norm, w_out, norm_ffn, w_router_group, b_router_group,
                w_router_expert, b_router_expert, w_gate, w_up, w_down, out):
    _, SEQ, D = x.shape
    TILES = SEQ // P
    KC = D // P
    CONV_A, D_LRU = conv_a_w.shape[1:]
    CONV_B, D_CONV = conv_b_w.shape[1:]
    HA, HB = D_LRU // P, D_CONV // P
    HC = (w_in.shape[2] - 2 * D_LRU - 3 * D_CONV) // 3 // P
    NG = w_router_group.shape[2]
    NE = w_router_expert.shape[2]
    EG = NE // NG
    F = w_gate.shape[3]
    FC = F // P
    assert (TILES, KC, FC, HA, HB, HC) == (2, 16, 4, 6, 4, 6)

    PW = 256
    PIECE = KC * PW * 4
    MIX_RING, MOE_RING = 4, 6
    BLK_XA, BLK_GA, BLK_BG = 0, HA, 2 * HA
    BLK_CG, BLK_XB = BLK_BG + HB, BLK_BG + 2 * HB
    BLK_Q = BLK_BG + 3 * HB
    BLK_K, BLK_V = BLK_Q + HC, BLK_Q + 2 * HC
    order = ([(BLK_Q + b) for b in range(0, HC, 2)] + [(BLK_K + b) for b in range(0, HC, 2)]
             + [(BLK_V + b) for b in range(0, HC, 2)] + [(BLK_XA + b) for b in range(0, HA, 2)]
             + [(BLK_GA + b) for b in range(0, HA, 2)] + [(BLK_XB + b) for b in range(0, HB, 2)]
             + [(BLK_CG + b) for b in range(0, HB, 2)] + [(BLK_BG + b) for b in range(0, HB, 2)])
    N_IN = len(order)
    N_OUT = D // PW
    N_MIX = N_IN + N_OUT
    S_V, S_XA, S_GA, S_XB = 6, 9, 12, 15
    T_USES = 4

    SLOTS = 32
    QI = 4
    QUADS = NE // QI
    XQ = 4
    NX = XQ * QI
    NI = NE + NX + QI
    H = KC // 2

    x_t = x[0].rearrange("(t p) d -> t p d", p=P)
    out_t = out[0].rearrange("(t p) d -> t p d", p=P)
    w_in_p = w_in[0].rearrange("(p c) n -> p c n", c=KC)
    w_out_p = w_out[0].rearrange("(c p) n -> p c n", p=P)
    w_gate_p = w_gate[0].rearrange("e (p c) f -> e p c f", c=KC)
    w_up_p = w_up[0].rearrange("e (p c) f -> e p c f", c=KC)
    w_down_p = w_down[0].rearrange("e (p c) n -> e p c n", c=FC)

    with ExitStack() as ctx:
        def sem(name):
            return ctx.enter_context(nc.semaphore(name))

        base = 16512

        def at(name, shape, dt, offset):
            return nc.alloc_sbuf_tensor_at(name, [P] + shape, dt, offset=base + offset)

        ring = at("ring", [MOE_RING, KC * PW], F32, 0)
        QB = PIECE // 4
        w_hi = at("w_hi", [4, 4, PW], F32R, MIX_RING * PIECE)
        w_lo = at("w_lo", [4, 4, PW], F32R, (MIX_RING + 1) * PIECE)
        o = MOE_RING * PIECE
        x_acc = at("x_acc", [TILES, D], F32, o)
        conv_a = at("conv_a", [HA, SEQ], F32, o)
        lru_u = at("lru_u", [HA, SEQ], F32, o + HA * SEQ * 4)
        o += TILES * D * 4
        hT_hi = at("hT_hi", [KC, SEQ], F32R, o)
        y_hi = at("y_hi", [KC, SEQ], F32R, o)
        h2T = at("h2T", [KC, SEQ], F32, o)
        o += KC * SEQ * 4
        hT_lo = at("hT_lo", [KC, SEQ], F32R, o)
        y_lo = at("y_lo", [KC, SEQ], F32R, o)
        o += KC * SEQ * 4
        o_proj = o
        h_perm = at("h_perm", [TILES, KC, P], F32, o)
        proj = at("proj", [BLK_V, SEQ], F32, o)
        h2_perm = at("h2_perm", [TILES, KC, P], F32, o)
        x_exp = at("x_exp", [KC, QI * SLOTS], F32, o + 16 * SEQ * 4)
        y_exp = at("y_exp", [D], F32, o + 24 * SEQ * 4)
        lru_w = at("lru_w", [2, HA, P], F32, o + BLK_BG * SEQ * 4)
        scores2 = at("scores2", [2, 2, TILES * P + P], F32, o + BLK_K * SEQ * 4)
        o += BLK_V * SEQ * 4
        v_tok = at("v_tok", [TILES, HC * P], F32, o)
        cross = at("cross", [NX + QI, NE], F32, o)
        match = at("match", [NX + QI, NE], F32, o + (NX + QI) * NE * 4)
        o += TILES * HC * P * 4
        temp = at("temp", [12, SEQ], F32, o)
        lru_a = at("lru_a", [HA, SEQ], F32, o)
        lru_e = at("lru_e", [HA, SEQ], F32, o + HA * SEQ * 4)
        scores0 = at("scores0", [2, 2, TILES * P + P], F32, o)
        scores1 = at("scores1", [2, 2, TILES * P + P], F32, o + 6 * SEQ * 4)
        gate_sb = at("gate_sb", [F], F32, o)
        up_sb = at("up_sb", [F], F32, o + 2048)
        silu_sb = at("silu_sb", [FC, SLOTS], F32, o + 4096)
        hidT = at("hidT", [FC, SLOTS], F32, o + 4608)
        pick = at("pick", [TILES, QI, SLOTS], F32, o + 5120)
        pick_gate = at("pick_gate", [TILES, QI, SLOTS], F32, o + 6144)
        give = at("give", [TILES, P], F32, o + 7168)
        rank_item = at("rank_item", [TILES, NI], F32, o + 8192)
        gate_item = at("gate_item", [TILES, NI], F32, o + 8704)
        small = at("small", [640], F32, o + 9216)
        o += 12 * SEQ * 4
        ident = at("ident", [P], F32, o)
        ones = at("ones", [P], F32, o + 512)
        w_rt = at("w_rt", [KC, NG + NE], F32, o + 1024)
        o += 1024 + KC * (NG + NE) * 4
        before = at("before", [P], BF16, o)
        ones_b = at("ones_b", [P], BF16, o + 256)
        fold = at("fold", [SLOTS], F32, o + 512)
        iota_s = at("iota_s", [SLOTS], F32, o + 640)
        prm_rows = at("prm_rows", [P], F32, o + 768)
        prm = at("prm", [80], F32, o + 1280)
        gain_mix = at("gain_mix", [KC], F32, o + 1600)
        gain_ffn = at("gain_ffn", [KC], F32, o + 1664)
        b_rt = at("b_rt", [NG + NE], F32, o + 1728)
        desc = at("desc", [12], F32, o + 1888)
        iota_e = at("iota_e", [NX + QI + NE], F32, o + 1952)
        tab = at("tab", [2 + NX], I32, o + 2176)
        c_eps = at("c_eps", [1], F32, o + 2272)
        lru_c = at("lru_c", [HA], F32, o + 2304)
        lru_t = at("lru_t", [3, HA], F32, o + 2336)
        ssq = at("ssq", [TILES, 10], F32, o + 2432)
        sel_b = at("sel_b", [TILES, NE], BF16, o + 2528)
        assert base + o + 2688 <= 229344
        scores = [scores0, scores1, scores2]

        R_CA, R_CAB = 0, CONV_A * HA
        R_BA, R_BX, R_LAM = R_CAB + HA, R_CAB + 2 * HA, R_CAB + 3 * HA
        R_CB = R_LAM + HA
        R_MIX = R_CB + CONV_B * HB
        R_Q, R_K = R_MIX + KC, R_MIX + KC + 1
        R_ALL = R_K + 1

        bank = [ctx.enter_context(nc.psum_tensor(f"bank{i}", [P, 512], F32)) for i in range(8)]
        AUX = 4
        b_gate, b_up, b_fold, b_down = bank[0], bank[1], bank[2], bank[3]
        b_gath, b_comb = [bank[4], bank[5]], [bank[6], bank[7]]

        x_in, par_in, router_in = sem("x_in"), sem("par_in"), sem("router_in")
        lru_in, x_again, out_done = sem("lru_in"), sem("x_again"), sem("out_done")
        piece_in = [sem(f"piece_in{i}") for i in range(MOE_RING)]
        consts_ready = sem("consts_ready")
        hi_ready, lo_ready = sem("hi_ready"), sem("lo_ready")
        quarter_used = sem("quarter_used")
        proj_full, proj_free = sem("proj_full"), sem("proj_free")
        aux_full, aux_free = sem("aux_full"), sem("aux_free")
        act_step, dve_step, pool_step = sem("act_step"), sem("dve_step"), sem("pool_step")
        ssq_ready, var_ready, std_ready = sem("ssq_ready"), sem("var_ready"), sem("std_ready")
        h_ready, hT_hi_ready = sem("h_ready"), sem("hT_hi_ready")
        prm_ready = sem("prm_ready")
        lam_abs, lam_exp = sem("lam_abs"), sem("lam_exp")
        qk_sq, qk_ready = sem("qk_sq"), sem("qk_ready")
        conv_ready = sem("conv_ready")
        z_masked, ln_ready = sem("z_masked"), sem("ln_ready")
        logw_ready, w_ready, wT_ready = sem("logw_ready"), sem("w_ready"), sem("wT_ready")
        sig_ready, y2_ready = sem("sig_ready"), sem("y2_ready")
        decay_ready, expm1_ready, root_ready = sem("decay_ready"), sem("expm1_ready"), sem("root_ready")
        gelu_ready, ya_ready = sem("gelu_ready"), sem("ya_ready")
        cx_ready, yb_ready = sem("cx_ready"), sem("yb_ready")
        y_sq, y_std, y_norm, y_split = sem("y_sq"), sem("y_std"), sem("y_norm"), sem("y_split")
        y_hi_ready = sem("y_hi_ready")
        x2_ready, ssq2_ready = sem("x2_ready"), sem("ssq2_ready")
        h2_ready, h2T_full, h2T_free = sem("h2_ready"), sem("h2T_full"), sem("h2T_free")
        logits_full, e_ready, sub_ready = sem("logits_full"), sem("e_ready"), sem("sub_ready")
        sel_ready, rank_full = sem("sel_ready"), sem("rank_full")
        table_ready = sem("table_ready")
        piece_used = sem("piece_used")
        fold_full = sem("fold_full")
        gate_out, up_out = sem("gate_out"), sem("up_out")
        silu_ready, hid_ready = sem("silu_ready"), sem("hid_ready")
        y_out_act, y_out_dve = sem("y_out_act"), sem("y_out_dve")
        comb_full, acc_done = sem("comb_full"), sem("acc_done")
        gath_full, gath_out = sem("gath_full"), sem("gath_out")
        pick_made, pick_ready = sem("pick_made"), sem("pick_ready")
        give_full, give_ready = sem("give_full"), sem("give_ready")

        MOE_PLACE = [(N_MIX + i) % MIX_RING for i in range(MIX_RING)] + [4, 5]
        MIX_USES = [len(range(i, N_MIX, MIX_RING)) for i in range(MIX_RING)] + [0, 0]

        def piece_count(i, item):
            return item * 16 + 16 * (MIX_USES[MOE_PLACE[i]] + 1)

        def piece_source(i, e):
            if i < 4:
                return (w_gate_p, w_up_p)[i % 2][e][:, (i // 2) * H:(i // 2 + 1) * H, :]
            return w_down_p[e][:, (i - 4) * (FC // 2):(i - 3) * (FC // 2), :]

        def place(i):
            return ring[:, MOE_PLACE[i], :]

        U_PRM = 0
        U_QK = 1
        U_Z = U_QK + HC
        U_WT = U_Z + HC
        U_PV = U_WT + HC
        U_LRU = U_PV + HC // 2
        U_YC = U_LRU + HA
        U_YA = U_YC + HC // 2
        U_YB = U_YA + HA // 2
        U_END = U_YB + HB // 2

        def aux(u):
            return bank[AUX + u % 4]

        def proj_bank(n, b):
            return bank[2 * (n % 2) + b]

        def y_block(c):
            return BLK_GA + c if c < HA + HB else BLK_Q + c - HA - HB

        Y_RUNS = {3: [(12, 16)], 2: [(8, 10), (10, 12)], 1: [(4, 8)], 0: [(0, 4)]}
        Y_NEED = {3: 3, 2: 8, 1: 8, 0: 8}

        block = ctx.enter_context(nc.Block())

        @block.sync
        def _(sp):
            for t in range(TILES):
                sp.dma_start(x_acc[:, t, :], x_t[t]).then_inc(x_in, 16)
            for n in range(N_MIX):
                if n >= MIX_RING:
                    sp.wait_ge(lo_ready, 4 * (n - MIX_RING) + 4)
                dst = ring[:, n % MIX_RING, :].rearrange("p (c n) -> p c n", c=KC)
                if n < N_IN:
                    src = w_in_p[:, :, order[n] * P:order[n] * P + PW]
                else:
                    src = w_out_p[:, :, (n - N_IN) * PW:(n - N_IN + 1) * PW]
                sp.dma_start(dst, src).then_inc(piece_in[n % MIX_RING], 16)
                if n == N_IN:
                    sp.wait_ge(ya_ready, 1)
                    for t in range(TILES):
                        sp.dma_start(x_acc[:, t, :], x_t[t]).then_inc(x_again, 16)
            for i in range(MOE_RING):
                if i < MIX_RING:
                    sp.wait_ge(lo_ready, 4 * (N_MIX - MIX_RING + i) + 4)
                else:
                    sp.wait_ge(quarter_used, 4 * N_MIX)
                sp.dma_start(place(i), piece_source(i, 0)).then_inc(piece_in[MOE_PLACE[i]], 16)
            with sp.Fori(1, NE) as item:
                for i in range(MOE_RING):
                    sp.wait_ge(piece_used, item * MOE_RING + (i + 1 - MOE_RING))
                    sp.dma_start(place(i), piece_source(i, item)).then_inc(piece_in[MOE_PLACE[i]], 16)
            sp.wait_ge(table_ready, 1)
            n_extra = sp.value_load(tab[0:1, 0:1], min_val=0, max_val=NX - 1)
            last_quad = sp.value_load(tab[0:1, 1:2], min_val=0, max_val=QUADS + XQ - 1)
            with sp.Fori(0, NX) as j:
                with sp.If(n_extra > j):
                    e = sp.value_load(tab[0:1, bass.ds(j + 2, 1)], min_val=0, max_val=NE - 1)
                    for i in range(MOE_RING):
                        sp.wait_ge(piece_used, j * MOE_RING + (NE - 1) * MOE_RING + i + 1)
                        sp.dma_start(place(i), piece_source(i, e)).then_inc(piece_in[MOE_PLACE[i]], 16)
            for t in range(TILES):
                sp.wait_ge(acc_done, last_quad * 8 + 4 * (t + 1))
                sp.dma_start(out_t[t], x_acc[:, t, :]).then_inc(out_done, 16)
            sp.wait_ge(out_done, 16 * TILES)

        @block.gpsimd
        def _(pool):
            steps = [0]

            def ordered(ins):
                steps[0] += 1
                ins.then_inc(pool_step, 1)
                pool.wait_ge(pool_step, steps[0])

            pool.memset(ident[:, :], 0.0)
            pool.memset(fold[:, :], 0.0)
            pool.memset(prm_rows[:, :], 0.0).then_inc(consts_ready, 1)
            pool.memset(ones[:, :], 1.0)
            pool.memset(ones_b[:, :], 1.0)
            pool.memset(c_eps[:, :], EPS)
            pool.memset(before[:, :], 1.0)
            pool.iota(iota_s[:, :], [[1, SLOTS]], base=0, channel_multiplier=0,
                      allow_small_or_imprecise_dtypes=True)
            pool.iota(iota_e[:, 0:NE], [[1, NE]], base=0, channel_multiplier=0,
                      allow_small_or_imprecise_dtypes=True)
            pool.iota(iota_e[:, NE:NE + NX + QI], [[1, NX + QI]], base=0, channel_multiplier=0,
                      allow_small_or_imprecise_dtypes=True)
            ordered(pool.iota(desc[:, :], [[-1, 12]], base=12, channel_multiplier=0,
                              allow_small_or_imprecise_dtypes=True))
            pool.affine_select(out=ident[:, :], in_=ident[:, :], compare_op=ALU.not_equal, fill=1.0,
                               base=0, pattern=[[-1, P]], channel_multiplier=1)
            for j in range(P // SLOTS):
                pool.affine_select(out=fold[:, :], in_=fold[:, :], compare_op=ALU.not_equal, fill=1.0,
                                   base=-SLOTS * j, pattern=[[-1, SLOTS]], channel_multiplier=1)
                if j + 1 < P // SLOTS:
                    ordered(pool.iota(small[:, 0:1], [[0, 1]], base=0, channel_multiplier=0,
                                      allow_small_or_imprecise_dtypes=True))
            pool.affine_select(out=before[:, :], in_=before[:, :], compare_op=ALU.is_gt, fill=0.0,
                               base=0, pattern=[[1, P]], channel_multiplier=-1).then_inc(consts_ready, 1)
            for j in range(HC):
                pool.wait_ge(proj_free, T_USES + j + 1)
                b = BLK_Q + 2 * j
                pool.tensor_tensor(temp[:, 2 * j:2 * j + 2, :], proj[:, b:b + 2, :], proj[:, b:b + 2, :],
                                   ALU.mult).then_inc(qk_sq, 1)
            for b in range(HC // 2):
                z = scores[b][:, 0]
                pool.wait_ge(aux_free, U_Z + 2 * b + 2)
                for part in (z[:, :, 0:P], z[:, :, 2 * P:3 * P]):
                    ins = pool.affine_select(out=part, in_=part, compare_op=ALU.is_gt, fill=MASKED,
                                             base=0, pattern=[[0, 2], [-1, P]], channel_multiplier=1)
                ins.then_inc(z_masked, 1)
            pool.wait_ge(aux_free, U_PV + HC // 2)
            for j in range(HC // 2):
                b = BLK_Q + 2 * j
                pool.tensor_tensor(proj[:, BLK_K + 2 * j:BLK_K + 2 * j + 2, :], proj[:, b:b + 2, :],
                                   proj[:, b:b + 2, :], ALU.mult).then_inc(y_sq, 1)
            pool.wait_ge(proj_free, T_USES + S_XB + 4)
            pool.tensor_tensor(proj[:, BLK_XB:BLK_XB + HB, :], proj[:, BLK_XB:BLK_XB + HB, :],
                               proj[:, BLK_CG:BLK_CG + HB, :], ALU.mult).then_inc(cx_ready, 1)
            pool.wait_ge(ya_ready, 1)
            for j in range(HA // 2):
                b = BLK_GA + 2 * j
                pool.tensor_tensor(proj[:, BLK_XA + 2 * j:BLK_XA + 2 * j + 2, :], proj[:, b:b + 2, :],
                                   proj[:, b:b + 2, :], ALU.mult).then_inc(y_sq, 1)
            for j in range(HB // 2):
                pool.wait_ge(yb_ready, j + 1)
                b = BLK_BG + 2 * j
                pool.tensor_tensor(proj[:, BLK_CG + 2 * j:BLK_CG + 2 * j + 2, :], proj[:, b:b + 2, :],
                                   proj[:, b:b + 2, :], ALU.mult).then_inc(y_sq, 1)

        @block.scalar
        def _(act):
            steps = [0]

            def ordered(ins):
                steps[0] += 1
                ins.then_inc(act_step, 1)
                act.wait_ge(act_step, steps[0])

            act.wait_ge(consts_ready, 1)
            rows = [(R_CA, conv_a_w[0].rearrange("j (h p) -> (j h) p", p=P)),
                    (R_CAB, conv_a_b[0].rearrange("(h p) -> h p", p=P)),
                    (R_BA, lru_ba[0].rearrange("(h p) -> h p", p=P)),
                    (R_BX, lru_bx[0].rearrange("(h p) -> h p", p=P)),
                    (R_LAM, lru_lam[0].rearrange("(h p) -> h p", p=P)),
                    (R_CB, conv_b_w[0].rearrange("j (h p) -> (j h) p", p=P)),
                    (R_MIX, mix_norm[0].rearrange("(h p) -> h p", p=P)),
                    (R_Q, q_norm), (R_K, k_norm)]
            for r, src in rows:
                act.dma_start(prm_rows[r:r + src.shape[0], :], src).then_inc(par_in, 16)
            act.dma_start(gain_mix[:, :], norm_mix[0].rearrange("(p c) -> p c", c=KC)).then_inc(par_in, 16)
            act.dma_start(gain_ffn[:, :], norm_ffn[0].rearrange("(p c) -> p c", c=KC)).then_inc(par_in, 16)
            PARS = 16 * (len(rows) + 2)
            act.dma_start(w_rt[:, :, 0:NG], w_router_group[0].rearrange("(p c) g -> p c g", c=KC)).then_inc(router_in, 16)
            act.dma_start(w_rt[:, :, NG:], w_router_expert[0].rearrange("(p c) g -> p c g", c=KC)).then_inc(router_in, 16)
            act.dma_start(b_rt[0:1, 0:NG], b_router_group).then_inc(router_in, 16)
            act.dma_start(b_rt[0:1, NG:], b_router_expert).then_inc(router_in, 16)

            for t in range(TILES):
                act.wait_ge(x_in, 16 * TILES)
                act.activation(h_perm[:, t].rearrange("p a b -> p (a b)"), x_acc[:, t, :],
                               ACT.Square, accum_out=ssq[:, t, 0:1]).then_inc(ssq_ready, 1)
            act.wait_ge(var_ready, 1)
            act.activation(ssq[:, :, 2:3], ssq[:, :, 1:2], ACT.Sqrt).then_inc(std_ready, 1)
            act.wait_ge(aux_full, U_PRM + 1)
            act.activation(prm[:, 0:R_ALL], aux(U_PRM)[:, 0:R_ALL], ACT.Copy).then_inc(aux_free, 1)
            act.wait_ge(aux_free, 1)
            ordered(act.activation(lru_t[:, 0, :], prm[:, R_LAM:R_LAM + HA], ACT.Abs))
            act.activation(lru_t[:, 1, :], lru_t[:, 0, :], ACT.Exp, scale=-1.0).then_inc(lam_exp, 1)
            act.wait_ge(par_in, PARS)
            for n in range(T_USES):
                act.wait_ge(proj_full, n + 1)
                for b in range(2):
                    for k in range(2):
                        c = 4 * n + 2 * b + k
                        act.activation(hT_hi[:, c, :], proj_bank(n, b)[:, k * SEQ:(k + 1) * SEQ], ACT.Copy,
                                       scale=gain_mix[:, c:c + 1]).then_inc(hT_hi_ready, 1)
            act.wait_ge(proj_full, T_USES)
            act.dma_start(lru_w[:, 0], lru_wa[0].rearrange("h i j -> i h j")).then_inc(lru_in, 16)
            act.dma_start(lru_w[:, 1], lru_wx[0].rearrange("h i j -> i h j")).then_inc(lru_in, 16)

            def split_high(n):
                act.wait_ge(piece_in[n % MIX_RING], 16 * (n // MIX_RING + 1))
                for k in range(4):
                    g = 4 * n + k
                    if g >= 4:
                        act.wait_ge(quarter_used, g - 3)
                    kk = k if n < N_IN else 3 - k
                    src = ring[:, n % MIX_RING, kk * 4 * PW:(kk + 1) * 4 * PW]
                    act.activation(w_hi[:, k].rearrange("p c n -> p (c n)"), src, ACT.Copy).then_inc(hi_ready, 1)

            def empty_projection(n):
                act.wait_ge(quarter_used, 4 * n + 4)
                for b in range(2):
                    src = proj_bank(n, b)[:, 0:PW]
                    if order[n] < BLK_V:
                        dst = proj[:, order[n] + b, :]
                    else:
                        c0 = (order[n] - BLK_V) * P
                        dst = v_tok[:, b, c0:c0 + PW]
                    ins = act.activation(dst, src, ACT.Copy)
                ins.then_inc(proj_free, 1)

            def stick_scores(b):
                z = scores[b][:, 0]
                act.wait_ge(aux_full, U_Z + 2 * b + 1)
                act.activation(z[:, :, P:3 * P], aux(U_Z + 2 * b)[:, :].rearrange("p (h k) -> p h k", h=2),
                               ACT.Copy, scale=float(P) ** -0.5).then_inc(aux_free, 1)
                act.wait_ge(aux_full, U_Z + 2 * b + 2)
                act.activation(z[:, :, 0:P], aux(U_Z + 2 * b + 1)[:, 0:2 * P].rearrange("p (h k) -> p h k", h=2),
                               ACT.Copy, scale=float(P) ** -0.5).then_inc(aux_free, 1)

            def stick_log(b):
                z, t = scores[b][:, 0], scores[b][:, 1]
                act.wait_ge(z_masked, b + 1)
                ordered(act.activation(t, z, ACT.Abs))
                ordered(act.activation(t, t, ACT.Exp, scale=-1.0))
                act.activation(t, t, ACT.Ln, bias=1.0).then_inc(ln_ready, 1)

            def stick_weights(b):
                act.wait_ge(logw_ready, b + 1)
                act.activation(scores[b][:, 0], scores[b][:, 1], ACT.Exp).then_inc(w_ready, 1)

            def weights_transposed(h):
                act.wait_ge(aux_full, U_WT + h + 1)
                act.activation(scores[h // 2][:, 1, h % 2, :], aux(U_WT + h)[:, 0:3 * P], ACT.Copy).then_inc(aux_free, 1)

            def attention_out(b):
                act.wait_ge(aux_full, U_PV + b + 1)
                act.activation(proj[:, BLK_Q + 2 * b:BLK_Q + 2 * b + 2, :],
                               aux(U_PV + b)[:, :].rearrange("p (h k) -> p h k", h=2), ACT.Copy).then_inc(aux_free, 1)

            def lru_gates():
                for h in range(HA):
                    u = U_LRU + h
                    act.wait_ge(aux_full, u + 1)
                    act.activation(proj[:, BLK_XA + h, :], aux(u)[:, 0:SEQ], ACT.Sigmoid,
                                   bias=prm[:, R_BA + h:R_BA + h + 1])
                    act.activation(lru_u[:, h, :], aux(u)[:, SEQ:2 * SEQ], ACT.Sigmoid,
                                   bias=prm[:, R_BX + h:R_BX + h + 1]).then_inc(aux_free, 1)

            def norm_std(uses, dst, ready):
                for j, u in enumerate(uses):
                    act.wait_ge(aux_full, u + 1)
                    act.activation(dst[:, 2 * j:2 * j + 2, :], aux(u)[:, :].rearrange("p (h k) -> p h k", h=2),
                                   ACT.Sqrt, scale=1.0 / P, bias=c_eps[:, 0:1]).then_inc(aux_free, 1)

            def y_split_high(quarter):
                act.wait_ge(y_norm, Y_NEED[quarter])
                c0 = 4 * quarter
                for a, b in Y_RUNS[quarter]:
                    ins = act.activation(y_hi[:, a:b, :], proj[:, y_block(a):y_block(a) + b - a, :], ACT.Copy)
                ins.then_inc(y_hi_ready, 1)

            def second_squares(k):
                act.wait_ge(proj_free, T_USES + N_IN + k + 1)
                for t in range(TILES):
                    ins = act.activation(h2_perm[:, t, 2 * k:2 * k + 2, :].rearrange("p a b -> p (a b)"),
                                         x_acc[:, t, k * PW:(k + 1) * PW], ACT.Square,
                                         accum_out=ssq[:, t, 2 + k:3 + k])
                ins.then_inc(ssq2_ready, 1)

            for n in range(N_MIX):
                split_high(n)
                if 1 <= n <= N_IN:
                    empty_projection(n - 1)
                if n == S_XA:
                    norm_std(range(U_QK, U_Z), temp, None)
                if n == 13:
                    for b in range(HC // 2):
                        stick_scores(b)
                    stick_log(0)
                    stick_log(1)
                if n == 14:
                    stick_weights(0)
                    stick_log(2)
                    stick_weights(1)
                if n == 15:
                    stick_weights(2)
                    for h in range(HC):
                        weights_transposed(h)
                if n == 17:
                    for b in range(HC // 2):
                        attention_out(b)
                    lru_gates()
                    act.wait_ge(y2_ready, 1)
                    act.activation(lru_a[:, :, :], proj[:, BLK_XA:BLK_XA + HA, :], ACT.Exp, scale=-0.5)
                    act.activation(lru_e[:, :, :], proj[:, BLK_XA:BLK_XA + HA, :], ACT.Exp, scale=-1.0).then_inc(decay_ready, 1)
                if n == 18:
                    act.activation(proj[:, BLK_GA:BLK_GA + HA, :], proj[:, BLK_GA:BLK_GA + HA, :],
                                   ACT.Gelu_apprx_tanh).then_inc(gelu_ready, 1)
                if n == 20:
                    act.wait_ge(expm1_ready, 1)
                    act.activation(conv_a[:, :, :], conv_a[:, :, :], ACT.Sqrt).then_inc(root_ready, 1)
                if n == N_IN:
                    norm_std(range(U_YC, U_YA), proj[:, BLK_K:BLK_K + HC, :], None)
                    norm_std(range(U_YA, U_YB), proj[:, BLK_XA:BLK_XA + HA, :], None)
                    norm_std(range(U_YB, U_END), proj[:, BLK_CG:BLK_CG + HB, :], None)
                    act.wait_ge(quarter_used, 4 * N_IN)
                    for quarter in (3, 2, 1, 0):
                        y_split_high(quarter)
                if n > N_IN:
                    second_squares(n - N_IN - 1)
            second_squares(N_OUT - 1)
            act.wait_ge(var_ready, 2)
            act.activation(ssq[:, :, 2:3], ssq[:, :, 1:2], ACT.Sqrt).then_inc(std_ready, 1)
            act.wait_ge(sub_ready, 1)
            act.activation(small[:, 0:TILES * NG], small[:, 0:TILES * NG], ACT.Exp).then_inc(e_ready, 1)
            act.wait_ge(sub_ready, 2)
            act.activation(small[:, 16:16 + TILES * EG], small[:, 16:16 + TILES * EG], ACT.Exp).then_inc(e_ready, 1)

            def item_step(q, k):
                i = q * QI + k
                act.wait_ge(piece_used, i * MOE_RING + 3)
                if not (isinstance(q, int) and i == 0):
                    act.wait_ge(fold_full, i)
                act.activation(gate_sb[:, :], b_gate[:, :], ACT.Copy).then_inc(gate_out, 1)
                act.wait_ge(fold_full, i + 1)
                if not (isinstance(q, int) and i == 0):
                    act.wait_ge(hid_ready, i)
                act.activation(silu_sb[:, :, :], b_fold[:, 0:P].rearrange("p (f s) -> p f s", f=FC),
                               ACT.Silu).then_inc(silu_ready, 1)
                act.wait_ge(piece_used, i * MOE_RING + 6)
                if not isinstance(q, int):
                    act.wait_ge(comb_full, q * 8)
                for n in range(2):
                    ins = act.activation(y_exp[SLOTS * k:SLOTS * (k + 1), n * 512:(n + 1) * 512],
                                         b_down[SLOTS * n:SLOTS * (n + 1), :], ACT.Copy)
                ins.then_inc(y_out_act, 1)

            def quad(q, n_extra=None):
                act.wait_ge(give_full, q + 1)
                act.activation(give[:, :, :], b_fold[:, 2 * P:4 * P].rearrange("p (t s) -> p t s", t=TILES),
                               ACT.Copy).then_inc(give_ready, 1)
                for k in range(QI):
                    if n_extra is None:
                        item_step(q, k)
                    else:
                        with act.If(n_extra > (q - QUADS) * QI + k):
                            item_step(q, k)

            quad(0)
            with act.Fori(1, QUADS) as q:
                quad(q)
            act.wait_ge(table_ready, 1)
            n_extra = act.value_load(tab[0:1, 0:1], min_val=0, max_val=NX - 1)
            with act.Fori(QUADS, QUADS + XQ) as q:
                with act.If(n_extra > (q - QUADS) * QI):
                    quad(q, n_extra)

        @block.vector
        def _(dve):
            steps = [0]

            def ordered(ins):
                steps[0] += 1
                ins.then_inc(dve_step, 1)
                dve.wait_ge(dve_step, steps[0])

            def token_rstd(round_):
                dve.wait_ge(std_ready, round_)
                r, v, w = ssq[:, :, 2:3], ssq[:, :, 1:2], ssq[:, :, 3:4]
                ordered(dve.reciprocal(r, r))
                ordered(dve.tensor_tensor(w, r, r, ALU.mult))
                ordered(dve.tensor_tensor(w, w, v, ALU.mult))
                ordered(dve.tensor_scalar(w, w, -0.5, 1.5, ALU.mult, ALU.add))
                ordered(dve.tensor_tensor(r, r, w, ALU.mult))

            dve.wait_ge(ssq_ready, TILES)
            dve.tensor_scalar(ssq[:, :, 1:2], ssq[:, :, 0:1], 1.0 / D, EPS, ALU.mult, ALU.add).then_inc(var_ready, 1)
            dve.wait_ge(var_ready, 1)
            token_rstd(1)
            for t in range(TILES):
                dve.tensor_scalar(h_perm[:, t].rearrange("p c k -> p k c"),
                                  x_acc[:, t, :].rearrange("p (k c) -> p k c", c=KC),
                                  ssq[:, t, 2:3], None, ALU.mult).then_inc(h_ready, 1)
            for n in range(T_USES):
                for b in range(2):
                    for k in range(2):
                        c = 4 * n + 2 * b + k
                        dve.wait_ge(hT_hi_ready, c - k + 2)
                        ins = dve.scalar_tensor_tensor(hT_lo[:, c, :], proj_bank(n, b)[:, k * SEQ:(k + 1) * SEQ],
                                                       gain_mix[:, c:c + 1], hT_hi[:, c, :].bitcast(F32),
                                                       ALU.mult, ALU.subtract)
                ins.then_inc(proj_free, 1)
            dve.wait_ge(lam_exp, 1)
            e_, s_, s2 = lru_t[:, 1, :], lru_t[:, 0, :], lru_t[:, 2, :]
            ordered(dve.tensor_scalar(s_, e_, 2.0, None, ALU.add))
            ordered(dve.reciprocal(s_, s_))
            ordered(dve.tensor_tensor(s_, s_, e_, ALU.mult))
            ordered(dve.tensor_tensor(s2, s_, s_, ALU.mult))
            ordered(dve.tensor_scalar(lru_c[:, :], s2, 1.0 / 19, None, ALU.mult))
            for k in range(8, 0, -1):
                ordered(dve.scalar_tensor_tensor(lru_c[:, :], lru_c[:, :], 1.0 / (2 * k + 1), s2, ALU.add, ALU.mult))
            ordered(dve.scalar_tensor_tensor(lru_c[:, :], lru_c[:, :], 1.0, s_, ALU.add, ALU.mult))
            ordered(dve.tensor_scalar(s2, prm[:, R_LAM:R_LAM + HA], -1.0, 0.0, ALU.mult, ALU.max))
            ordered(dve.scalar_tensor_tensor(lru_c[:, :], lru_c[:, :], 2.0, s2, ALU.mult, ALU.add))
            ordered(dve.tensor_scalar(lru_c[:, :], lru_c[:, :], 2 * LRU_C, None, ALU.mult))

            def split_low(n):
                for k in range(4):
                    g = 4 * n + k
                    dve.wait_ge(hi_ready, g + 1)
                    if g >= 4:
                        dve.wait_ge(quarter_used, g - 3)
                    kk = k if n < N_IN else 3 - k
                    src = ring[:, n % MIX_RING, kk * 4 * PW:(kk + 1) * 4 * PW]
                    dve.tensor_tensor(w_lo[:, k].rearrange("p c n -> p (c n)"), src,
                                      w_hi[:, k].rearrange("p c n -> p (c n)").bitcast(F32),
                                      ALU.subtract).then_inc(lo_ready, 1)

            def normalise_qk():
                for j in range(HC):
                    dve.wait_ge(aux_free, U_QK + j + 1)
                    t = temp[:, 2 * j:2 * j + 2, :]
                    ordered(dve.reciprocal(t, t))
                    for b in range(2):
                        blk = BLK_Q + 2 * j + b
                        gain = R_Q if blk < BLK_K else R_K
                        ins = dve.scalar_tensor_tensor(proj[:, blk, :], proj[:, blk, :], prm[:, gain:gain + 1],
                                                       temp[:, 2 * j + b, :], ALU.mult, ALU.mult)
                    ins.then_inc(qk_ready, 1)

            def causal_conv(dst, src, taps, tap_col, bias_col, blocks, dst0, src0, ready=None):
                for h in range(blocks):
                    d, s = dst[:, dst0 + h, :], src[:, src0 + h, :]
                    last = tap_col(taps - 1, h)
                    if bias_col is None:
                        ins = dve.tensor_scalar(d, s, prm[:, last:last + 1], None, ALU.mult)
                    else:
                        ins = dve.tensor_scalar(d, s, prm[:, last:last + 1],
                                                prm[:, bias_col + h:bias_col + h + 1], ALU.mult, ALU.add)
                ordered(ins)
                for back in range(1, taps):
                    for h in range(blocks):
                        d, s = dst[:, dst0 + h, :], src[:, src0 + h, :]
                        w = tap_col(taps - 1 - back, h)
                        ins = dve.scalar_tensor_tensor(d[:, back:], s[:, 0:SEQ - back], prm[:, w:w + 1],
                                                       d[:, back:], ALU.mult, ALU.add)
                    if back < taps - 1 or ready is None:
                        ordered(ins)
                    else:
                        ins.then_inc(ready, 1)

            def stick(b):
                z, t = scores[b][:, 0], scores[b][:, 1]
                dve.wait_ge(ln_ready, b + 1)
                ordered(dve.scalar_tensor_tensor(t, z, 0.0, t, ALU.max, ALU.add))
                for h in range(2):
                    for a, e in ((0, P), (P, 3 * P)):
                        back = t[:, h, a:e][:, ::-1]
                        ins = dve.tensor_tensor_scan(back, back, back, 0.0, ALU.add, ALU.max)
                ordered(ins)
                dve.tensor_tensor(t, z, t, ALU.subtract).then_inc(logw_ready, 1)

            def normalise_y(uses, std, first, chunk0, need):
                for j, u in enumerate(uses):
                    dve.wait_ge(aux_free, u + 1)
                    t = proj[:, std + 2 * j:std + 2 * j + 2, :]
                    ordered(dve.reciprocal(t, t))
                    for b in range(2):
                        blk, c = first + 2 * j + b, chunk0 + 2 * j + b
                        ins = dve.scalar_tensor_tensor(proj[:, blk, :], proj[:, blk, :],
                                                       prm[:, R_MIX + c:R_MIX + c + 1],
                                                       proj[:, std + 2 * j + b, :], ALU.mult, ALU.mult)
                    ins.then_inc(y_norm, 1)

            def gated_conv(j):
                dve.wait_ge(proj_free, T_USES + N_IN - 1 + j)
                b = 2 * j
                dve.tensor_tensor(proj[:, BLK_BG + b:BLK_BG + b + 2, :], proj[:, BLK_BG + b:BLK_BG + b + 2, :],
                                  proj[:, BLK_CG + b:BLK_CG + b + 2, :], ALU.mult).then_inc(yb_ready, 1)

            def residual(k):
                dve.wait_ge(quarter_used, 4 * (N_IN + k) + 4)
                if k == 0:
                    dve.wait_ge(x_again, 16 * TILES)
                for t in range(TILES):
                    dst = x_acc[:, t, k * PW:(k + 1) * PW]
                    ins = dve.tensor_tensor(dst, dst, proj_bank(N_IN + k, t)[:, 0:PW], ALU.add)
                ins.then_inc(proj_free, 1)

            y_, p_ = proj[:, BLK_XA:BLK_XA + HA, :], conv_a[:, :, :]

            for n in range(N_MIX):
                split_low(n)
                if n == S_XA:
                    normalise_qk()
                if n == 12:
                    dve.wait_ge(proj_free, T_USES + 12)
                    causal_conv(conv_a, proj, CONV_A, lambda j, h: R_CA + j * HA + h, R_CAB, HA, 0, BLK_XA,
                                conv_ready)
                if n in (13, 14, 15):
                    stick(n - 13)
                if n == 17:
                    dve.wait_ge(aux_free, U_LRU + HA)
                    for h in range(HA):
                        ins = dve.tensor_scalar(proj[:, BLK_XA + h, :], proj[:, BLK_XA + h, :],
                                                lru_c[:, h:h + 1], None, ALU.mult)
                    ins.then_inc(y2_ready, 1)
                    dve.tensor_tensor(lru_u[:, :, :], lru_u[:, :, :], conv_a[:, :, :], ALU.mult)
                if n == 18:
                    dve.wait_ge(decay_ready, 1)
                    ordered(dve.tensor_scalar(y_, y_, POLY_BELOW, None, ALU.min))
                    ordered(dve.tensor_scalar(p_, y_, -1.0 / 720, None, ALU.mult))
                    ordered(dve.scalar_tensor_tensor(p_, p_, 1.0 / 120, y_, ALU.add, ALU.mult))
                    ordered(dve.scalar_tensor_tensor(p_, p_, -1.0 / 24, y_, ALU.add, ALU.mult))
                if n == 19:
                    ordered(dve.scalar_tensor_tensor(p_, p_, 1.0 / 6, y_, ALU.add, ALU.mult))
                    ordered(dve.scalar_tensor_tensor(p_, p_, -0.5, y_, ALU.add, ALU.mult))
                    ordered(dve.scalar_tensor_tensor(p_, p_, 1.0, y_, ALU.add, ALU.mult))
                    ordered(dve.tensor_scalar(lru_e[:, :, :], lru_e[:, :, :], -1.0, 1.0, ALU.mult, ALU.add))
                    dve.wait_ge(cx_ready, 1)
                    causal_conv(proj, proj, CONV_B, lambda j, h: R_CB + j * HB + h, None, HB, BLK_CG, BLK_XB)
                if n == 20:
                    ordered(dve.tensor_tensor(lru_e[:, :, :], lru_e[:, :, :], p_, ALU.subtract))
                    ordered(dve.scalar_tensor_tensor(lru_e[:, :, :], y_, POLY_BELOW, lru_e[:, :, :], ALU.is_ge, ALU.mult))
                    dve.tensor_tensor(p_, p_, lru_e[:, :, :], ALU.add).then_inc(expm1_ready, 1)
                    gated_conv(0)
                    dve.wait_ge(root_ready, 1)
                    ordered(dve.tensor_tensor(lru_u[:, :, :], lru_u[:, :, :], p_, ALU.mult))
                    for h in range(HA):
                        ins = dve.tensor_tensor_scan(lru_e[:, h, :], lru_a[:, h, :], lru_u[:, h, :], 0.0,
                                                     ALU.mult, ALU.add)
                    ordered(ins)
                    dve.wait_ge(gelu_ready, 1)
                    dve.tensor_tensor(proj[:, BLK_GA:BLK_GA + HA, :], proj[:, BLK_GA:BLK_GA + HA, :],
                                      lru_e[:, :, :], ALU.mult).then_inc(ya_ready, 1)
                if n == N_IN:
                    gated_conv(1)
                    normalise_y(range(U_YC, U_YA), BLK_K, BLK_Q, HA + HB, None)
                    normalise_y(range(U_YA, U_YB), BLK_XA, BLK_GA, 0, None)
                    normalise_y(range(U_YB, U_END), BLK_CG, BLK_BG, HA, None)
                    for k, quarter in enumerate((3, 2, 1, 0)):
                        dve.wait_ge(y_hi_ready, k + 1)
                        for a, b in Y_RUNS[quarter]:
                            ins = dve.tensor_tensor(y_lo[:, a:b, :], proj[:, y_block(a):y_block(a) + b - a, :],
                                                    y_hi[:, a:b, :].bitcast(F32), ALU.subtract)
                        ins.then_inc(y_split, 1)
                if n > N_IN:
                    residual(n - N_IN - 1)
            residual(N_OUT - 1)

            dve.wait_ge(ssq2_ready, N_OUT)
            ordered(dve.tensor_reduce(ssq[:, :, 0:1], ssq[:, :, 2:2 + N_OUT], AX, ALU.add))
            dve.tensor_scalar(ssq[:, :, 1:2], ssq[:, :, 0:1], 1.0 / D, EPS, ALU.mult, ALU.add).then_inc(var_ready, 1)
            dve.wait_ge(var_ready, 2)
            token_rstd(2)
            for t in range(TILES):
                dve.tensor_scalar(h2_perm[:, t].rearrange("p c k -> p k c"),
                                  x_acc[:, t, :].rearrange("p (k c) -> p k c", c=KC),
                                  ssq[:, t, 2:3], None, ALU.mult).then_inc(h2_ready, 1)
            for c in range(0, KC, 2):
                dve.wait_ge(h2T_full, c // 2 + 1)
                dve.tensor_tensor(h2T[:, c:c + 2, :], bank[(c // 2) % 4][:, :].rearrange("p (c t) -> p c t", c=2),
                                  gain_ffn[:, c:c + 2].unsqueeze(2).to_broadcast([P, 2, SEQ]),
                                  ALU.mult).then_inc(h2T_free, 1)

            def take(n, shape, a=[48]):
                v = small[:, a[0]:a[0] + n]
                a[0] += n
                names = "tgj"[:len(shape)] if len(shape) < 3 else "tgj"
                if len(shape) == 2:
                    return v.rearrange("p (t g) -> p t g", t=shape[0])
                return v.rearrange("p (t g j) -> p t g j", t=shape[0], g=shape[1])

            TT = TILES
            g_exp = small[:, 0:TT * NG].rearrange("p (t g) -> p t g", t=TT)
            e_exp = small[:, 16:16 + TT * EG].rearrange("p (t g) -> p t g", t=TT)
            lg = take(TT * (NG + NE), (TT, NG + NE))
            g_one = take(TT * NG, (TT, NG))
            t4 = take(TT * NG, (TT, NG))
            m = take(TT, (TT, 1))
            pg = take(TT, (TT, 1))
            m1, m2, mm = take(TT, (TT, 1)), take(TT, (TT, 1)), take(TT, (TT, 1))
            ing = take(TT * EG, (TT, EG))
            one1, one2, t8 = take(TT * EG, (TT, EG)), take(TT * EG, (TT, EG)), take(TT * EG, (TT, EG))
            big = take(TT * NE, (TT, NG, EG))
            sel = take(TT * NE, (TT, NG, EG))
            cnt = take(NE, (1, NE))[:, 0]
            excl = take(NE, (1, NE))[:, 0]
            incl = take(NE, (1, NE))[:, 0]
            ntab = take(2 + NX + QI, (1, 2 + NX + QI))[:, 0]

            def wide(a, n):
                return a.to_broadcast([P, TT, n])

            def first_max(one, p, n, mx, tmp):
                ordered(dve.tensor_reduce(mx, p, AX, ALU.max))
                ordered(dve.tensor_tensor(tmp, p, wide(mx, n), ALU.is_equal))
                ordered(dve.tensor_tensor(tmp, tmp, desc[:, 0:n].unsqueeze(1).to_broadcast([P, TT, n]), ALU.mult))
                ordered(dve.tensor_reduce(mm, tmp, AX, ALU.max))
                ordered(dve.tensor_tensor(one, tmp, wide(mm, n), ALU.is_equal))

            dve.wait_ge(logits_full, 1)
            ordered(dve.tensor_copy(lg, bank[4][:, 0:TT * (NG + NE)].rearrange("p (t g) -> p t g", t=TT)))
            first_max(g_one, lg[:, :, 0:NG], NG, m, t4)
            dve.tensor_tensor(g_exp, lg[:, :, 0:NG], wide(m, NG), ALU.subtract).then_inc(sub_ready, 1)
            ordered(dve.tensor_tensor(big, lg[:, :, NG:].rearrange("p t (g j) -> p t g j", g=NG),
                                      g_one.unsqueeze(3).to_broadcast([P, TT, NG, EG]), ALU.mult))
            ordered(dve.tensor_reduce(ing, big.transpose([0, 1, 3, 2]), AX, ALU.add))
            ordered(dve.tensor_reduce(m1, ing, AX, ALU.max))
            dve.tensor_tensor(e_exp, ing, wide(m1, EG), ALU.subtract).then_inc(sub_ready, 1)
            dve.wait_ge(e_ready, 1)
            ordered(dve.tensor_reduce(pg, g_exp, AX, ALU.add))
            ordered(dve.reciprocal(pg, pg))
            dve.wait_ge(e_ready, 2)
            ordered(dve.tensor_reduce(m, e_exp, AX, ALU.add))
            ordered(dve.reciprocal(m, m))
            ordered(dve.tensor_tensor(e_exp, e_exp, wide(m, EG), ALU.mult))
            first_max(one1, e_exp, EG, m1, t8)
            ordered(dve.scalar_tensor_tensor(e_exp, one1, -2.0, e_exp, ALU.mult, ALU.add))
            first_max(one2, e_exp, EG, m2, t8)
            ordered(dve.tensor_tensor(m, m1, m2, ALU.add))
            ordered(dve.reciprocal(m, m))
            ordered(dve.tensor_tensor(m1, m1, m, ALU.mult))
            ordered(dve.tensor_tensor(m2, m2, m, ALU.mult))
            ordered(dve.tensor_tensor(m1, m1, pg, ALU.mult))
            ordered(dve.tensor_tensor(m2, m2, pg, ALU.mult))
            ordered(dve.tensor_tensor(t8, one1, one2, ALU.add))
            g4 = g_one.unsqueeze(3).to_broadcast([P, TT, NG, EG])
            ordered(dve.tensor_tensor(sel, g4, t8.unsqueeze(2).to_broadcast([P, TT, NG, EG]), ALU.mult))
            dve.tensor_copy(sel_b[:, :, :], sel.rearrange("p t g j -> p t (g j)")).then_inc(sel_ready, 1)
            ordered(dve.tensor_tensor(one1, one1, wide(m1, EG), ALU.mult))
            ordered(dve.tensor_tensor(one2, one2, wide(m2, EG), ALU.mult))
            ordered(dve.tensor_tensor(one1, one1, one2, ALU.add))
            gates = gate_item[:, :, 0:NE]
            ordered(dve.tensor_tensor(gates.rearrange("p t (g j) -> p t g j", g=NG), g4,
                                      one1.unsqueeze(2).to_broadcast([P, TT, NG, EG]), ALU.mult))
            ranks = rank_item[:, :, 0:NE]
            dve.wait_ge(rank_full, 1)
            ordered(dve.scalar_tensor_tensor(ranks, bank[5][:, 0:TT * NE].rearrange("p (t e) -> p t e", t=TT), 1.0,
                                             sel.rearrange("p t g j -> p t (g j)"), ALU.add, ALU.mult))
            ordered(dve.tensor_copy(cnt, bank[5][:, TT * NE:(TT + 1) * NE]))
            ordered(dve.tensor_scalar(ranks, ranks, -1.0, None, ALU.add))

            def make_pick(q, mark):
                r = rank_item[:, :, bass.ds(q * QI, QI)]
                g = gate_item[:, :, bass.ds(q * QI, QI)]
                for t in range(TILES):
                    ins = dve.tensor_tensor(pick[:, t], r[:, t].unsqueeze(2).to_broadcast([P, QI, SLOTS]),
                                            iota_s[:, :].unsqueeze(1).to_broadcast([P, QI, SLOTS]), ALU.is_equal)
                ins.then_inc(pick_made, 1)
                dve.wait_ge(pick_made, mark)
                for t in range(TILES):
                    ins = dve.tensor_tensor(pick_gate[:, t], pick[:, t],
                                            g[:, t].unsqueeze(2).to_broadcast([P, QI, SLOTS]), ALU.mult)
                ins.then_inc(pick_ready, 1)

            make_pick(0, 1)

            ordered(dve.tensor_scalar(incl, cnt, float(SLOTS), None, ALU.is_gt))
            for k in range(2, SEQ // SLOTS):
                ordered(dve.scalar_tensor_tensor(incl, cnt, float(SLOTS * k), incl, ALU.is_gt, ALU.add))
            ordered(dve.tensor_copy(excl, incl))
            ordered(dve.tensor_tensor_scan(incl, excl, excl, 0.0, ALU.add, ALU.max))
            ordered(dve.tensor_tensor(excl, incl, excl, ALU.subtract))
            M = NX + QI
            it = iota_e[:, NE:NE + M]
            by_item = it.unsqueeze(2).to_broadcast([P, M, NE])

            def by_expert(a):
                return a.unsqueeze(1).to_broadcast([P, M, NE])

            mt, cr = match[:, :, :], cross[:, :, :]
            ordered(dve.tensor_tensor(mt, by_item, by_expert(excl), ALU.is_ge))
            ordered(dve.tensor_tensor(cr, by_item, by_expert(incl), ALU.is_lt))
            ordered(dve.tensor_tensor(mt, mt, cr, ALU.mult))
            ordered(dve.tensor_tensor(cr, mt, by_expert(iota_e[:, 0:NE]), ALU.mult))
            ordered(dve.tensor_reduce(ntab[:, 2:2 + M], cr, AX, ALU.add))
            ordered(dve.tensor_copy(ntab[:, 0:1], incl[:, NE - 1:NE]))
            ordered(dve.tensor_scalar(ntab[:, 1:2], ntab[:, 0:1], 0.0, float(QUADS - 1), ALU.is_gt, ALU.add))
            for k in range(1, XQ):
                ordered(dve.scalar_tensor_tensor(ntab[:, 1:2], ntab[:, 0:1], float(QI * k), ntab[:, 1:2],
                                                 ALU.is_gt, ALU.add))
            dve.tensor_copy(tab[:, :], ntab[:, 0:2 + NX]).then_inc(table_ready, 1)
            for t in range(TILES):
                ordered(dve.tensor_tensor(cr, by_item, by_expert(excl), ALU.subtract))
                ordered(dve.tensor_scalar(cr, cr, -float(SLOTS), -float(SLOTS) + 1.0, ALU.mult, ALU.add))
                ordered(dve.tensor_tensor(cr, cr, by_expert(rank_item[:, t, 0:NE]), ALU.add))
                ordered(dve.tensor_tensor(cr, cr, mt, ALU.mult))
                ordered(dve.tensor_reduce(rank_item[:, t, NE:NE + M], cr, AX, ALU.add))
                ordered(dve.tensor_scalar(rank_item[:, t, NE:NE + M], rank_item[:, t, NE:NE + M], -1.0, None, ALU.add))
                ordered(dve.tensor_tensor(cr, mt, by_expert(gate_item[:, t, 0:NE]), ALU.mult))
                ordered(dve.tensor_reduce(gate_item[:, t, NE:NE + M], cr, AX, ALU.add))

            def gather_out(q):
                for b in range(4):
                    dve.wait_ge(gath_full, q * 4 + (b + 1))
                    if not isinstance(q, int) and b == 0:
                        dve.wait_ge(piece_used, q * (QI * MOE_RING) - 2)
                    dve.tensor_tensor(x_exp[:, 4 * b:4 * b + 4, :],
                                      b_gath[b % 2][:, :].rearrange("p (c s) -> p c s", c=4),
                                      gain_ffn[:, 4 * b:4 * b + 4].unsqueeze(2).to_broadcast([P, 4, P]),
                                      ALU.mult).then_inc(gath_out, 1)

            def accumulate(q, back):
                for b in range(8):
                    t, n = b // 4, b % 4
                    dve.wait_ge(comb_full, q * 8 + (b + 1 - 8 * back))
                    dst = x_acc[:, t, n * 512:(n + 1) * 512]
                    dve.tensor_tensor(dst, dst, b_comb[b % 2][:, :], ALU.add).then_inc(acc_done, 1)

            def item_step(q, k):
                i = q * QI + k
                first = isinstance(q, int) and i == 0
                dve.wait_ge(piece_used, i * MOE_RING + 4)
                if not first:
                    dve.wait_ge(fold_full, i)
                dve.tensor_copy(up_sb[:, :], b_up[:, :]).then_inc(up_out, 1)
                dve.wait_ge(silu_ready, i + 1)
                if not first:
                    dve.wait_ge(piece_used, i * MOE_RING)
                dve.tensor_tensor(hidT[:, :, :], silu_sb[:, :, :],
                                  b_fold[:, P:2 * P].rearrange("p (f s) -> p f s", f=FC),
                                  ALU.mult).then_inc(hid_ready, 1)
                dve.wait_ge(piece_used, i * MOE_RING + 6)
                if not isinstance(q, int):
                    dve.wait_ge(comb_full, q * 8)
                for n in range(2, 4):
                    ins = dve.tensor_copy(y_exp[SLOTS * k:SLOTS * (k + 1), n * 512:(n + 1) * 512],
                                          b_down[SLOTS * n:SLOTS * (n + 1), :])
                ins.then_inc(y_out_dve, 1)

            def quad(q, n_extra=None):
                if not isinstance(q, int):
                    accumulate(q, 1)
                gather_out(q)
                dve.wait_ge(give_full, q + 1)
                make_pick(q + 1, q + 2)
                for k in range(QI):
                    if n_extra is None:
                        item_step(q, k)
                    else:
                        with dve.If(n_extra > (q - QUADS) * QI + k):
                            item_step(q, k)

            quad(0)
            with dve.Fori(1, QUADS) as q:
                quad(q)
            n_extra = dve.value_load(tab[0:1, 0:1], min_val=0, max_val=NX - 1)
            last_quad = dve.value_load(tab[0:1, 1:2], min_val=0, max_val=QUADS + XQ - 1)
            with dve.Fori(QUADS, QUADS + XQ) as q:
                with dve.If(n_extra > (q - QUADS) * QI):
                    quad(q, n_extra)
            accumulate(last_quad, 0)

        @block.tensor
        def _(pe):
            pe.wait_ge(consts_ready, 2)
            pe.wait_ge(par_in, 16 * 11)
            pe.transpose(aux(U_PRM)[:, 0:P], prm_rows[:, :], ident[:, :]).then_inc(aux_full, 1)
            pe.wait_ge(h_ready, TILES)
            for n in range(T_USES):
                if n >= 2:
                    pe.wait_ge(proj_free, n - 1)
                for b in range(2):
                    for k in range(2):
                        for t in range(TILES):
                            ins = pe.transpose(proj_bank(n, b)[:, k * SEQ + t * P:k * SEQ + (t + 1) * P],
                                               h_perm[:, t, 4 * n + 2 * b + k, :], ident[:, :])
                ins.then_inc(proj_full, 1)

            def piece(n, parity, kind):
                pe.wait_ge(proj_free, n + (T_USES - 1))
                for k in range(4):
                    pe.wait_ge(lo_ready, n * 4 + (k + 1))
                    if kind == "y" and isinstance(n, int):
                        pe.wait_ge(y_split, k + 1)
                    for cc in range(4):
                        c = 4 * (3 - k if kind == "y" else k) + cc
                        for b in range(2):
                            dst = bank[2 * parity + b][:, 0:PW]
                            hi, lo = w_hi[:, k, cc, :], w_lo[:, k, cc, :]
                            cols = slice(b * P, (b + 1) * P)
                            if kind == "w":
                                trio = [(hi[:, cols], hT_hi[:, c, :]), (hi[:, cols], hT_lo[:, c, :]),
                                        (lo[:, cols], hT_hi[:, c, :])]
                            else:
                                a_hi, a_lo = (y_hi, y_lo) if kind == "y" else (hT_hi, hT_lo)
                                trio = [(a_hi[:, c, cols], hi), (a_hi[:, c, cols], lo), (a_lo[:, c, cols], hi)]
                            for j, (stationary, moving) in enumerate(trio):
                                ins = pe.matmul(dst, stationary, moving, start=(k == 0 and cc == 0 and j == 0),
                                                stop=(k == 3 and cc == 3 and j == 2))
                    ins.then_inc(quarter_used, 1)

            def pieces(first, last, kind):
                with pe.Fori(first, last, 2) as n:
                    piece(n, first % 2, kind)
                    piece(n + 1, (first + 1) % 2, kind)

            def use(u):
                if u >= 4:
                    pe.wait_ge(aux_free, u - 3)
                return aux(u)

            def sums(u, squares):
                for b in range(2):
                    ins = pe.matmul(use(u)[:, b * SEQ:(b + 1) * SEQ], ones[:, :], squares[:, b, :], start=True, stop=True)
                ins.then_inc(aux_full, 1)

            pe.wait_ge(proj_free, T_USES)
            pieces(0, S_V, "w")
            for n in range(S_V, S_XA):
                piece(n, n % 2, "h")
            for j in range(HC):
                pe.wait_ge(qk_sq, j + 1)
                sums(U_QK + j, temp[:, 2 * j:2 * j + 2, :])
            pieces(9, 13, "w")
            pe.wait_ge(qk_ready, HC)
            for b in range(HC // 2):
                u = U_Z + 2 * b
                for h in range(2):
                    q, k = proj[:, BLK_Q + 2 * b + h, :], proj[:, BLK_K + 2 * b + h, :]
                    ins = pe.matmul(use(u)[:, h * SEQ:(h + 1) * SEQ], q[:, P:2 * P], k, start=True, stop=True)
                ins.then_inc(aux_full, 1)
                for h in range(2):
                    q, k = proj[:, BLK_Q + 2 * b + h, :], proj[:, BLK_K + 2 * b + h, :]
                    ins = pe.matmul(use(u + 1)[:, h * P:(h + 1) * P], q[:, 0:P], k[:, 0:P], start=True, stop=True)
                ins.then_inc(aux_full, 1)
            pieces(13, 15, "w")
            for h in range(HC):
                w = scores[h // 2][:, 0, h % 2, :]
                pe.wait_ge(w_ready, h // 2 + 1)
                for k in range(3):
                    ins = pe.transpose(use(U_WT + h)[:, k * P:(k + 1) * P], w[:, k * P:(k + 1) * P], ident[:, :])
                ins.then_inc(aux_full, 1)
            pieces(15, 17, "w")
            for b in range(HC // 2):
                for hh in range(2):
                    h = 2 * b + hh
                    wT = scores[b][:, 1, hh, :]
                    pe.wait_ge(aux_free, U_WT + h + 1)
                    dst = use(U_PV + b)
                    pe.matmul(dst[:, hh * SEQ:(hh + 1) * SEQ], v_tok[:, 0, h * P:(h + 1) * P], wT[:, 0:SEQ],
                              start=True, stop=False)
                    ins = pe.matmul(dst[:, hh * SEQ + P:(hh + 1) * SEQ], v_tok[:, 1, h * P:(h + 1) * P],
                                    wT[:, SEQ:SEQ + P], start=False, stop=True)
                ins.then_inc(aux_full, 1)
            pe.wait_ge(conv_ready, 1)
            pe.wait_ge(lru_in, 32)
            for h in range(HA):
                for g in range(2):
                    ins = pe.matmul(use(U_LRU + h)[:, g * SEQ:(g + 1) * SEQ], lru_w[:, g, h, :], conv_a[:, h, :],
                                    start=True, stop=True)
                ins.then_inc(aux_full, 1)
            pieces(17, 21, "w")
            for j in range(HC // 2):
                pe.wait_ge(y_sq, j + 1)
                sums(U_YC + j, proj[:, BLK_K + 2 * j:BLK_K + 2 * j + 2, :])
            for j in range(HA // 2):
                pe.wait_ge(y_sq, HC // 2 + j + 1)
                sums(U_YA + j, proj[:, BLK_XA + 2 * j:BLK_XA + 2 * j + 2, :])
            for j in range(HB // 2):
                pe.wait_ge(y_sq, HC // 2 + HA // 2 + j + 1)
                sums(U_YB + j, proj[:, BLK_CG + 2 * j:BLK_CG + 2 * j + 2, :])
            piece(N_IN, N_IN % 2, "y")
            piece(N_IN + 1, (N_IN + 1) % 2, "y")
            pieces(N_IN + 2, N_MIX, "y")

            for c in range(0, KC, 2):
                if c == 0:
                    pe.wait_ge(h2_ready, TILES)
                    pe.wait_ge(proj_free, T_USES + N_MIX)
                if c >= 8:
                    pe.wait_ge(h2T_free, c // 2 - 3)
                for k in range(2):
                    for t in range(TILES):
                        ins = pe.transpose(bank[(c // 2) % 4][:, k * SEQ + t * P:k * SEQ + (t + 1) * P],
                                           h2_perm[:, t, c + k, :], ident[:, :])
                ins.then_inc(h2T_full, 1)
            pe.wait_ge(router_in, 64)
            pe.wait_ge(aux_free, U_END)
            NR = NG + NE
            for t in range(TILES):
                dst = bank[4][:, t * NR:(t + 1) * NR]
                for c in range(KC):
                    if t == 0 and c % 2 == 0:
                        pe.wait_ge(h2T_free, c // 2 + 1)
                    pe.matmul(dst, h2T[:, c, t * P:(t + 1) * P], w_rt[:, c, :], start=(c == 0), stop=False)
                ins = pe.matmul(dst, ones[0:1, :], b_rt[0:1, :], start=False, stop=True)
            ins.then_inc(logits_full, 1)
            pe.wait_ge(sel_ready, 1)
            pe.matmul(bank[5][:, 0:NE], before[:, :], sel_b[:, 0, :], start=True, stop=True)
            pe.matmul(bank[5][:, NE:2 * NE], ones_b[:, :], sel_b[:, 0, :], start=True, stop=False)
            pe.matmul(bank[5][:, NE:2 * NE], before[:, :], sel_b[:, 1, :], start=False, stop=True)
            pe.matmul(bank[5][:, 2 * NE:3 * NE], ones_b[:, :], sel_b[:, 0, :], start=True, stop=False)
            pe.matmul(bank[5][:, 2 * NE:3 * NE], ones_b[:, :], sel_b[:, 1, :], start=False, stop=True).then_inc(rank_full, 1)

            def combine(q, back, items):
                pe.wait_ge(y_out_act, items)
                pe.wait_ge(y_out_dve, items)
                pe.wait_ge(give_ready, q + (1 - back))
                for b in range(8):
                    if b >= 2:
                        pe.wait_ge(acc_done, q * 8 + (b - 1 - 8 * back))
                    pe.matmul(b_comb[b % 2][:, :], give[:, b // 4, :], y_exp[:, (b % 4) * 512:(b % 4 + 1) * 512],
                              start=True, stop=True).then_inc(comb_full, 1)

            def gather(q):
                pe.wait_ge(pick_ready, q + 1)
                for b in range(4):
                    if not (isinstance(q, int) and b < 2):
                        pe.wait_ge(gath_out, q * 4 + (b - 1))
                    for c in range(4):
                        for t in range(TILES):
                            ins = pe.matmul(b_gath[b % 2][:, c * P:(c + 1) * P], h2_perm[:, t, 4 * b + c, :],
                                            pick[:, t].rearrange("p i s -> p (i s)"), start=(t == 0), stop=(t == 1))
                    ins.then_inc(gath_full, 1)

            def item_step(q, k):
                i = q * QI + k
                first = isinstance(q, int) and i == 0
                cols = slice(SLOTS * k, SLOTS * (k + 1))
                if k == 0:
                    pe.wait_ge(gath_out, q * 4 + 4)
                for p in range(4):
                    pe.wait_ge(piece_in[MOE_PLACE[p]], piece_count(p, i))
                    dst = (b_gate, b_up)[p % 2]
                    if p < 2 and not first:
                        pe.wait_ge((gate_out, up_out)[p], i)
                    for cc in range(H):
                        c = (p // 2) * H + cc
                        j = c % 4
                        ins = pe.matmul(dst[SLOTS * j:SLOTS * (j + 1), :], x_exp[:, c, cols],
                                        place(p)[:, cc * F:(cc + 1) * F], start=(c < 4), stop=(c >= KC - 4))
                    ins.then_inc(piece_used, 1)
                pe.wait_ge(gate_out, i + 1)
                pe.wait_ge(up_out, i + 1)
                if not first:
                    pe.wait_ge(hid_ready, i)
                if k == 0:
                    pe.wait_ge(give_ready, q + 1)
                for m, part in enumerate((gate_sb, up_sb)):
                    for f in range(FC):
                        ins = pe.matmul(b_fold[:, m * P + f * SLOTS:m * P + (f + 1) * SLOTS],
                                        part[:, :].rearrange("p (k f) -> p f k", f=FC)[:, f, :], fold[:, :],
                                        start=True, stop=True)
                ins.then_inc(fold_full, 1)
                pe.wait_ge(hid_ready, i + 1)
                if not first:
                    pe.wait_ge(y_out_act, i)
                    pe.wait_ge(y_out_dve, i)
                for p in range(2):
                    pe.wait_ge(piece_in[MOE_PLACE[4 + p]], piece_count(4 + p, i))
                    for ff in range(FC // 2):
                        f = p * (FC // 2) + ff
                        for n in range(4):
                            ins = pe.matmul(b_down[SLOTS * n:SLOTS * (n + 1), :], hidT[:, f, :],
                                            place(4 + p)[:, ff * D + n * 512:ff * D + (n + 1) * 512],
                                            start=(f == 0), stop=(f == FC - 1))
                    ins.then_inc(piece_used, 1)

            def quad(q, n_extra=None):
                if not isinstance(q, int):
                    combine(q, 1, q * QI)
                gather(q)
                if not isinstance(q, int):
                    pe.wait_ge(give_ready, q)
                    pe.wait_ge(hid_ready, q * QI)
                for t in range(TILES):
                    ins = pe.transpose(b_fold[:, (2 + t) * P:(3 + t) * P],
                                       pick_gate[:, t].rearrange("p i s -> p (i s)"), ident[:, :])
                ins.then_inc(give_full, 1)
                for k in range(QI):
                    if n_extra is None:
                        item_step(q, k)
                    else:
                        with pe.If(n_extra > (q - QUADS) * QI + k):
                            item_step(q, k)

            quad(0)
            with pe.Fori(1, QUADS) as q:
                quad(q)
            pe.wait_ge(table_ready, 1)
            n_extra = pe.value_load(tab[0:1, 0:1], min_val=0, max_val=NX - 1)
            last_quad = pe.value_load(tab[0:1, 1:2], min_val=0, max_val=QUADS + XQ - 1)
            with pe.Fori(QUADS, QUADS + XQ) as q:
                with pe.If(n_extra > (q - QUADS) * QI):
                    quad(q, n_extra)
            combine(last_quad, 0, n_extra + NE)


_INS = ['x', 'norm_mix', 'w_in', 'conv_a_w', 'conv_a_b', 'lru_wa', 'lru_ba', 'lru_wx', 'lru_bx', 'lru_lam',
        'conv_b_w', 'q_norm', 'k_norm', 'mix_norm', 'w_out', 'norm_ffn', 'w_router_group', 'b_router_group',
        'w_router_expert', 'b_router_expert', 'w_gate', 'w_up', 'w_down']


def kernel(**inputs):
    import concourse.bacc as _bacc
    from concourse.bass_utils import run_bass_kernel_spmd as _run

    nc = _bacc.Bacc("TRN2", target_bir_lowering=False, num_devices=1)
    arrays, args = {}, []
    for name in _INS:
        a = np.ascontiguousarray(inputs[name])
        arrays[f"in_{name}"] = a
        args.append(nc.dram_tensor(f"in_{name}", a.shape, mybir.dt.from_np(a.dtype), kind="ExternalInput").ap())
    args.append(nc.dram_tensor("out_0", inputs["x"].shape, F32, kind="ExternalOutput").ap())
    hymba_layer(nc, *args)
    r = _run(nc, [arrays], core_ids=[0])
    return r.results[0]["out_0"]
```

```python
from contextlib import ExitStack

import numpy as np

import concourse.bass as bass
from concourse import mybir

F32 = mybir.dt.float32
F32R = mybir.dt.float32r
BF16 = mybir.dt.bfloat16
I32 = mybir.dt.int32
ALU = mybir.AluOpType
ACT = mybir.ActivationFunctionType
AX = mybir.AxisListType.X

P = 128
EPS = 1e-6
MASKED = -1e30
LRU_C = 8.0
POLY_BELOW = 0.25


def hymba_layer(nc, x, norm_mix, w_in, conv_a_w, conv_a_b, lru_wa, lru_ba, lru_wx, lru_bx, lru_lam,
                conv_b_w, q_norm, k_norm, mix_norm, w_out, norm_ffn, w_router_group, b_router_group,
                w_router_expert, b_router_expert, w_gate, w_up, w_down, out):
    _, SEQ, D = x.shape
    TILES = SEQ // P
    KC = D // P
    CONV_A, D_LRU = conv_a_w.shape[1:]
    CONV_B, D_CONV = conv_b_w.shape[1:]
    HA, HB = D_LRU // P, D_CONV // P
    HC = (w_in.shape[2] - 2 * D_LRU - 3 * D_CONV) // 3 // P
    NG = w_router_group.shape[2]
    NE = w_router_expert.shape[2]
    EG = NE // NG
    F = w_gate.shape[3]
    FC = F // P
    assert (TILES, KC, FC, HA, HB, HC) == (2, 16, 4, 6, 4, 6)

    PW = 256
    PIECE = KC * PW * 4
    MIX_RING, MOE_RING = 4, 8
    BLK_XA, BLK_GA, BLK_BG = 0, HA, 2 * HA
    BLK_CG, BLK_XB = BLK_BG + HB, BLK_BG + 2 * HB
    BLK_Q = BLK_BG + 3 * HB
    BLK_K, BLK_V = BLK_Q + HC, BLK_Q + 2 * HC
    order = ([(BLK_Q + b) for b in range(0, HC, 2)] + [(BLK_K + b) for b in range(0, HC, 2)]
             + [(BLK_XA + b) for b in range(0, HA, 2)] + [(BLK_V + b) for b in range(0, HC, 2)]
             + [(BLK_GA + b) for b in range(0, HA, 2)] + [(BLK_XB + b) for b in range(0, HB, 2)]
             + [(BLK_CG + b) for b in range(0, HB, 2)] + [(BLK_BG + b) for b in range(0, HB, 2)])
    N_IN = len(order)
    N_OUT = D // PW
    N_MIX = N_IN + N_OUT
    S_XA, S_V, S_GA, S_XB, S_CG, S_BG = 6, 9, 12, 15, 17, 19
    Y_ORDER = (3, 0, 1, 2)

    PARTS = 6
    SLOTS = 32
    QI = 4
    QUADS = NE // QI
    XQ = 4
    NX = XQ * QI
    NI = NE + NX + QI
    H = KC // 2

    x_t = x[0].rearrange("(t p) d -> t p d", p=P)
    out_t = out[0].rearrange("(t p) d -> t p d", p=P)
    w_in_p = w_in[0].rearrange("(p c) n -> p c n", c=KC)
    w_out_p = w_out[0].rearrange("(c p) n -> p c n", p=P)
    w_gate_p = w_gate[0].rearrange("e (p c) f -> e p c f", c=KC)
    w_up_p = w_up[0].rearrange("e (p c) f -> e p c f", c=KC)
    w_down_p = w_down[0].rearrange("e (p c) n -> e p c n", c=FC)

    with ExitStack() as ctx:
        def sem(name):
            return ctx.enter_context(nc.semaphore(name))

        base = 16512

        def at(name, shape, dt, offset):
            return nc.alloc_sbuf_tensor_at(name, [P] + shape, dt, offset=base + offset)

        o_proj = 6 * PIECE + TILES * D * 4 + 2 * KC * SEQ * 4
        w_hi = at("w_hi", [4, 4, PW], F32R, 4 * PIECE)
        w_lo = at("w_lo", [4, 4, PW], F32R, 5 * PIECE)
        ring_at = [i * PIECE for i in range(6)] + [o_proj + 16 * SEQ * 4 + i * PIECE for i in range(2)]
        ring = [at(f"ring{i}", [KC * PW], F32, ring_at[i]) for i in range(MOE_RING)]
        o = 6 * PIECE
        x_acc = at("x_acc", [TILES, D], F32, o)
        conv_a = at("conv_a", [HA, SEQ], F32, o)
        lru_u = at("lru_u", [HA, SEQ], F32, o + HA * SEQ * 4)
        o += TILES * D * 4
        hT_hi = at("hT_hi", [KC, SEQ], F32R, o)
        y_hi = at("y_hi", [KC, SEQ], F32R, o)
        x_exp = at("x_exp", [KC, QI * SLOTS], F32, o)
        y_exp = at("y_exp", [D], F32, o + 8192)
        o += KC * SEQ * 4
        hT_lo = at("hT_lo", [KC, SEQ], F32R, o)
        y_lo = at("y_lo", [KC, SEQ], F32R, o)
        gate_sb = at("gate_sb", [F], F32, o)
        up_sb = at("up_sb", [F], F32, o + 2048)
        silu_sb = at("silu_sb", [FC, SLOTS], F32, o + 4096)
        hidT = at("hidT", [FC, SLOTS], F32, o + 4608)
        pick = at("pick", [TILES, QI, SLOTS], F32, o + 5120)
        pick_gate = at("pick_gate", [TILES, QI, SLOTS], F32, o + 6144)
        give = at("give", [TILES, P], F32, o + 7168)
        rank_item = at("rank_item", [TILES, NI], F32, o + 8192)
        gate_item = at("gate_item", [TILES, NI], F32, o + 8704)
        small = at("small", [640], F32, o + 9216)
        logitsT = at("logitsT", [SEQ], F32, o + 12288)
        o += KC * SEQ * 4
        h_perm = at("h_perm", [TILES, KC, P], F32, o)
        proj = at("proj", [BLK_V, SEQ], F32, o)
        x2_perm = at("x2_perm", [TILES, KC, P], F32, o)
        lru_w = at("lru_w", [2, HA, P], F32, o + BLK_BG * SEQ * 4)
        lru_a = at("lru_a", [HA, SEQ], F32, o + BLK_BG * SEQ * 4)
        scores2 = at("scores2", [2, 2, TILES * P + P], F32, o + BLK_K * SEQ * 4)
        o += BLK_V * SEQ * 4
        v_tok = at("v_tok", [TILES, HC * P], F32, o)
        o += TILES * HC * P * 4
        gain_row = at("gain_row", [D], F32, o)
        temp = at("temp", [12, SEQ], F32, o)
        scores0 = at("scores0", [2, 2, TILES * P + P], F32, o)
        scores1 = at("scores1", [2, 2, TILES * P + P], F32, o + 6 * SEQ * 4)
        x2T = at("x2T", [2, 2, SEQ], F32, o + 6 * SEQ * 4)
        cross = at("cross", [NX + QI, NE], F32, o + 6 * SEQ * 4)
        match = at("match", [NX + QI, NE], F32, o + 6 * SEQ * 4 + (NX + QI) * NE * 4)
        o += 12 * SEQ * 4
        ident = at("ident", [P], F32, o)
        ones = at("ones", [P], F32, o + 512)
        w_rt = at("w_rt", [KC, NG + NE], F32, o + 1024)
        o += 1024 + KC * (NG + NE) * 4
        before = at("before", [P], BF16, o)
        ones_b = at("ones_b", [P], BF16, o + 256)
        fold = at("fold", [SLOTS], F32, o + 512)
        iota_s = at("iota_s", [SLOTS], F32, o + 640)
        prm_rows = at("prm_rows", [P], F32, o + 768)
        prm = at("prm", [96], F32, o + 1280)
        gain_ffn = at("gain_ffn", [KC], F32, o + 1664)
        b_rt = at("b_rt", [NG + NE], F32, o + 1728)
        desc = at("desc", [12], F32, o + 1888)
        iota_e = at("iota_e", [NX + QI + NE], F32, o + 1952)
        tab = at("tab", [2 + NX], I32, o + 2176)
        c_eps = at("c_eps", [1], F32, o + 2272)
        lru_c = at("lru_c", [HA], F32, o + 2304)
        lru_t = at("lru_t", [3, HA], F32, o + 2336)
        ssq = at("ssq", [TILES, 12], F32, o + 2432)
        sel_b = at("sel_b", [TILES, NE], BF16, o + 2528)
        squares = at("squares", [TILES, PW], F32, o + 2688)
        assert base + o + 2688 + 2048 <= 229344
        scores = [scores0, scores1, scores2]

        R_CA, R_CAB = 0, CONV_A * HA
        R_BA, R_BX, R_LAM = R_CAB + HA, R_CAB + 2 * HA, R_CAB + 3 * HA
        R_CB = R_LAM + HA
        R_MIX = R_CB + CONV_B * HB
        R_Q, R_K = R_MIX + KC, R_MIX + KC + 1
        R_FFN = R_K + 1
        R_ALL = R_FFN + KC

        prm_sources = [(R_CA, conv_a_w[0].rearrange("j (h p) -> (j h) p", p=P)),
                       (R_CAB, conv_a_b[0].rearrange("(h p) -> h p", p=P)),
                       (R_BA, lru_ba[0].rearrange("(h p) -> h p", p=P)),
                       (R_BX, lru_bx[0].rearrange("(h p) -> h p", p=P)),
                       (R_LAM, lru_lam[0].rearrange("(h p) -> h p", p=P)),
                       (R_CB, conv_b_w[0].rearrange("j (h p) -> (j h) p", p=P)),
                       (R_MIX, mix_norm[0].rearrange("(h p) -> h p", p=P)),
                       (R_Q, q_norm), (R_K, k_norm), (R_FFN, norm_ffn[0].rearrange("(h p) -> h p", p=P))]
        PARS = 16 * len(prm_sources)
        ROUTER_PARS = 16 * 5

        bank = [ctx.enter_context(nc.psum_tensor(f"bank{i}", [P, 512], F32)) for i in range(8)]
        AUX = 4
        b_gate, b_up, b_fold, b_down = bank[0], bank[1], bank[2], bank[3]
        b_gath, b_comb = [bank[4], bank[5]], [bank[6], bank[7]]

        x_in, par_in, router_in = [sem(f"x_in{t}") for t in range(TILES)], sem("par_in"), sem("router_in")
        lru_in, x_again, out_done = sem("lru_in"), sem("x_again"), sem("out_done")
        piece_in = [sem(f"piece_in{i}") for i in range(MOE_RING)]
        consts_ready = sem("consts_ready")
        hi_ready, lo_ready = sem("hi_ready"), sem("lo_ready")
        quarter_used = sem("quarter_used")
        proj_free = sem("proj_free")
        aux_full, aux_free = sem("aux_full"), sem("aux_free")
        act_step, dve_step, pool_step = sem("act_step"), sem("dve_step"), sem("pool_step")
        ssq_ready, var_ready, std_ready = sem("ssq_ready"), sem("var_ready"), sem("std_ready")
        gain_in, h_ready, hT_full = sem("gain_in"), sem("h_ready"), sem("hT_full")
        hT_hi_ready, hT_ready = sem("hT_hi_ready"), sem("hT_ready")
        prm_ready = sem("prm_ready")
        lam_abs, lam_exp = sem("lam_abs"), sem("lam_exp")
        qk_sq, qk_ready = sem("qk_sq"), sem("qk_ready")
        conv_ready = sem("conv_ready")
        z_masked, ln_ready = sem("z_masked"), sem("ln_ready")
        logw_ready, w_ready, wT_ready = sem("logw_ready"), sem("w_ready"), sem("wT_ready")
        sig_ready, y2_ready = sem("sig_ready"), sem("y2_ready")
        decay_ready, gated_in = sem("decay_ready"), sem("gated_in")
        expm1_ready, root_ready = sem("expm1_ready"), sem("root_ready")
        u_ready, lru_out = sem("u_ready"), sem("lru_out")
        gelu_ready, ya_ready = sem("gelu_ready"), sem("ya_ready")
        cx_ready, yb_ready = sem("cx_ready"), sem("yb_ready")
        rstd_ready = sem("rstd_ready")
        y_sq, y_norm, y_split = sem("y_sq"), sem("y_norm"), sem("y_split")
        y_hi_ready = sem("y_hi_ready")
        x2_ready, ssq2_ready = sem("x2_ready"), sem("ssq2_ready")
        x2_perm_ready = sem("x2_perm_ready")
        x2T_full, x2T_ready, x2T_used = sem("x2T_full"), sem("x2T_ready"), sem("x2T_used")
        logitsT_full, logitsT_ready = sem("logitsT_full"), sem("logitsT_ready")
        logits_full, e_ready, sub_ready = sem("logits_full"), sem("e_ready"), sem("sub_ready")
        sel_ready, rank_full = sem("sel_ready"), sem("rank_full")
        table_ready = sem("table_ready")
        piece_used = sem("piece_used")
        fold_full = sem("fold_full")
        gate_out, up_out = sem("gate_out"), sem("up_out")
        silu_ready, hid_ready = sem("silu_ready"), sem("hid_ready")
        y_out_act, y_out_dve = sem("y_out_act"), sem("y_out_dve")
        comb_full, acc_done = sem("comb_full"), sem("acc_done")
        gath_full, gath_out = sem("gath_full"), sem("gath_out")
        pick_made, pick_ready = sem("pick_made"), sem("pick_ready")
        give_full, give_ready = sem("give_full"), sem("give_ready")

        MOE_ORDER = [6, 7] + [(N_MIX + i) % MIX_RING for i in range(MIX_RING)] + [4, 5]
        MIX_USES = [len(range(i, N_MIX, MIX_RING)) for i in range(MIX_RING)] + [0] * 4
        PER_QUAD = PARTS * QI
        assert PER_QUAD % MOE_RING == 0

        def place_of(k, i):
            return MOE_ORDER[(PARTS * k + i) % MOE_RING]

        def piece_count(q, k, i):
            rounds = (PARTS * k + i) // MOE_RING + 1 + MIX_USES[place_of(k, i)]
            return q * (16 * PER_QUAD // MOE_RING) + 16 * rounds

        def piece_source(i, e):
            if i < 4:
                return (w_gate_p, w_up_p)[i % 2][e][:, (i // 2) * H:(i // 2 + 1) * H, :]
            return w_down_p[e][:, (i - 4) * (FC // 2):(i - 3) * (FC // 2), :]

        U_PRM = 0
        U_QK = 1
        U_Z = U_QK + HC
        U_LRU = U_Z + HC
        U_WT = U_LRU + HA
        U_PV = U_WT + HC
        U_YC = U_PV + HC // 2
        U_YA = U_YC + HC // 2
        U_YB = U_YA + HA // 2
        U_END = U_YB + HB // 2

        def aux(u):
            return bank[AUX + u % 4]

        def proj_bank(n, b):
            return bank[2 * (n % 2) + b]

        def y_block(c):
            return BLK_GA + c if c < HA + HB else BLK_Q + c - HA - HB

        Y_RUNS = {3: [(12, 16)], 2: [(8, 10), (10, 12)], 1: [(4, 8)], 0: [(0, 4)]}
        Y_NEED = {3: 3, 0: 5, 1: 7, 2: 8}

        block = ctx.enter_context(nc.Block())

        @block.sync
        def _(sp):
            for t in range(TILES):
                sp.dma_start(x_acc[:, t, :], x_t[t]).then_inc(x_in[t], 16)
            sp.dma_start(gain_row[:, :], norm_mix.to_broadcast([P, D])).then_inc(gain_in, 16)

            def parameters():
                sp.wait_ge(consts_ready, 1)
                for r, src in prm_sources:
                    sp.dma_start(prm_rows[r:r + src.shape[0], :], src).then_inc(par_in, 16)

            def router_parameters():
                sp.dma_start(w_rt[:, :, 0:NG], w_router_group[0].rearrange("(c p) g -> p c g", p=P)).then_inc(router_in, 16)
                sp.dma_start(w_rt[:, :, NG:], w_router_expert[0].rearrange("(c p) g -> p c g", p=P)).then_inc(router_in, 16)
                sp.dma_start(b_rt[:, 0:NG], b_router_group.to_broadcast([P, NG])).then_inc(router_in, 16)
                sp.dma_start(b_rt[:, NG:], b_router_expert.to_broadcast([P, NE])).then_inc(router_in, 16)
                sp.dma_start(gain_ffn[:, :], norm_ffn[0].rearrange("(p c) -> p c", c=KC)).then_inc(router_in, 16)
                sp.wait_ge(hT_full, KC // 2)
                sp.dma_start(lru_w[:, 0], lru_wa[0].rearrange("h i j -> i h j")).then_inc(lru_in, 16)
                sp.dma_start(lru_w[:, 1], lru_wx[0].rearrange("h i j -> i h j")).then_inc(lru_in, 16)

            for n in range(N_MIX):
                if n >= MIX_RING:
                    sp.wait_ge(lo_ready, 4 * (n - MIX_RING) + 4)
                dst = ring[n % MIX_RING][:, :].rearrange("p (c n) -> p c n", c=KC)
                if n < N_IN:
                    src = w_in_p[:, :, order[n] * P:order[n] * P + PW]
                else:
                    src = w_out_p[:, :, (n - N_IN) * PW:(n - N_IN + 1) * PW]
                sp.dma_start(dst, src).then_inc(piece_in[n % MIX_RING], 16)
                if n == 1:
                    parameters()
                if n == MIX_RING - 1:
                    router_parameters()
                if n == N_IN + 1:
                    sp.wait_ge(lru_out, 1)
                    for t in range(TILES):
                        sp.dma_start(x_acc[:, t, :], x_t[t]).then_inc(x_again, 16)

            def quad(q, n_extra=None):
                def item_pieces(k, e):
                    for i in range(PARTS):
                        m = PARTS * k + i
                        if isinstance(q, int) and m < 2:
                            sp.wait_ge(y_split, 4)
                        elif isinstance(q, int) and m < 6:
                            sp.wait_ge(lo_ready, 4 * (N_MIX - 6 + m) + 4)
                        elif isinstance(q, int) and m < 8:
                            sp.wait_ge(quarter_used, 4 * N_MIX)
                        else:
                            sp.wait_ge(piece_used, q * PER_QUAD + (m - MOE_RING + 1))
                        place = place_of(k, i)
                        sp.dma_start(ring[place][:, :], piece_source(i, e)).then_inc(piece_in[place], 16)

                for k in range(QI):
                    if n_extra is None:
                        item_pieces(k, q * QI + k)
                    else:
                        with sp.If(n_extra > (q - QUADS) * QI + k):
                            item_pieces(k, sp.value_load(tab[0:1, bass.ds((q - QUADS) * QI + (k + 2), 1)],
                                                         min_val=0, max_val=NE - 1))

            quad(0)
            with sp.Fori(1, QUADS) as q:
                quad(q)
            sp.wait_ge(table_ready, 1)
            n_extra = sp.value_load(tab[0:1, 0:1], min_val=0, max_val=NX - 1)
            last_quad = sp.value_load(tab[0:1, 1:2], min_val=0, max_val=QUADS + XQ - 1)
            with sp.Fori(QUADS, QUADS + XQ) as q:
                with sp.If(n_extra > (q - QUADS) * QI):
                    quad(q, n_extra)
            for b in range(8):
                t, n = b // 4, b % 4
                sp.wait_ge(acc_done, last_quad * 8 + (b + 1))
                sp.dma_start(out_t[t][:, n * 512:(n + 1) * 512], x_acc[:, t, n * 512:(n + 1) * 512]).then_inc(out_done, 16)
            sp.wait_ge(out_done, 16 * 8)

        @block.gpsimd
        def _(pool):
            steps = [0]

            def ordered(ins):
                steps[0] += 1
                ins.then_inc(pool_step, 1)
                pool.wait_ge(pool_step, steps[0])

            pool.memset(ident[:, :], 0.0)
            pool.memset(fold[:, :], 0.0)
            pool.memset(prm_rows[:, :], 0.0).then_inc(consts_ready, 1)
            pool.memset(ones[:, :], 1.0)
            pool.memset(ones_b[:, :], 1.0)
            pool.memset(c_eps[:, :], EPS)
            pool.memset(before[:, :], 1.0)
            pool.iota(iota_s[:, :], [[1, SLOTS]], base=0, channel_multiplier=0,
                      allow_small_or_imprecise_dtypes=True)
            pool.iota(iota_e[:, 0:NE], [[1, NE]], base=0, channel_multiplier=0,
                      allow_small_or_imprecise_dtypes=True)
            pool.iota(iota_e[:, NE:NE + NX + QI], [[1, NX + QI]], base=0, channel_multiplier=0,
                      allow_small_or_imprecise_dtypes=True)
            ordered(pool.iota(desc[:, :], [[-1, 12]], base=12, channel_multiplier=0,
                              allow_small_or_imprecise_dtypes=True))
            pool.affine_select(out=ident[:, :], in_=ident[:, :], compare_op=ALU.not_equal, fill=1.0,
                               base=0, pattern=[[-1, P]], channel_multiplier=1)
            for j in range(P // SLOTS):
                pool.affine_select(out=fold[:, :], in_=fold[:, :], compare_op=ALU.not_equal, fill=1.0,
                                   base=-SLOTS * j, pattern=[[-1, SLOTS]], channel_multiplier=1)
                if j + 1 < P // SLOTS:
                    ordered(pool.iota(small[:, 0:1], [[0, 1]], base=0, channel_multiplier=0,
                                      allow_small_or_imprecise_dtypes=True))
            pool.affine_select(out=before[:, :], in_=before[:, :], compare_op=ALU.is_gt, fill=0.0,
                               base=0, pattern=[[1, P]], channel_multiplier=-1).then_inc(consts_ready, 1)
            def square_blocks(dst, src, ready):
                pool.tensor_tensor(dst, src, src, ALU.mult).then_inc(ready, 1)

            for j in range(HC):
                pool.wait_ge(proj_free, j + 1)
                b = BLK_Q + 2 * j
                square_blocks(temp[:, 2 * j:2 * j + 2, :], proj[:, b:b + 2, :], qk_sq)
            for b in range(HC // 2):
                z = scores[b][:, 0]
                pool.wait_ge(aux_free, U_Z + 2 * b + 2)
                for part in (z[:, :, 0:P], z[:, :, 2 * P:3 * P]):
                    ins = pool.affine_select(out=part, in_=part, compare_op=ALU.is_gt, fill=MASKED,
                                             base=0, pattern=[[0, 2], [-1, P]], channel_multiplier=1)
                ins.then_inc(z_masked, 1)
            pool.wait_ge(aux_free, U_LRU + HA)
            pool.tensor_tensor(lru_u[:, :, :], lru_u[:, :, :], conv_a[:, :, :], ALU.mult).then_inc(gated_in, 1)
            pool.wait_ge(root_ready, 1)
            pool.tensor_tensor(lru_u[:, :, :], lru_u[:, :, :], conv_a[:, :, :], ALU.mult).then_inc(u_ready, 1)
            pool.wait_ge(aux_free, U_PV + HC // 2)
            for j in range(HC // 2):
                b = BLK_Q + 2 * j
                square_blocks(proj[:, BLK_K + 2 * j:BLK_K + 2 * j + 2, :], proj[:, b:b + 2, :], y_sq)
            pool.wait_ge(lru_out, 1)
            pool.wait_ge(gelu_ready, 1)
            ordered(pool.tensor_tensor(proj[:, BLK_GA:BLK_GA + HA, :], proj[:, BLK_GA:BLK_GA + HA, :],
                                       proj[:, BLK_XA:BLK_XA + HA, :], ALU.mult))
            for j in range(HA // 2):
                b = BLK_GA + 2 * j
                square_blocks(proj[:, BLK_XA + 2 * j:BLK_XA + 2 * j + 2, :], proj[:, b:b + 2, :], y_sq)
            pool.wait_ge(proj_free, S_BG)
            pool.tensor_tensor(proj[:, BLK_XB:BLK_XB + HB, :], proj[:, BLK_XB:BLK_XB + HB, :],
                               proj[:, BLK_CG:BLK_CG + HB, :], ALU.mult).then_inc(cx_ready, 1)
            for j in range(HB // 2):
                pool.wait_ge(yb_ready, j + 1)
                b = BLK_BG + 2 * j
                square_blocks(proj[:, BLK_CG + 2 * j:BLK_CG + 2 * j + 2, :], proj[:, b:b + 2, :], y_sq)
            for k in range(N_OUT):
                pool.wait_ge(proj_free, N_IN + k + 1)
                rows = slice(k * PW // KC, (k + 1) * PW // KC)
                for t in range(TILES):
                    ins = pool.tensor_copy(x2_perm[:, t, :, rows].rearrange("p c k -> p k c"),
                                           x_acc[:, t, k * PW:(k + 1) * PW].rearrange("p (k c) -> p k c", c=KC))
                ins.then_inc(x2_perm_ready, 1)

        @block.scalar
        def _(act):
            steps = [0]

            def ordered(ins):
                steps[0] += 1
                ins.then_inc(act_step, 1)
                act.wait_ge(act_step, steps[0])


            act.wait_ge(x_in[0], 16)
            act.activation(h_perm[:, 0].rearrange("p a b -> p (a b)"), x_acc[:, 0, :], ACT.Square,
                           accum_out=ssq[:, 0, 0:1]).then_inc(ssq_ready, 1)
            act.wait_ge(var_ready, 1)
            act.activation(ssq[:, :, 2:3], ssq[:, :, 1:2], ACT.Sqrt).then_inc(std_ready, 1)

            def hT_high():
                for j in range(KC // 2):
                    act.wait_ge(hT_full, j + 1)
                    act.activation(hT_hi[:, 2 * j:2 * j + 2, :], bank[j][:, :].rearrange("p (c t) -> p c t", c=2),
                                   ACT.Copy).then_inc(hT_hi_ready, 1)

            def parameters():
                act.wait_ge(aux_full, U_PRM + 1)
                act.activation(prm[:, 0:R_ALL], aux(U_PRM)[:, 0:R_ALL], ACT.Copy).then_inc(aux_free, 1)
                act.wait_ge(aux_free, U_PRM + 1)
                ordered(act.activation(lru_t[:, 0, :], prm[:, R_LAM:R_LAM + HA], ACT.Abs))
                act.activation(lru_t[:, 1, :], lru_t[:, 0, :], ACT.Exp, scale=-1.0).then_inc(lam_exp, 1)

            def split_high(n, quarters=range(4)):
                if 0 in quarters:
                    act.wait_ge(piece_in[n % MIX_RING], 16 * (n // MIX_RING + 1))
                for k in quarters:
                    g = 4 * n + k
                    if g >= 4:
                        act.wait_ge(quarter_used, g - 3)
                    kk = k if n < N_IN else Y_ORDER[k]
                    src = ring[n % MIX_RING][:, kk * 4 * PW:(kk + 1) * 4 * PW]
                    act.activation(w_hi[:, k].rearrange("p c n -> p (c n)"), src, ACT.Copy).then_inc(hi_ready, 1)

            def empty_projection(n):
                act.wait_ge(quarter_used, 4 * n + 4)
                for b in range(2):
                    src = proj_bank(n, b)[:, 0:PW]
                    if order[n] < BLK_V:
                        dst = proj[:, order[n] + b, :]
                    else:
                        c0 = (order[n] - BLK_V) * P
                        dst = v_tok[:, b, c0:c0 + PW]
                    ins = act.activation(dst, src, ACT.Copy)
                ins.then_inc(proj_free, 1)

            def stick_scores(b):
                z = scores[b][:, 0]
                act.wait_ge(aux_full, U_Z + 2 * b + 1)
                act.activation(z[:, :, P:3 * P], aux(U_Z + 2 * b)[:, :].rearrange("p (h k) -> p h k", h=2),
                               ACT.Copy, scale=float(P) ** -0.5).then_inc(aux_free, 1)
                act.wait_ge(aux_full, U_Z + 2 * b + 2)
                act.activation(z[:, :, 0:P], aux(U_Z + 2 * b + 1)[:, 0:2 * P].rearrange("p (h k) -> p h k", h=2),
                               ACT.Copy, scale=float(P) ** -0.5).then_inc(aux_free, 1)

            def stick_log(b):
                z, t = scores[b][:, 0], scores[b][:, 1]
                act.wait_ge(z_masked, b + 1)
                ordered(act.activation(t, z, ACT.Abs))
                ordered(act.activation(t, t, ACT.Exp, scale=-1.0))
                act.activation(t, t, ACT.Ln, bias=1.0).then_inc(ln_ready, 1)

            def stick_weights(b):
                act.wait_ge(logw_ready, b + 1)
                act.activation(scores[b][:, 0], scores[b][:, 1], ACT.Exp).then_inc(w_ready, 1)

            def weights_transposed(h):
                act.wait_ge(aux_full, U_WT + h + 1)
                act.activation(scores[h // 2][:, 1, h % 2, :], aux(U_WT + h)[:, 0:3 * P], ACT.Copy).then_inc(aux_free, 1)

            def attention_out(b):
                act.wait_ge(aux_full, U_PV + b + 1)
                act.activation(proj[:, BLK_Q + 2 * b:BLK_Q + 2 * b + 2, :],
                               aux(U_PV + b)[:, :].rearrange("p (h k) -> p h k", h=2), ACT.Copy).then_inc(aux_free, 1)

            def lru_gates():
                for h in range(HA):
                    u = U_LRU + h
                    act.wait_ge(aux_full, u + 1)
                    act.activation(proj[:, BLK_XA + h, :], aux(u)[:, 0:SEQ], ACT.Sigmoid,
                                   bias=prm[:, R_BA + h:R_BA + h + 1])
                    act.activation(lru_u[:, h, :], aux(u)[:, SEQ:2 * SEQ], ACT.Sigmoid,
                                   bias=prm[:, R_BX + h:R_BX + h + 1]).then_inc(aux_free, 1)

            def norm_rstd(uses, dst):
                for j, u in enumerate(uses):
                    act.wait_ge(aux_full, u + 1)
                    d = dst[:, 2 * j:2 * j + 2, :]
                    act.activation(d, aux(u)[:, :].rearrange("p (h k) -> p h k", h=2), ACT.Ln, scale=1.0 / P,
                                   bias=c_eps[:, 0:1]).then_inc(aux_free, 1)
                    act.wait_ge(aux_free, u + 1)
                    act.activation(d, d, ACT.Exp, scale=-0.5).then_inc(rstd_ready, 1)

            def y_split_high(quarter):
                act.wait_ge(y_norm, Y_NEED[quarter])
                c0 = 4 * quarter
                for a, b in Y_RUNS[quarter]:
                    ins = act.activation(y_hi[:, a:b, :], proj[:, y_block(a):y_block(a) + b - a, :], ACT.Copy)
                ins.then_inc(y_hi_ready, 1)

            def after_residual(k):
                act.wait_ge(proj_free, N_IN + k + 1)
                if k > 0:
                    act.wait_ge(ssq2_ready, k)
                for t in range(TILES):
                    ins = act.activation(squares[:, t, :], x_acc[:, t, k * PW:(k + 1) * PW], ACT.Square,
                                         accum_out=ssq[:, t, 4 + k:5 + k])
                ins.then_inc(ssq2_ready, 1)

            def transposed_x2(k):
                act.wait_ge(x2T_full, k + 1)
                if k >= 2:
                    act.wait_ge(x2T_used, k - 1)
                for c in range(2):
                    ins = act.activation(x2T[:, k % 2, c, :], bank[AUX + k % 2][:, c * SEQ:(c + 1) * SEQ], ACT.Copy,
                                         scale=prm[:, R_FFN + 2 * k + c:R_FFN + 2 * k + c + 1])
                ins.then_inc(x2T_ready, 1)

            for n in range(N_MIX):
                if n == N_IN:
                    split_high(n, range(3))
                    act.wait_ge(quarter_used, 4 * N_IN)
                    y_split_high(Y_ORDER[0])
                    empty_projection(n - 1)
                    split_high(n, range(3, 4))
                else:
                    split_high(n)
                    if n == 0:
                        hT_high()
                    elif n < N_IN:
                        empty_projection(n - 1)
                if n == 1:
                    parameters()
                if n == 8:
                    norm_rstd(range(U_QK, U_Z), temp)
                if n == 11:
                    for b in range(HC // 2):
                        stick_scores(b)
                    stick_log(0)
                    stick_log(1)
                if n == 12:
                    stick_log(2)
                    stick_weights(0)
                    lru_gates()
                if n == 13:
                    stick_weights(1)
                    stick_weights(2)
                    act.wait_ge(y2_ready, 1)
                    y = proj[:, BLK_XA:BLK_XA + HA, :]
                    ordered(act.activation(lru_a[:, :, :], y, ACT.Exp, scale=-0.5))
                    act.activation(y, y, ACT.Tanh, scale=0.5).then_inc(decay_ready, 1)
                if n == 14:
                    for h in range(HC):
                        weights_transposed(h)
                if n == 15:
                    act.wait_ge(expm1_ready, 1)
                    act.activation(conv_a[:, :, :], conv_a[:, :, :], ACT.Sqrt).then_inc(root_ready, 1)
                if n == 16:
                    for b in range(HC // 2):
                        attention_out(b)
                    act.wait_ge(proj_free, S_XB)
                    act.activation(proj[:, BLK_GA:BLK_GA + HA, :], proj[:, BLK_GA:BLK_GA + HA, :],
                                   ACT.Gelu_apprx_tanh).then_inc(gelu_ready, 1)
                if n == 20:
                    norm_rstd(range(U_YC, U_YA), proj[:, BLK_K:BLK_K + HC, :])
                    norm_rstd(range(U_YA, U_YB), proj[:, BLK_XA:BLK_XA + HA, :])
                if n == N_IN:
                    y_split_high(Y_ORDER[1])
                    norm_rstd(range(U_YB, U_YB + 1), proj[:, BLK_CG:BLK_CG + 2, :])
                    y_split_high(Y_ORDER[2])
                    norm_rstd(range(U_YB + 1, U_END), proj[:, BLK_CG + 2:BLK_CG + HB, :])
                    y_split_high(Y_ORDER[3])
                if n > N_IN:
                    after_residual(n - N_IN - 1)
                if n > N_IN + 1:
                    transposed_x2(n - N_IN - 2)
            after_residual(N_OUT - 1)
            act.wait_ge(var_ready, 2)
            act.activation(ssq[:, :, 2:3], ssq[:, :, 1:2], ACT.Sqrt).then_inc(std_ready, 1)
            transposed_x2(N_OUT - 2)
            transposed_x2(N_OUT - 1)
            act.wait_ge(sub_ready, 1)
            act.activation(small[:, 0:TILES * NG], small[:, 0:TILES * NG], ACT.Exp).then_inc(e_ready, 1)
            act.wait_ge(sub_ready, 2)
            act.activation(small[:, 16:16 + TILES * EG], small[:, 16:16 + TILES * EG], ACT.Exp).then_inc(e_ready, 1)

            def item_step(q, k):
                i = q * QI + k
                act.wait_ge(piece_used, i * PARTS + 3)
                if not (isinstance(q, int) and i == 0):
                    act.wait_ge(fold_full, i)
                act.activation(gate_sb[:, :], b_gate[:, :], ACT.Copy).then_inc(gate_out, 1)
                act.wait_ge(fold_full, i + 1)
                if not (isinstance(q, int) and i == 0):
                    act.wait_ge(hid_ready, i)
                act.activation(silu_sb[:, :, :], b_fold[:, 0:P].rearrange("p (f s) -> p f s", f=FC),
                               ACT.Silu).then_inc(silu_ready, 1)
                act.wait_ge(piece_used, i * PARTS + 6)
                if not isinstance(q, int):
                    act.wait_ge(comb_full, q * 8)
                for n in range(2):
                    ins = act.activation(y_exp[SLOTS * k:SLOTS * (k + 1), n * 512:(n + 1) * 512],
                                         b_down[SLOTS * n:SLOTS * (n + 1), :], ACT.Copy)
                ins.then_inc(y_out_act, 1)

            def quad(q, n_extra=None):
                act.wait_ge(give_full, q + 1)
                act.activation(give[:, :, :], b_fold[:, 2 * P:4 * P].rearrange("p (t s) -> p t s", t=TILES),
                               ACT.Copy).then_inc(give_ready, 1)
                for k in range(QI):
                    if n_extra is None:
                        item_step(q, k)
                    else:
                        with act.If(n_extra > (q - QUADS) * QI + k):
                            item_step(q, k)

            quad(0)
            with act.Fori(1, QUADS) as q:
                quad(q)
            act.wait_ge(table_ready, 1)
            n_extra = act.value_load(tab[0:1, 0:1], min_val=0, max_val=NX - 1)
            with act.Fori(QUADS, QUADS + XQ) as q:
                with act.If(n_extra > (q - QUADS) * QI):
                    quad(q, n_extra)

        @block.vector
        def _(dve):
            steps = [0]

            def ordered(ins):
                steps[0] += 1
                ins.then_inc(dve_step, 1)
                dve.wait_ge(dve_step, steps[0])

            def token_rstd(round_):
                dve.wait_ge(std_ready, round_)
                r, v, w = ssq[:, :, 2:3], ssq[:, :, 1:2], ssq[:, :, 3:4]
                ordered(dve.reciprocal(r, r))
                ordered(dve.tensor_tensor(w, r, r, ALU.mult))
                ordered(dve.tensor_tensor(w, w, v, ALU.mult))
                ordered(dve.tensor_scalar(w, w, -0.5, 1.5, ALU.mult, ALU.add))
                ordered(dve.tensor_tensor(r, r, w, ALU.mult))

            dve.wait_ge(x_in[1], 16)
            dve.scalar_tensor_tensor(h_perm[:, 1].rearrange("p a b -> p (a b)"), x_acc[:, 1, :], 1.0, x_acc[:, 1, :],
                                     ALU.mult, ALU.mult, accum_out=ssq[:, 1, 0:1]).then_inc(ssq_ready, 1)
            dve.wait_ge(ssq_ready, TILES)
            dve.tensor_scalar(ssq[:, :, 1:2], ssq[:, :, 0:1], 1.0 / D, EPS, ALU.mult, ALU.add).then_inc(var_ready, 1)
            dve.wait_ge(var_ready, 1)
            token_rstd(1)
            dve.wait_ge(gain_in, 16)
            dve.wait_ge(x_in[0], 16)
            for t in range(TILES):
                dve.scalar_tensor_tensor(h_perm[:, t].rearrange("p c k -> p k c"),
                                         x_acc[:, t, :].rearrange("p (k c) -> p k c", c=KC), ssq[:, t, 2:3],
                                         gain_row[:, :].rearrange("p (k c) -> p k c", c=KC),
                                         ALU.mult, ALU.mult).then_inc(h_ready, 1)

            def hT_low(quarter):
                for j in (2 * quarter, 2 * quarter + 1):
                    dve.wait_ge(hT_hi_ready, j + 1)
                    dve.tensor_tensor(hT_lo[:, 2 * j:2 * j + 2, :], bank[j][:, :].rearrange("p (c t) -> p c t", c=2),
                                      hT_hi[:, 2 * j:2 * j + 2, :].bitcast(F32), ALU.subtract).then_inc(hT_ready, 1)

            def softplus_lam():
                dve.wait_ge(lam_exp, 1)
                e_, s_, s2 = lru_t[:, 1, :], lru_t[:, 0, :], lru_t[:, 2, :]
                ordered(dve.tensor_scalar(s_, e_, 2.0, None, ALU.add))
                ordered(dve.reciprocal(s_, s_))
                ordered(dve.tensor_tensor(s_, s_, e_, ALU.mult))
                ordered(dve.tensor_tensor(s2, s_, s_, ALU.mult))
                ordered(dve.tensor_scalar(lru_c[:, :], s2, 1.0 / 19, None, ALU.mult))
                for k in range(8, 0, -1):
                    ordered(dve.scalar_tensor_tensor(lru_c[:, :], lru_c[:, :], 1.0 / (2 * k + 1), s2, ALU.add, ALU.mult))
                ordered(dve.scalar_tensor_tensor(lru_c[:, :], lru_c[:, :], 1.0, s_, ALU.add, ALU.mult))
                ordered(dve.tensor_scalar(s2, prm[:, R_LAM:R_LAM + HA], -1.0, 0.0, ALU.mult, ALU.max))
                ordered(dve.scalar_tensor_tensor(lru_c[:, :], lru_c[:, :], 2.0, s2, ALU.mult, ALU.add))
                ordered(dve.tensor_scalar(lru_c[:, :], lru_c[:, :], 2 * LRU_C, None, ALU.mult))

            def split_low(n, quarters=range(4)):
                for k in quarters:
                    g = 4 * n + k
                    dve.wait_ge(hi_ready, g + 1)
                    if g >= 4:
                        dve.wait_ge(quarter_used, g - 3)
                    kk = k if n < N_IN else Y_ORDER[k]
                    src = ring[n % MIX_RING][:, kk * 4 * PW:(kk + 1) * 4 * PW]
                    dve.tensor_tensor(w_lo[:, k].rearrange("p c n -> p (c n)"), src,
                                      w_hi[:, k].rearrange("p c n -> p (c n)").bitcast(F32),
                                      ALU.subtract).then_inc(lo_ready, 1)

            def normalise_qk(pairs):
                for j in pairs:
                    dve.wait_ge(rstd_ready, j + 1)
                    for b in range(2):
                        blk = BLK_Q + 2 * j + b
                        gain = R_Q if blk < BLK_K else R_K
                        ins = dve.scalar_tensor_tensor(proj[:, blk, :], proj[:, blk, :], prm[:, gain:gain + 1],
                                                       temp[:, 2 * j + b, :], ALU.mult, ALU.mult)
                    ins.then_inc(qk_ready, 1)

            def causal_conv(dst, src, taps, tap_col, bias_col, blocks, dst0, src0, ready=None):
                for h in range(blocks):
                    d, s = dst[:, dst0 + h, :], src[:, src0 + h, :]
                    last = tap_col(taps - 1, h)
                    if bias_col is None:
                        ins = dve.tensor_scalar(d, s, prm[:, last:last + 1], None, ALU.mult)
                    else:
                        ins = dve.tensor_scalar(d, s, prm[:, last:last + 1],
                                                prm[:, bias_col + h:bias_col + h + 1], ALU.mult, ALU.add)
                ordered(ins)
                for back in range(1, taps):
                    for h in range(blocks):
                        d, s = dst[:, dst0 + h, :], src[:, src0 + h, :]
                        w = tap_col(taps - 1 - back, h)
                        ins = dve.scalar_tensor_tensor(d[:, back:], s[:, 0:SEQ - back], prm[:, w:w + 1],
                                                       d[:, back:], ALU.mult, ALU.add)
                    if back < taps - 1 or ready is None:
                        ordered(ins)
                    else:
                        ins.then_inc(ready, 1)

            def stick(b):
                z, t = scores[b][:, 0], scores[b][:, 1]
                dve.wait_ge(ln_ready, b + 1)
                ordered(dve.scalar_tensor_tensor(t, z, 0.0, t, ALU.max, ALU.add))
                for h in range(2):
                    for a, e in ((0, P), (P, 3 * P)):
                        back = t[:, h, a:e][:, ::-1]
                        ins = dve.tensor_tensor_scan(back, back, back, 0.0, ALU.add, ALU.max)
                ordered(ins)
                dve.tensor_tensor(t, z, t, ALU.subtract).then_inc(logw_ready, 1)

            def normalise_y(pairs, done, rstd, first, chunk0):
                for j in range(pairs):
                    dve.wait_ge(rstd_ready, HC + done + j + 1)
                    for b in range(2):
                        blk, c = first + 2 * j + b, chunk0 + 2 * j + b
                        ins = dve.scalar_tensor_tensor(proj[:, blk, :], proj[:, blk, :],
                                                       prm[:, R_MIX + c:R_MIX + c + 1],
                                                       proj[:, rstd + 2 * j + b, :], ALU.mult, ALU.mult)
                    ins.then_inc(y_norm, 1)

            def y_split_low(k):
                dve.wait_ge(y_hi_ready, k + 1)
                for a, b in Y_RUNS[Y_ORDER[k]]:
                    ins = dve.tensor_tensor(y_lo[:, a:b, :], proj[:, y_block(a):y_block(a) + b - a, :],
                                            y_hi[:, a:b, :].bitcast(F32), ALU.subtract)
                ins.then_inc(y_split, 1)

            def gated_conv(j):
                dve.wait_ge(proj_free, S_BG + 1 + j)
                b = 2 * j
                dve.tensor_tensor(proj[:, BLK_BG + b:BLK_BG + b + 2, :], proj[:, BLK_BG + b:BLK_BG + b + 2, :],
                                  proj[:, BLK_CG + b:BLK_CG + b + 2, :], ALU.mult).then_inc(yb_ready, 1)

            def residual(k):
                dve.wait_ge(quarter_used, 4 * (N_IN + k) + 4)
                if k == 0:
                    dve.wait_ge(x_again, 16 * TILES)
                for t in range(TILES):
                    dst = x_acc[:, t, k * PW:(k + 1) * PW]
                    ins = dve.tensor_tensor(dst, dst, proj_bank(N_IN + k, t)[:, 0:PW], ALU.add)
                ins.then_inc(proj_free, 1)

            y_, w_ = proj[:, BLK_XA:BLK_XA + HA, :], conv_a[:, :, :]

            for n in range(N_MIX):
                if n == N_IN:
                    split_low(n, range(3))
                    y_split_low(0)
                    gated_conv(1)
                    split_low(n, range(3, 4))
                elif n == 0:
                    for k in range(4):
                        split_low(0, range(k, k + 1))
                        hT_low(k)
                else:
                    split_low(n)
                if n == 2:
                    softplus_lam()
                if n == 8:
                    normalise_qk(range(0, HC // 2))
                if n == 9:
                    normalise_qk(range(HC // 2, HC))
                if n == 10:
                    dve.wait_ge(proj_free, S_V)
                    causal_conv(conv_a, proj, CONV_A, lambda j, h: R_CA + j * HA + h, R_CAB, HA, 0, BLK_XA,
                                conv_ready)
                if n == 11:
                    stick(0)
                if n == 12:
                    stick(1)
                    stick(2)
                if n == 13:
                    dve.wait_ge(aux_free, U_LRU + HA)
                    for h in range(HA):
                        ins = dve.tensor_scalar(proj[:, BLK_XA + h, :], proj[:, BLK_XA + h, :],
                                                lru_c[:, h:h + 1], None, ALU.mult)
                    ins.then_inc(y2_ready, 1)
                if n == 14:
                    dve.wait_ge(decay_ready, 1)
                    dve.wait_ge(gated_in, 1)
                    ordered(dve.tensor_tensor(w_, lru_a[:, :, :], lru_a[:, :, :], ALU.mult))
                    dve.scalar_tensor_tensor(w_, w_, 1.0, y_, ALU.add, ALU.mult).then_inc(expm1_ready, 1)
                if n == 16:
                    dve.wait_ge(u_ready, 1)
                    for h in range(HA):
                        ins = dve.tensor_tensor_scan(proj[:, BLK_XA + h, :], lru_a[:, h, :], lru_u[:, h, :], 0.0,
                                                     ALU.mult, ALU.add)
                    ins.then_inc(lru_out, 1)
                if n == 19:
                    dve.wait_ge(cx_ready, 1)
                    causal_conv(proj, proj, CONV_B, lambda j, h: R_CB + j * HB + h, None, HB, BLK_CG, BLK_XB)
                if n == 20:
                    gated_conv(0)
                    normalise_y(HC // 2, 0, BLK_K, BLK_Q, HA + HB)
                    normalise_y(HA // 2, HC // 2, BLK_XA, BLK_GA, 0)
                if n == N_IN:
                    y_split_low(1)
                    normalise_y(1, (HC + HA) // 2, BLK_CG, BLK_BG, HA)
                    y_split_low(2)
                    normalise_y(1, (HC + HA) // 2 + 1, BLK_CG + 2, BLK_BG + 2, HA + 2)
                    y_split_low(3)
                if n > N_IN:
                    residual(n - N_IN - 1)
            residual(N_OUT - 1)

            dve.wait_ge(ssq2_ready, N_OUT)
            ordered(dve.tensor_reduce(ssq[:, :, 0:1], ssq[:, :, 4:4 + N_OUT], AX, ALU.add))
            dve.tensor_scalar(ssq[:, :, 1:2], ssq[:, :, 0:1], 1.0 / D, EPS, ALU.mult, ALU.add).then_inc(var_ready, 1)
            dve.wait_ge(var_ready, 2)
            token_rstd(2)
            dve.wait_ge(logitsT_full, 1)
            dve.tensor_copy(logitsT[0:NG + NE, :], bank[AUX + 2][0:NG + NE, 0:SEQ]).then_inc(logitsT_ready, 1)

            def take(n, shape, a=[48]):
                v = small[:, a[0]:a[0] + n]
                a[0] += n
                names = "tgj"[:len(shape)] if len(shape) < 3 else "tgj"
                if len(shape) == 2:
                    return v.rearrange("p (t g) -> p t g", t=shape[0])
                return v.rearrange("p (t g j) -> p t g j", t=shape[0], g=shape[1])

            TT = TILES
            g_exp = small[:, 0:TT * NG].rearrange("p (t g) -> p t g", t=TT)
            e_exp = small[:, 16:16 + TT * EG].rearrange("p (t g) -> p t g", t=TT)
            lg = take(TT * (NG + NE), (TT, NG + NE))
            g_one = take(TT * NG, (TT, NG))
            t4 = take(TT * NG, (TT, NG))
            m = take(TT, (TT, 1))
            pg = take(TT, (TT, 1))
            m1, m2, mm = take(TT, (TT, 1)), take(TT, (TT, 1)), take(TT, (TT, 1))
            ing = take(TT * EG, (TT, EG))
            one1, one2, t8 = take(TT * EG, (TT, EG)), take(TT * EG, (TT, EG)), take(TT * EG, (TT, EG))
            big = take(TT * NE, (TT, NG, EG))
            sel = take(TT * NE, (TT, NG, EG))
            cnt = take(NE, (1, NE))[:, 0]
            excl = take(NE, (1, NE))[:, 0]
            incl = take(NE, (1, NE))[:, 0]
            ntab = take(2 + NX + QI, (1, 2 + NX + QI))[:, 0]

            def wide(a, n):
                return a.to_broadcast([P, TT, n])

            def first_max(one, p, n, mx, tmp):
                ordered(dve.tensor_reduce(mx, p, AX, ALU.max))
                ordered(dve.tensor_tensor(tmp, p, wide(mx, n), ALU.is_equal))
                ordered(dve.tensor_tensor(tmp, tmp, desc[:, 0:n].unsqueeze(1).to_broadcast([P, TT, n]), ALU.mult))
                ordered(dve.tensor_reduce(mm, tmp, AX, ALU.max))
                ordered(dve.tensor_tensor(one, tmp, wide(mm, n), ALU.is_equal))

            dve.wait_ge(logits_full, 1)
            dve.wait_ge(router_in, ROUTER_PARS)
            for t in range(TILES):
                ins = dve.scalar_tensor_tensor(lg[:, t], bank[AUX + 3][:, t * (NG + NE):(t + 1) * (NG + NE)],
                                               ssq[:, t, 2:3], b_rt[:, :], ALU.mult, ALU.add)
            ordered(ins)
            first_max(g_one, lg[:, :, 0:NG], NG, m, t4)
            dve.tensor_tensor(g_exp, lg[:, :, 0:NG], wide(m, NG), ALU.subtract).then_inc(sub_ready, 1)
            ordered(dve.tensor_tensor(big, lg[:, :, NG:].rearrange("p t (g j) -> p t g j", g=NG),
                                      g_one.unsqueeze(3).to_broadcast([P, TT, NG, EG]), ALU.mult))
            ordered(dve.tensor_reduce(ing, big.transpose([0, 1, 3, 2]), AX, ALU.add))
            ordered(dve.tensor_reduce(m1, ing, AX, ALU.max))
            dve.tensor_tensor(e_exp, ing, wide(m1, EG), ALU.subtract).then_inc(sub_ready, 1)
            dve.wait_ge(e_ready, 1)
            ordered(dve.tensor_reduce(pg, g_exp, AX, ALU.add))
            ordered(dve.reciprocal(pg, pg))
            dve.wait_ge(e_ready, 2)
            ordered(dve.tensor_reduce(m, e_exp, AX, ALU.add))
            ordered(dve.reciprocal(m, m))
            ordered(dve.tensor_tensor(e_exp, e_exp, wide(m, EG), ALU.mult))
            first_max(one1, e_exp, EG, m1, t8)
            ordered(dve.scalar_tensor_tensor(e_exp, one1, -2.0, e_exp, ALU.mult, ALU.add))
            first_max(one2, e_exp, EG, m2, t8)
            ordered(dve.tensor_tensor(m, m1, m2, ALU.add))
            ordered(dve.reciprocal(m, m))
            ordered(dve.tensor_tensor(m1, m1, m, ALU.mult))
            ordered(dve.tensor_tensor(m2, m2, m, ALU.mult))
            ordered(dve.tensor_tensor(m1, m1, pg, ALU.mult))
            ordered(dve.tensor_tensor(m2, m2, pg, ALU.mult))
            ordered(dve.tensor_tensor(t8, one1, one2, ALU.add))
            g4 = g_one.unsqueeze(3).to_broadcast([P, TT, NG, EG])
            ordered(dve.tensor_tensor(sel, g4, t8.unsqueeze(2).to_broadcast([P, TT, NG, EG]), ALU.mult))
            dve.tensor_copy(sel_b[:, :, :], sel.rearrange("p t g j -> p t (g j)")).then_inc(sel_ready, 1)
            ordered(dve.tensor_tensor(one1, one1, wide(m1, EG), ALU.mult))
            ordered(dve.tensor_tensor(one2, one2, wide(m2, EG), ALU.mult))
            ordered(dve.tensor_tensor(one1, one1, one2, ALU.add))
            gates = gate_item[:, :, 0:NE]
            ordered(dve.tensor_tensor(gates.rearrange("p t (g j) -> p t g j", g=NG), g4,
                                      one1.unsqueeze(2).to_broadcast([P, TT, NG, EG]), ALU.mult))
            ranks = rank_item[:, :, 0:NE]
            dve.wait_ge(rank_full, 1)
            ordered(dve.scalar_tensor_tensor(ranks, bank[5][:, 0:TT * NE].rearrange("p (t e) -> p t e", t=TT), 1.0,
                                             sel.rearrange("p t g j -> p t (g j)"), ALU.add, ALU.mult))
            ordered(dve.tensor_copy(cnt, bank[5][:, TT * NE:(TT + 1) * NE]))
            ordered(dve.tensor_scalar(ranks, ranks, -1.0, None, ALU.add))

            def make_pick(q, mark):
                r = rank_item[:, :, bass.ds(q * QI, QI)]
                g = gate_item[:, :, bass.ds(q * QI, QI)]
                for t in range(TILES):
                    ins = dve.tensor_tensor(pick[:, t], r[:, t].unsqueeze(2).to_broadcast([P, QI, SLOTS]),
                                            iota_s[:, :].unsqueeze(1).to_broadcast([P, QI, SLOTS]), ALU.is_equal)
                ins.then_inc(pick_made, 1)
                dve.wait_ge(pick_made, mark + mark - 1)
                for t in range(TILES):
                    ins = dve.tensor_tensor(pick_gate[:, t], pick[:, t],
                                            g[:, t].unsqueeze(2).to_broadcast([P, QI, SLOTS]), ALU.mult)
                ins.then_inc(pick_made, 1)
                dve.wait_ge(pick_made, mark + mark)
                for t in range(TILES):
                    ins = dve.tensor_scalar(pick[:, t], pick[:, t], ssq[:, t, 2:3], None, ALU.mult)
                ins.then_inc(pick_ready, 1)

            make_pick(0, 1)

            ordered(dve.tensor_scalar(incl, cnt, float(SLOTS), None, ALU.is_gt))
            for k in range(2, SEQ // SLOTS):
                ordered(dve.scalar_tensor_tensor(incl, cnt, float(SLOTS * k), incl, ALU.is_gt, ALU.add))
            ordered(dve.tensor_copy(excl, incl))
            ordered(dve.tensor_tensor_scan(incl, excl, excl, 0.0, ALU.add, ALU.max))
            ordered(dve.tensor_tensor(excl, incl, excl, ALU.subtract))
            M = NX + QI
            it = iota_e[:, NE:NE + M]
            by_item = it.unsqueeze(2).to_broadcast([P, M, NE])

            def by_expert(a):
                return a.unsqueeze(1).to_broadcast([P, M, NE])

            mt, cr = match[:, :, :], cross[:, :, :]
            ordered(dve.tensor_tensor(mt, by_item, by_expert(excl), ALU.is_ge))
            ordered(dve.tensor_tensor(cr, by_item, by_expert(incl), ALU.is_lt))
            ordered(dve.tensor_tensor(mt, mt, cr, ALU.mult))
            ordered(dve.tensor_tensor(cr, mt, by_expert(iota_e[:, 0:NE]), ALU.mult))
            ordered(dve.tensor_reduce(ntab[:, 2:2 + M], cr, AX, ALU.add))
            ordered(dve.tensor_copy(ntab[:, 0:1], incl[:, NE - 1:NE]))
            ordered(dve.tensor_scalar(ntab[:, 1:2], ntab[:, 0:1], 0.0, float(QUADS - 1), ALU.is_gt, ALU.add))
            for k in range(1, XQ):
                ordered(dve.scalar_tensor_tensor(ntab[:, 1:2], ntab[:, 0:1], float(QI * k), ntab[:, 1:2],
                                                 ALU.is_gt, ALU.add))
            dve.tensor_copy(tab[:, :], ntab[:, 0:2 + NX]).then_inc(table_ready, 1)
            for t in range(TILES):
                ordered(dve.tensor_tensor(cr, by_item, by_expert(excl), ALU.subtract))
                ordered(dve.tensor_scalar(cr, cr, -float(SLOTS), -float(SLOTS) + 1.0, ALU.mult, ALU.add))
                ordered(dve.tensor_tensor(cr, cr, by_expert(rank_item[:, t, 0:NE]), ALU.add))
                ordered(dve.tensor_tensor(cr, cr, mt, ALU.mult))
                ordered(dve.tensor_reduce(rank_item[:, t, NE:NE + M], cr, AX, ALU.add))
                ordered(dve.tensor_scalar(rank_item[:, t, NE:NE + M], rank_item[:, t, NE:NE + M], -1.0, None, ALU.add))
                ordered(dve.tensor_tensor(cr, mt, by_expert(gate_item[:, t, 0:NE]), ALU.mult))
                ordered(dve.tensor_reduce(gate_item[:, t, NE:NE + M], cr, AX, ALU.add))

            def gather_out(q):
                for b in range(4):
                    dve.wait_ge(gath_full, q * 4 + (b + 1))
                    if not isinstance(q, int) and b == 0:
                        dve.wait_ge(piece_used, q * PER_QUAD - 2)
                    dve.tensor_tensor(x_exp[:, 4 * b:4 * b + 4, :],
                                      b_gath[b % 2][:, :].rearrange("p (c s) -> p c s", c=4),
                                      gain_ffn[:, 4 * b:4 * b + 4].unsqueeze(2).to_broadcast([P, 4, P]),
                                      ALU.mult).then_inc(gath_out, 1)

            def accumulate(q, back):
                for b in range(8):
                    t, n = b // 4, b % 4
                    dve.wait_ge(comb_full, q * 8 + (b + 1 - 8 * back))
                    dst = x_acc[:, t, n * 512:(n + 1) * 512]
                    dve.tensor_tensor(dst, dst, b_comb[b % 2][:, :], ALU.add).then_inc(acc_done, 1)

            def item_step(q, k):
                i = q * QI + k
                first = isinstance(q, int) and i == 0
                dve.wait_ge(piece_used, i * PARTS + 4)
                if not first:
                    dve.wait_ge(fold_full, i)
                dve.tensor_copy(up_sb[:, :], b_up[:, :]).then_inc(up_out, 1)
                dve.wait_ge(silu_ready, i + 1)
                if not first:
                    dve.wait_ge(piece_used, i * PARTS)
                dve.tensor_tensor(hidT[:, :, :], silu_sb[:, :, :],
                                  b_fold[:, P:2 * P].rearrange("p (f s) -> p f s", f=FC),
                                  ALU.mult).then_inc(hid_ready, 1)
                dve.wait_ge(piece_used, i * PARTS + 6)
                if not isinstance(q, int):
                    dve.wait_ge(comb_full, q * 8)
                for n in range(2, 4):
                    ins = dve.tensor_copy(y_exp[SLOTS * k:SLOTS * (k + 1), n * 512:(n + 1) * 512],
                                          b_down[SLOTS * n:SLOTS * (n + 1), :])
                ins.then_inc(y_out_dve, 1)

            def quad(q, n_extra=None):
                if not isinstance(q, int):
                    accumulate(q, 1)
                gather_out(q)
                dve.wait_ge(give_full, q + 1)
                make_pick(q + 1, q + 2)
                for k in range(QI):
                    if n_extra is None:
                        item_step(q, k)
                    else:
                        with dve.If(n_extra > (q - QUADS) * QI + k):
                            item_step(q, k)

            quad(0)
            with dve.Fori(1, QUADS) as q:
                quad(q)
            n_extra = dve.value_load(tab[0:1, 0:1], min_val=0, max_val=NX - 1)
            last_quad = dve.value_load(tab[0:1, 1:2], min_val=0, max_val=QUADS + XQ - 1)
            with dve.Fori(QUADS, QUADS + XQ) as q:
                with dve.If(n_extra > (q - QUADS) * QI):
                    quad(q, n_extra)
            accumulate(last_quad, 0)

        @block.tensor
        def _(pe):
            pe.wait_ge(consts_ready, 2)
            for t in range(TILES):
                pe.wait_ge(h_ready, t + 1)
                for j in range(KC // 2):
                    for c in range(2):
                        ins = pe.transpose(bank[j][:, c * SEQ + t * P:c * SEQ + (t + 1) * P],
                                           h_perm[:, t, 2 * j + c, :], ident[:, :])
                    if t == TILES - 1:
                        ins.then_inc(hT_full, 1)

            def piece(n, parity, kind):
                if not (isinstance(n, int) and n < 2):
                    pe.wait_ge(proj_free, n - 1)
                for k in range(4):
                    pe.wait_ge(lo_ready, n * 4 + (k + 1))
                    if isinstance(n, int) and n == 0:
                        pe.wait_ge(hT_ready, 2 * k + 2)
                    if isinstance(n, int) and n == N_IN:
                        if k == 2:
                            yb_sums(1)
                        pe.wait_ge(y_split, k + 1)
                    for cc in range(4):
                        c = 4 * (Y_ORDER[k] if kind == "y" else k) + cc
                        for b in range(2):
                            dst = bank[2 * parity + b][:, 0:PW]
                            hi, lo = w_hi[:, k, cc, :], w_lo[:, k, cc, :]
                            cols = slice(b * P, (b + 1) * P)
                            if kind == "w":
                                trio = [(hi[:, cols], hT_hi[:, c, :]), (hi[:, cols], hT_lo[:, c, :]),
                                        (lo[:, cols], hT_hi[:, c, :])]
                            else:
                                a_hi, a_lo = (y_hi, y_lo) if kind == "y" else (hT_hi, hT_lo)
                                trio = [(a_hi[:, c, cols], hi), (a_hi[:, c, cols], lo), (a_lo[:, c, cols], hi)]
                            for j, (stationary, moving) in enumerate(trio):
                                ins = pe.matmul(dst, stationary, moving, start=(k == 0 and cc == 0 and j == 0),
                                                stop=(k == 3 and cc == 3 and j == 2))
                    ins.then_inc(quarter_used, 1)

            def pieces(first, last, kind):
                with pe.Fori(first, last, 2) as n:
                    piece(n, first % 2, kind)
                    piece(n + 1, (first + 1) % 2, kind)

            def use(u):
                if u >= 4:
                    pe.wait_ge(aux_free, u - 3)
                return aux(u)

            def sums(u, squares):
                for b in range(2):
                    ins = pe.matmul(use(u)[:, b * SEQ:(b + 1) * SEQ], ones[:, :], squares[:, b, :], start=True, stop=True)
                ins.then_inc(aux_full, 1)

            def yb_sums(j):
                pe.wait_ge(y_sq, (HC + HA) // 2 + j + 1)
                sums(U_YB + j, proj[:, BLK_CG + 2 * j:BLK_CG + 2 * j + 2, :])

            piece(0, 0, "w")
            pe.wait_ge(par_in, PARS)
            pe.transpose(aux(U_PRM)[:, 0:P], prm_rows[:, :], ident[:, :]).then_inc(aux_full, 1)
            piece(1, 1, "w")
            pieces(2, 8, "w")
            for j in range(HC):
                pe.wait_ge(qk_sq, j + 1)
                sums(U_QK + j, temp[:, 2 * j:2 * j + 2, :])
            piece(8, 0, "w")
            piece(9, 1, "h")
            piece(10, 0, "h")
            pe.wait_ge(qk_ready, HC)
            for b in range(HC // 2):
                u = U_Z + 2 * b
                for h in range(2):
                    q, k = proj[:, BLK_Q + 2 * b + h, :], proj[:, BLK_K + 2 * b + h, :]
                    ins = pe.matmul(use(u)[:, h * SEQ:(h + 1) * SEQ], q[:, P:2 * P], k, start=True, stop=True)
                ins.then_inc(aux_full, 1)
                for h in range(2):
                    q, k = proj[:, BLK_Q + 2 * b + h, :], proj[:, BLK_K + 2 * b + h, :]
                    ins = pe.matmul(use(u + 1)[:, h * P:(h + 1) * P], q[:, 0:P], k[:, 0:P], start=True, stop=True)
                ins.then_inc(aux_full, 1)
            piece(11, 1, "h")
            pe.wait_ge(conv_ready, 1)
            pe.wait_ge(lru_in, 32)
            for h in range(HA):
                for g in range(2):
                    ins = pe.matmul(use(U_LRU + h)[:, g * SEQ:(g + 1) * SEQ], lru_w[:, g, h, :], conv_a[:, h, :],
                                    start=True, stop=True)
                ins.then_inc(aux_full, 1)
            pieces(12, 14, "w")
            for h in range(HC):
                w = scores[h // 2][:, 0, h % 2, :]
                pe.wait_ge(w_ready, h // 2 + 1)
                for k in range(3):
                    ins = pe.transpose(use(U_WT + h)[:, k * P:(k + 1) * P], w[:, k * P:(k + 1) * P], ident[:, :])
                ins.then_inc(aux_full, 1)
            pieces(14, 16, "w")
            for b in range(HC // 2):
                for hh in range(2):
                    h = 2 * b + hh
                    wT = scores[b][:, 1, hh, :]
                    pe.wait_ge(aux_free, U_WT + h + 1)
                    dst = use(U_PV + b)
                    pe.matmul(dst[:, hh * SEQ:(hh + 1) * SEQ], v_tok[:, 0, h * P:(h + 1) * P], wT[:, 0:SEQ],
                              start=True, stop=False)
                    ins = pe.matmul(dst[:, hh * SEQ + P:(hh + 1) * SEQ], v_tok[:, 1, h * P:(h + 1) * P],
                                    wT[:, SEQ:SEQ + P], start=False, stop=True)
                ins.then_inc(aux_full, 1)
            pieces(16, 20, "w")
            for j in range(HC // 2):
                pe.wait_ge(y_sq, j + 1)
                sums(U_YC + j, proj[:, BLK_K + 2 * j:BLK_K + 2 * j + 2, :])
            for j in range(HA // 2):
                pe.wait_ge(y_sq, HC // 2 + j + 1)
                sums(U_YA + j, proj[:, BLK_XA + 2 * j:BLK_XA + 2 * j + 2, :])
            piece(20, 0, "w")
            yb_sums(0)

            NR = NG + NE
            logits_bank = bank[AUX + 2]

            def transpose_x2(k):
                pe.wait_ge(proj_free, N_IN + k + 1)
                if k == 0:
                    pe.wait_ge(aux_free, U_END)
                if k >= 2:
                    pe.wait_ge(x2T_ready, k - 1)
                for c in range(2):
                    for t in range(TILES):
                        ins = pe.transpose(bank[AUX + k % 2][:, c * SEQ + t * P:c * SEQ + (t + 1) * P],
                                           x_acc[:, t, (2 * k + c) * P:(2 * k + c + 1) * P], ident[:, :])
                ins.then_inc(x2T_full, 1)

            def logits(k):
                pe.wait_ge(x2T_ready, k + 1)
                for c in range(2):
                    ins = pe.matmul(logits_bank[0:NR, 0:SEQ], w_rt[:, 2 * k + c, :], x2T[:, k % 2, c, :],
                                    start=(k == 0 and c == 0), stop=(k == N_OUT - 1 and c == 1))
                ins.then_inc(x2T_used if k < N_OUT - 1 else logitsT_full, 1)

            pe.wait_ge(router_in, ROUTER_PARS)
            for k in range(N_OUT):
                piece(N_IN + k, (N_IN + k) % 2, "y")
                if k >= 1:
                    transpose_x2(k - 1)
                if k >= 2:
                    logits(k - 2)
            transpose_x2(N_OUT - 1)
            logits(N_OUT - 2)
            logits(N_OUT - 1)
            pe.wait_ge(logitsT_ready, 1)
            for t in range(TILES):
                ins = pe.transpose(bank[AUX + 3][:, t * NR:(t + 1) * NR], logitsT[0:NR, t * P:(t + 1) * P],
                                   ident[0:NR, 0:NR])
            ins.then_inc(logits_full, 1)
            pe.wait_ge(sel_ready, 1)
            pe.matmul(bank[5][:, 0:NE], before[:, :], sel_b[:, 0, :], start=True, stop=True)
            pe.matmul(bank[5][:, NE:2 * NE], ones_b[:, :], sel_b[:, 0, :], start=True, stop=False)
            pe.matmul(bank[5][:, NE:2 * NE], before[:, :], sel_b[:, 1, :], start=False, stop=True)
            pe.matmul(bank[5][:, 2 * NE:3 * NE], ones_b[:, :], sel_b[:, 0, :], start=True, stop=False)
            pe.matmul(bank[5][:, 2 * NE:3 * NE], ones_b[:, :], sel_b[:, 1, :], start=False, stop=True).then_inc(rank_full, 1)

            def combine(q, back, items):
                pe.wait_ge(y_out_act, items)
                pe.wait_ge(y_out_dve, items)
                pe.wait_ge(give_ready, q + (1 - back))
                for b in range(8):
                    if b >= 2:
                        pe.wait_ge(acc_done, q * 8 + (b - 1 - 8 * back))
                    pe.matmul(b_comb[b % 2][:, :], give[:, b // 4, :], y_exp[:, (b % 4) * 512:(b % 4 + 1) * 512],
                              start=True, stop=True).then_inc(comb_full, 1)

            def gather(q):
                if isinstance(q, int):
                    pe.wait_ge(x2_perm_ready, N_OUT)
                pe.wait_ge(pick_ready, q + 1)
                for b in range(4):
                    if not (isinstance(q, int) and b < 2):
                        pe.wait_ge(gath_out, q * 4 + (b - 1))
                    for c in range(4):
                        for t in range(TILES):
                            ins = pe.matmul(b_gath[b % 2][:, c * P:(c + 1) * P], x2_perm[:, t, 4 * b + c, :],
                                            pick[:, t].rearrange("p i s -> p (i s)"), start=(t == 0), stop=(t == 1))
                    ins.then_inc(gath_full, 1)

            def item_step(q, k):
                i = q * QI + k
                first = isinstance(q, int) and i == 0
                cols = slice(SLOTS * k, SLOTS * (k + 1))
                for p in range(4):
                    weights = ring[place_of(k, p)]
                    pe.wait_ge(piece_in[place_of(k, p)], piece_count(q, k, p))
                    dst = (b_gate, b_up)[p % 2]
                    if p < 2 and not first:
                        pe.wait_ge((gate_out, up_out)[p], i)
                    for cc in range(H):
                        c = (p // 2) * H + cc
                        j = c % 4
                        if k == 0 and p % 2 == 0 and j == 0:
                            pe.wait_ge(gath_out, q * 4 + (c // 4 + 1))
                        ins = pe.matmul(dst[SLOTS * j:SLOTS * (j + 1), :], x_exp[:, c, cols],
                                        weights[:, cc * F:(cc + 1) * F], start=(c < 4), stop=(c >= KC - 4))
                    ins.then_inc(piece_used, 1)
                pe.wait_ge(gate_out, i + 1)
                pe.wait_ge(up_out, i + 1)
                if not first:
                    pe.wait_ge(hid_ready, i)
                if k == 0:
                    pe.wait_ge(give_ready, q + 1)
                for m, part in enumerate((gate_sb, up_sb)):
                    for f in range(FC):
                        ins = pe.matmul(b_fold[:, m * P + f * SLOTS:m * P + (f + 1) * SLOTS],
                                        part[:, :].rearrange("p (k f) -> p f k", f=FC)[:, f, :], fold[:, :],
                                        start=True, stop=True)
                ins.then_inc(fold_full, 1)
                pe.wait_ge(hid_ready, i + 1)
                if not first:
                    pe.wait_ge(y_out_act, i)
                    pe.wait_ge(y_out_dve, i)
                for p in range(2):
                    weights = ring[place_of(k, 4 + p)]
                    pe.wait_ge(piece_in[place_of(k, 4 + p)], piece_count(q, k, 4 + p))
                    for ff in range(FC // 2):
                        f = p * (FC // 2) + ff
                        for n in range(4):
                            ins = pe.matmul(b_down[SLOTS * n:SLOTS * (n + 1), :], hidT[:, f, :],
                                            weights[:, ff * D + n * 512:ff * D + (n + 1) * 512],
                                            start=(f == 0), stop=(f == FC - 1))
                    ins.then_inc(piece_used, 1)

            def quad(q, n_extra=None):
                if not isinstance(q, int):
                    combine(q, 1, q * QI)
                gather(q)
                if not isinstance(q, int):
                    pe.wait_ge(give_ready, q)
                    pe.wait_ge(hid_ready, q * QI)
                for t in range(TILES):
                    ins = pe.transpose(b_fold[:, (2 + t) * P:(3 + t) * P],
                                       pick_gate[:, t].rearrange("p i s -> p (i s)"), ident[:, :])
                ins.then_inc(give_full, 1)
                for k in range(QI):
                    if n_extra is None:
                        item_step(q, k)
                    else:
                        with pe.If(n_extra > (q - QUADS) * QI + k):
                            item_step(q, k)

            quad(0)
            with pe.Fori(1, QUADS) as q:
                quad(q)
            pe.wait_ge(table_ready, 1)
            n_extra = pe.value_load(tab[0:1, 0:1], min_val=0, max_val=NX - 1)
            last_quad = pe.value_load(tab[0:1, 1:2], min_val=0, max_val=QUADS + XQ - 1)
            with pe.Fori(QUADS, QUADS + XQ) as q:
                with pe.If(n_extra > (q - QUADS) * QI):
                    quad(q, n_extra)
            combine(last_quad, 0, n_extra + NE)


_INS = ['x', 'norm_mix', 'w_in', 'conv_a_w', 'conv_a_b', 'lru_wa', 'lru_ba', 'lru_wx', 'lru_bx', 'lru_lam',
        'conv_b_w', 'q_norm', 'k_norm', 'mix_norm', 'w_out', 'norm_ffn', 'w_router_group', 'b_router_group',
        'w_router_expert', 'b_router_expert', 'w_gate', 'w_up', 'w_down']


def kernel(**inputs):
    import concourse.bacc as _bacc
    from concourse.bass_utils import run_bass_kernel_spmd as _run

    nc = _bacc.Bacc("TRN2", target_bir_lowering=False, num_devices=1)
    arrays, args = {}, []
    for name in _INS:
        a = np.ascontiguousarray(inputs[name])
        arrays[f"in_{name}"] = a
        args.append(nc.dram_tensor(f"in_{name}", a.shape, mybir.dt.from_np(a.dtype), kind="ExternalInput").ap())
    args.append(nc.dram_tensor("out_0", inputs["x"].shape, F32, kind="ExternalOutput").ap())
    hymba_layer(nc, *args)
    r = _run(nc, [arrays], core_ids=[0])
    return r.results[0]["out_0"]
```

```python
from contextlib import ExitStack

import numpy as np

import concourse.bass as bass
from concourse import mybir

F32 = mybir.dt.float32
F32R = mybir.dt.float32r
BF16 = mybir.dt.bfloat16
I32 = mybir.dt.int32
ALU = mybir.AluOpType
ACT = mybir.ActivationFunctionType
AX = mybir.AxisListType.X

P = 128
EPS = 1e-6
MASKED = -1e30
LRU_C = 8.0


def hymba_layer(nc, x, norm_mix, w_in, conv_a_w, conv_a_b, lru_wa, lru_ba, lru_wx, lru_bx, lru_lam,
                conv_b_w, q_norm, k_norm, mix_norm, w_out, norm_ffn, w_router_group, b_router_group,
                w_router_expert, b_router_expert, w_gate, w_up, w_down, out):
    _, SEQ, D = x.shape
    TILES = SEQ // P
    KC = D // P
    CONV_A, D_LRU = conv_a_w.shape[1:]
    CONV_B, D_CONV = conv_b_w.shape[1:]
    HA, HB = D_LRU // P, D_CONV // P
    HC = (w_in.shape[2] - 2 * D_LRU - 3 * D_CONV) // 3 // P
    NG = w_router_group.shape[2]
    NE = w_router_expert.shape[2]
    EG = NE // NG
    F = w_gate.shape[3]
    FC = F // P
    assert (TILES, KC, FC, HA, HB, HC) == (2, 16, 4, 6, 4, 6)

    PW = 256
    PIECE = KC * PW * 4
    MIX_RING, MOE_RING = 4, 8
    BLK_XA, BLK_GA, BLK_BG = 0, HA, 2 * HA
    BLK_CG, BLK_XB = BLK_BG + HB, BLK_BG + 2 * HB
    BLK_Q = BLK_BG + 3 * HB
    BLK_K, BLK_V = BLK_Q + HC, BLK_Q + 2 * HC
    order = ([(BLK_Q + b) for b in range(0, HC, 2)] + [(BLK_K + b) for b in range(0, HC, 2)]
             + [(BLK_XA + b) for b in range(0, HA, 2)] + [(BLK_V + b) for b in range(0, HC, 2)]
             + [(BLK_GA + b) for b in range(0, HA, 2)] + [(BLK_XB + b) for b in range(0, HB, 2)]
             + [(BLK_CG + b) for b in range(0, HB, 2)] + [(BLK_BG + b) for b in range(0, HB, 2)])
    N_IN = len(order)
    N_OUT = D // PW
    N_MIX = N_IN + N_OUT
    S_XA, S_V, S_GA, S_XB, S_CG, S_BG = 6, 9, 12, 15, 17, 19
    Y_ORDER = (3, 0, 1, 2)

    PARTS = 6
    SLOTS = 32
    QI = 4
    QUADS = NE // QI
    XQ = 4
    NX = XQ * QI
    NI = NE + NX + QI
    H = KC // 2

    x_t = x[0].rearrange("(t p) d -> t p d", p=P)
    out_t = out[0].rearrange("(t p) d -> t p d", p=P)
    w_in_p = w_in[0].rearrange("(p c) n -> p c n", c=KC)
    w_out_p = w_out[0].rearrange("(c p) n -> p c n", p=P)
    w_gate_p = w_gate[0].rearrange("e (p c) f -> e p c f", c=KC)
    w_up_p = w_up[0].rearrange("e (p c) f -> e p c f", c=KC)
    w_down_p = w_down[0].rearrange("e (p c) n -> e p c n", c=FC)

    with ExitStack() as ctx:
        def sem(name):
            return ctx.enter_context(nc.semaphore(name))

        base = 16512

        def at(name, shape, dt, offset):
            return nc.alloc_sbuf_tensor_at(name, [P] + shape, dt, offset=base + offset)

        o_proj = 6 * PIECE + TILES * D * 4 + 2 * KC * SEQ * 4
        w_hi = at("w_hi", [4, 4, PW], F32R, 4 * PIECE)
        w_lo = at("w_lo", [4, 4, PW], F32R, 5 * PIECE)
        ring_at = [i * PIECE for i in range(6)] + [o_proj + 16 * SEQ * 4 + i * PIECE for i in range(2)]
        ring = [at(f"ring{i}", [KC * PW], F32, ring_at[i]) for i in range(MOE_RING)]
        o = 6 * PIECE
        x_acc = at("x_acc", [TILES, D], F32, o)
        conv_a = at("conv_a", [HA, SEQ], F32, o)
        lru_u = at("lru_u", [HA, SEQ], F32, o + HA * SEQ * 4)
        o += TILES * D * 4
        hT_hi = at("hT_hi", [KC, SEQ], F32R, o)
        y_hi = at("y_hi", [KC, SEQ], F32R, o)
        x_exp = at("x_exp", [KC, QI * SLOTS], F32, o)
        y_exp = at("y_exp", [D], F32, o + 8192)
        o += KC * SEQ * 4
        hT_lo = at("hT_lo", [KC, SEQ], F32R, o)
        y_lo = at("y_lo", [KC, SEQ], F32R, o)
        gate_sb = at("gate_sb", [F], F32, o)
        up_sb = at("up_sb", [F], F32, o + 2048)
        silu_sb = at("silu_sb", [FC, SLOTS], F32, o + 4096)
        hidT = at("hidT", [FC, SLOTS], F32, o + 4608)
        pick = at("pick", [TILES, QI, SLOTS], F32, o + 5120)
        pick_gate = at("pick_gate", [TILES, QI, SLOTS], F32, o + 6144)
        give = at("give", [TILES, P], F32, o + 7168)
        rank_item = at("rank_item", [TILES, NI], F32, o + 8192)
        gate_item = at("gate_item", [TILES, NI], F32, o + 8704)
        small = at("small", [640], F32, o + 9216)
        logitsT = at("logitsT", [SEQ], F32, o + 12288)
        chosen = at("chosen", [TILES, QI, SLOTS], F32, o + 13312)
        o += KC * SEQ * 4
        h_perm = at("h_perm", [TILES, KC, P], F32, o)
        squares_x = at("squares_x", [TILES, D], F32, o + TILES * D * 4)
        proj = at("proj", [BLK_V, SEQ], F32, o)
        x2_perm = at("x2_perm", [TILES, KC, P], F32, o)
        lru_w = at("lru_w", [2, HA, P], F32, o + BLK_BG * SEQ * 4)
        lru_a = at("lru_a", [HA, SEQ], F32, o + BLK_BG * SEQ * 4)
        scores2 = at("scores2", [2, 2, TILES * P + P], F32, o + BLK_K * SEQ * 4)
        o += BLK_V * SEQ * 4
        v_tok = at("v_tok", [TILES, HC * P], F32, o)
        o += TILES * HC * P * 4
        temp = at("temp", [12, SEQ], F32, o)
        scores0 = at("scores0", [2, 2, TILES * P + P], F32, o)
        scores1 = at("scores1", [2, 2, TILES * P + P], F32, o + 6 * SEQ * 4)
        x2T = at("x2T", [2, 2, SEQ], F32, o + 6 * SEQ * 4)
        cross = at("cross", [NX + QI, NE], F32, o + 6 * SEQ * 4)
        match = at("match", [NX + QI, NE], F32, o + 6 * SEQ * 4 + (NX + QI) * NE * 4)
        o += 12 * SEQ * 4
        ident = at("ident", [P], F32, o)
        ones = at("ones", [P], F32, o + 512)
        w_rt = at("w_rt", [KC, NG + NE], F32, o + 1024)
        o += 1024 + KC * (NG + NE) * 4
        before = at("before", [P], BF16, o)
        ones_b = at("ones_b", [P], BF16, o + 256)
        fold = at("fold", [SLOTS], F32, o + 512)
        iota_s = at("iota_s", [SLOTS], F32, o + 640)
        prm_rows = at("prm_rows", [P], F32, o + 768)
        prm = at("prm", [96], F32, o + 1280)
        gain_ffn = at("gain_ffn", [KC], F32, o + 1664)
        b_rt = at("b_rt", [NG + NE], F32, o + 1728)
        desc = at("desc", [12], F32, o + 1888)
        iota_e = at("iota_e", [NX + QI + NE], F32, o + 1952)
        tab = at("tab", [2 + NX], I32, o + 2176)
        c_eps = at("c_eps", [1], F32, o + 2272)
        lru_c = at("lru_c", [HA], F32, o + 2304)
        lru_t = at("lru_t", [3, HA], F32, o + 2336)
        ssq = at("ssq", [TILES, 12], F32, o + 2432)
        sel_b = at("sel_b", [TILES, NE], BF16, o + 2528)
        squares = at("squares", [TILES, PW], F32, o + 2688)
        gain_mix = at("gain_mix", [KC], F32, o + 2688 + 2048)
        table_scratch = at("table_scratch", [8], F32, o + 2688 + 2112)
        assert base + o + 2688 + 2144 <= 229344
        scores = [scores0, scores1, scores2]

        R_CA, R_CAB = 0, CONV_A * HA
        R_BA, R_BX, R_LAM = R_CAB + HA, R_CAB + 2 * HA, R_CAB + 3 * HA
        R_CB = R_LAM + HA
        R_MIX = R_CB + CONV_B * HB
        R_Q, R_K = R_MIX + KC, R_MIX + KC + 1
        R_FFN = R_K + 1
        R_ALL = R_FFN + KC

        prm_sources = [(R_CA, conv_a_w[0].rearrange("j (h p) -> (j h) p", p=P)),
                       (R_CAB, conv_a_b[0].rearrange("(h p) -> h p", p=P)),
                       (R_BA, lru_ba[0].rearrange("(h p) -> h p", p=P)),
                       (R_BX, lru_bx[0].rearrange("(h p) -> h p", p=P)),
                       (R_LAM, lru_lam[0].rearrange("(h p) -> h p", p=P)),
                       (R_CB, conv_b_w[0].rearrange("j (h p) -> (j h) p", p=P)),
                       (R_MIX, mix_norm[0].rearrange("(h p) -> h p", p=P)),
                       (R_Q, q_norm), (R_K, k_norm), (R_FFN, norm_ffn[0].rearrange("(h p) -> h p", p=P))]
        PARS = 16 * len(prm_sources)
        ROUTER_PARS = 16 * 5

        bank = [ctx.enter_context(nc.psum_tensor(f"bank{i}", [P, 512], F32)) for i in range(8)]
        AUX = 4
        b_gate, b_up, b_fold = bank[0], bank[1], bank[2]
        b_down = [bank[3], bank[4]]
        b_gath, b_comb = [bank[4], bank[5]], [bank[6], bank[7]]

        x_in, par_in, router_in = [sem(f"x_in{t}") for t in range(TILES)], sem("par_in"), sem("router_in")
        lru_in, x_again, out_done = sem("lru_in"), sem("x_again"), sem("out_done")
        piece_in = [sem(f"piece_in{i}") for i in range(MOE_RING)]
        consts_ready = sem("consts_ready")
        hi_ready, lo_ready = sem("hi_ready"), sem("lo_ready")
        quarter_used = sem("quarter_used")
        proj_free = sem("proj_free")
        aux_full, aux_free = sem("aux_full"), sem("aux_free")
        act_step, dve_step, pool_step = sem("act_step"), sem("dve_step"), sem("pool_step")
        ssq_ready, var_ready, std_ready = sem("ssq_ready"), sem("var_ready"), sem("std_ready")
        gain_in, rstd1_ready = sem("gain_in"), sem("rstd1_ready")
        h0_ready, h1_ready, hT_full = sem("h0_ready"), sem("h1_ready"), sem("hT_full")
        hT_hi_ready, hT_ready = sem("hT_hi_ready"), sem("hT_ready")
        lam_exp = sem("lam_exp")
        qk_sq, qk_ready = sem("qk_sq"), sem("qk_ready")
        conv_ready = sem("conv_ready")
        z_masked, ln_ready = sem("z_masked"), sem("ln_ready")
        logw_ready, w_ready = sem("logw_ready"), sem("w_ready")
        y2_ready = sem("y2_ready")
        decay_ready, gated_in = sem("decay_ready"), sem("gated_in")
        expm1_ready, root_ready = sem("expm1_ready"), sem("root_ready")
        u_ready, lru_out = sem("u_ready"), sem("lru_out")
        gelu_ready = sem("gelu_ready")
        cx_ready, yb_ready = sem("cx_ready"), sem("yb_ready")
        rstd_ready = sem("rstd_ready")
        y_sq, y_norm, y_split = sem("y_sq"), sem("y_norm"), sem("y_split")
        y_hi_ready = sem("y_hi_ready")
        ssq2_ready = sem("ssq2_ready")
        x2_perm_ready = sem("x2_perm_ready")
        x2T_full, x2T_ready, x2T_used = sem("x2T_full"), sem("x2T_ready"), sem("x2T_used")
        logitsT_full, logitsT_ready = sem("logitsT_full"), sem("logitsT_ready")
        logits_full, e_ready, sub_ready = sem("logits_full"), sem("e_ready"), sem("sub_ready")
        sel_ready, rank_full = sem("sel_ready"), sem("rank_full")
        table_ready = sem("table_ready")
        piece_used = sem("piece_used")
        fold_full = sem("fold_full")
        gate_out, up_out = sem("gate_out"), sem("up_out")
        silu_ready, hid_ready = sem("silu_ready"), sem("hid_ready")
        y_out_act, y_out_dve = sem("y_out_act"), sem("y_out_dve")
        comb_full, acc_done = sem("comb_full"), sem("acc_done")
        gath_full, gath_out = sem("gath_full"), sem("gath_out")
        chosen_made, pick_ready, pick_gate_ready = sem("chosen_made"), sem("pick_ready"), sem("pick_gate_ready")
        give_full, give_ready = sem("give_full"), sem("give_ready")

        MOE_ORDER = [6, 7] + [(N_MIX + i) % MIX_RING for i in range(MIX_RING)] + [4, 5]
        MIX_USES = [len(range(i, N_MIX, MIX_RING)) for i in range(MIX_RING)] + [0] * 4
        PER_QUAD = PARTS * QI
        assert PER_QUAD % MOE_RING == 0

        def place_of(k, i):
            return MOE_ORDER[(PARTS * k + i) % MOE_RING]

        def piece_count(q, k, i):
            rounds = (PARTS * k + i) // MOE_RING + 1 + MIX_USES[place_of(k, i)]
            return q * (16 * PER_QUAD // MOE_RING) + 16 * rounds

        def piece_source(i, e):
            if i < 4:
                return (w_gate_p, w_up_p)[i % 2][e][:, (i // 2) * H:(i // 2 + 1) * H, :]
            return w_down_p[e][:, :, (i - 4) * (D // 2):(i - 3) * (D // 2)]

        def out_block(b):
            return b // 2 % 2, 2 * (b // 4) + b % 2

        U_PRM = 0
        U_QK = 1
        U_Z = U_QK + HC
        U_LRU = U_Z + HC
        U_WT = U_LRU + HA
        U_PV = U_WT + HC
        U_YC = U_PV + HC // 2
        U_YA = U_YC + HC // 2
        U_YB = U_YA + HA // 2
        U_END = U_YB + HB // 2

        def aux(u):
            return bank[AUX + u % 4]

        def proj_bank(n, b):
            return bank[2 * (n % 2) + b]

        def y_block(c):
            return BLK_GA + c if c < HA + HB else BLK_Q + c - HA - HB

        Y_RUNS = {3: [(3, 12, 16)], 0: [(5, 0, 4)], 1: [(7, 4, 8)], 2: [(3, 10, 12), (8, 8, 10)]}

        DB = D // 8

        def y_cols(k, h, n):
            return y_exp[SLOTS * k:SLOTS * (k + 1), (4 * h + n) * DB:(4 * h + n + 1) * DB]

        block = ctx.enter_context(nc.Block())

        @block.sync
        def _(sp):
            for t in range(TILES):
                sp.dma_start(x_acc[:, t, :], x_t[t]).then_inc(x_in[t], 16)
            sp.dma_start(gain_mix[:, :], norm_mix[0].rearrange("(p c) -> p c", c=KC)).then_inc(gain_in, 16)

            def parameters():
                sp.wait_ge(consts_ready, 1)
                for r, src in prm_sources:
                    sp.dma_start(prm_rows[r:r + src.shape[0], :], src).then_inc(par_in, 16)

            def router_parameters():
                sp.dma_start(w_rt[:, :, 0:NG], w_router_group[0].rearrange("(c p) g -> p c g", p=P)).then_inc(router_in, 16)
                sp.dma_start(w_rt[:, :, NG:], w_router_expert[0].rearrange("(c p) g -> p c g", p=P)).then_inc(router_in, 16)
                sp.dma_start(b_rt[:, 0:NG], b_router_group.to_broadcast([P, NG])).then_inc(router_in, 16)
                sp.dma_start(b_rt[:, NG:], b_router_expert.to_broadcast([P, NE])).then_inc(router_in, 16)
                sp.dma_start(gain_ffn[:, :], norm_ffn[0].rearrange("(p c) -> p c", c=KC)).then_inc(router_in, 16)
                sp.wait_ge(hT_full, KC // 2)
                sp.dma_start(lru_w[:, 0], lru_wa[0].rearrange("h i j -> i h j")).then_inc(lru_in, 16)
                sp.dma_start(lru_w[:, 1], lru_wx[0].rearrange("h i j -> i h j")).then_inc(lru_in, 16)

            for n in range(N_MIX):
                if n >= MIX_RING:
                    sp.wait_ge(lo_ready, 4 * (n - MIX_RING) + 4)
                dst = ring[n % MIX_RING][:, :].rearrange("p (c n) -> p c n", c=KC)
                if n < N_IN:
                    src = w_in_p[:, :, order[n] * P:order[n] * P + PW]
                else:
                    src = w_out_p[:, :, (n - N_IN) * PW:(n - N_IN + 1) * PW]
                sp.dma_start(dst, src).then_inc(piece_in[n % MIX_RING], 16)
                if n == 1:
                    parameters()
                if n == MIX_RING - 1:
                    router_parameters()
                if n == N_IN + 1:
                    sp.wait_ge(lru_out, 1)
                    for t in range(TILES):
                        sp.dma_start(x_acc[:, t, :], x_t[t]).then_inc(x_again, 16)

            def quad(q, n_extra=None):
                def item_pieces(k, e):
                    for i in range(PARTS):
                        m = PARTS * k + i
                        if isinstance(q, int) and m < 2:
                            sp.wait_ge(y_split, 4)
                        elif isinstance(q, int) and m < 6:
                            sp.wait_ge(lo_ready, 4 * (N_MIX - 6 + m) + 4)
                        elif isinstance(q, int) and m < 8:
                            sp.wait_ge(quarter_used, 4 * N_MIX)
                        else:
                            sp.wait_ge(piece_used, q * PER_QUAD + (m - MOE_RING + 1))
                        place = place_of(k, i)
                        src = piece_source(i, e)
                        sp.dma_start(ring[place][:, :].rearrange("p (c n) -> p c n", n=src.shape[2]),
                                     src).then_inc(piece_in[place], 16)

                for k in range(QI):
                    if n_extra is None:
                        item_pieces(k, q * QI + k)
                    else:
                        with sp.If(n_extra > (q - QUADS) * QI + k):
                            item_pieces(k, sp.value_load(tab[0:1, bass.ds((q - QUADS) * QI + (k + 2), 1)],
                                                         min_val=0, max_val=NE - 1))

            quad(0)
            with sp.Fori(1, QUADS) as q:
                quad(q)
            sp.wait_ge(table_ready, 1)
            n_extra = sp.value_load(tab[0:1, 0:1], min_val=0, max_val=NX - 1)
            last_quad = sp.value_load(tab[0:1, 1:2], min_val=0, max_val=QUADS + XQ - 1)
            with sp.Fori(QUADS, QUADS + XQ) as q:
                with sp.If(n_extra > (q - QUADS) * QI):
                    quad(q, n_extra)
            for b in range(8):
                t, n = out_block(b)
                sp.wait_ge(acc_done, last_quad * 8 + (b + 1))
                sp.dma_start(out_t[t][:, n * 512:(n + 1) * 512], x_acc[:, t, n * 512:(n + 1) * 512]).then_inc(out_done, 16)
            sp.wait_ge(out_done, 16 * 8)

        @block.gpsimd
        def _(pool):
            steps = [0]

            def ordered(ins):
                steps[0] += 1
                ins.then_inc(pool_step, 1)
                pool.wait_ge(pool_step, steps[0])

            pool.memset(ident[:, :], 0.0)
            pool.memset(fold[:, :], 0.0)
            pool.memset(c_eps[:, :], EPS)
            pool.memset(prm_rows[:, :], 0.0).then_inc(consts_ready, 1)
            pool.memset(ones[:, :], 1.0)
            pool.memset(ones_b[:, :], 1.0)
            pool.memset(before[:, :], 1.0)
            pool.iota(iota_s[:, :], [[1, SLOTS]], base=1, channel_multiplier=0,
                      allow_small_or_imprecise_dtypes=True)
            pool.iota(iota_e[:, 0:NE], [[1, NE]], base=0, channel_multiplier=0,
                      allow_small_or_imprecise_dtypes=True)
            pool.iota(iota_e[:, NE:NE + NX + QI], [[1, NX + QI]], base=0, channel_multiplier=0,
                      allow_small_or_imprecise_dtypes=True)
            ordered(pool.iota(desc[:, :], [[-1, 12]], base=12, channel_multiplier=0,
                              allow_small_or_imprecise_dtypes=True))
            pool.affine_select(out=ident[:, :], in_=ident[:, :], compare_op=ALU.not_equal, fill=1.0,
                               base=0, pattern=[[-1, P]], channel_multiplier=1)
            for j in range(P // SLOTS):
                pool.affine_select(out=fold[:, :], in_=fold[:, :], compare_op=ALU.not_equal, fill=1.0,
                                   base=-SLOTS * j, pattern=[[-1, SLOTS]], channel_multiplier=1)
                if j + 1 < P // SLOTS:
                    ordered(pool.iota(small[:, 0:1], [[0, 1]], base=0, channel_multiplier=0,
                                      allow_small_or_imprecise_dtypes=True))
            pool.affine_select(out=before[:, :], in_=before[:, :], compare_op=ALU.is_gt, fill=0.0,
                               base=0, pattern=[[1, P]], channel_multiplier=-1).then_inc(consts_ready, 1)
            def square_blocks(dst, src, ready):
                pool.tensor_tensor(dst, src, src, ALU.mult).then_inc(ready, 1)

            for j in range(HC):
                pool.wait_ge(proj_free, j + 1)
                b = BLK_Q + 2 * j
                square_blocks(temp[:, 2 * j:2 * j + 2, :], proj[:, b:b + 2, :], qk_sq)
            for b in range(HC // 2):
                z = scores[b][:, 0]
                pool.wait_ge(aux_free, U_Z + 2 * b + 2)
                for part in (z[:, :, 0:P], z[:, :, 2 * P:3 * P]):
                    ins = pool.affine_select(out=part, in_=part, compare_op=ALU.is_gt, fill=MASKED,
                                             base=0, pattern=[[0, 2], [-1, P]], channel_multiplier=1)
                ins.then_inc(z_masked, 1)
            pool.wait_ge(aux_free, U_LRU + HA)
            pool.tensor_tensor(lru_u[:, :, :], lru_u[:, :, :], conv_a[:, :, :], ALU.mult).then_inc(gated_in, 1)
            pool.wait_ge(root_ready, 1)
            pool.tensor_tensor(lru_u[:, :, :], lru_u[:, :, :], conv_a[:, :, :], ALU.mult).then_inc(u_ready, 1)
            pool.wait_ge(aux_free, U_PV + HC // 2)
            for j in range(HC // 2):
                b = BLK_Q + 2 * j
                square_blocks(proj[:, BLK_K + 2 * j:BLK_K + 2 * j + 2, :], proj[:, b:b + 2, :], y_sq)
            pool.wait_ge(lru_out, 1)
            pool.wait_ge(gelu_ready, 1)
            ordered(pool.tensor_tensor(proj[:, BLK_GA:BLK_GA + HA, :], proj[:, BLK_GA:BLK_GA + HA, :],
                                       proj[:, BLK_XA:BLK_XA + HA, :], ALU.mult))
            for j in range(HA // 2):
                b = BLK_GA + 2 * j
                square_blocks(proj[:, BLK_XA + 2 * j:BLK_XA + 2 * j + 2, :], proj[:, b:b + 2, :], y_sq)
            pool.wait_ge(proj_free, S_BG)
            pool.tensor_tensor(proj[:, BLK_XB:BLK_XB + HB, :], proj[:, BLK_XB:BLK_XB + HB, :],
                               proj[:, BLK_CG:BLK_CG + HB, :], ALU.mult).then_inc(cx_ready, 1)
            for j in range(HB // 2):
                pool.wait_ge(yb_ready, j + 1)
                b = BLK_BG + 2 * j
                square_blocks(proj[:, BLK_CG + 2 * j:BLK_CG + 2 * j + 2, :], proj[:, b:b + 2, :], y_sq)
            for k in range(N_OUT):
                pool.wait_ge(proj_free, N_IN + k + 1)
                rows = slice(k * PW // KC, (k + 1) * PW // KC)
                for t in range(TILES):
                    ins = pool.tensor_copy(x2_perm[:, t, :, rows].rearrange("p c k -> p k c"),
                                           x_acc[:, t, k * PW:(k + 1) * PW].rearrange("p (k c) -> p k c", c=KC))
                ins.then_inc(x2_perm_ready, 1)

        @block.scalar
        def _(act):
            steps = [0]

            def ordered(ins):
                steps[0] += 1
                ins.then_inc(act_step, 1)
                act.wait_ge(act_step, steps[0])


            scratch_used = [0]

            def load_table(function):
                scratch_used[0] += 1
                act.activation(table_scratch[:, scratch_used[0] - 1:scratch_used[0]], c_eps[:, 0:1], function)

            act.wait_ge(consts_ready, 1)
            load_table(ACT.Sqrt)
            for t in range(TILES):
                act.wait_ge(x_in[t], 16)
                ins = act.activation(squares_x[:, t, 0:D // 2], x_acc[:, t, 0:D // 2], ACT.Square,
                                     accum_out=ssq[:, t, 4:5])
            ins.then_inc(ssq_ready, 1)
            act.wait_ge(var_ready, 1)
            act.activation(ssq[:, :, 2:3], ssq[:, :, 1:2], ACT.Sqrt).then_inc(std_ready, 1)
            act.wait_ge(rstd1_ready, 1)
            act.activation(h_perm[:, 0].rearrange("p c k -> p k c"), x_acc[:, 0, :].rearrange("p (k c) -> p k c", c=KC),
                           ACT.Copy, scale=ssq[:, 0, 2:3]).then_inc(h0_ready, 1)

            def hT_high(quarter):
                if quarter == 0:
                    act.wait_ge(gain_in, 16)
                for j in (2 * quarter, 2 * quarter + 1):
                    act.wait_ge(hT_full, j + 1)
                    for c in range(2):
                        ins = act.activation(hT_hi[:, 2 * j + c, :], bank[j][:, c * SEQ:(c + 1) * SEQ], ACT.Copy,
                                             scale=gain_mix[:, 2 * j + c:2 * j + c + 1])
                    ins.then_inc(hT_hi_ready, 1)

            def parameters():
                act.wait_ge(aux_full, U_PRM + 1)
                act.activation(prm[:, 0:R_ALL], aux(U_PRM)[:, 0:R_ALL], ACT.Copy).then_inc(aux_free, 1)
                act.wait_ge(aux_free, U_PRM + 1)
                ordered(act.activation(lru_t[:, 0, :], prm[:, R_LAM:R_LAM + HA], ACT.Abs))
                act.activation(lru_t[:, 1, :], lru_t[:, 0, :], ACT.Exp, scale=-1.0).then_inc(lam_exp, 1)

            def split_high(n, quarters=range(4)):
                if 0 in quarters:
                    act.wait_ge(piece_in[n % MIX_RING], 16 * (n // MIX_RING + 1))
                for k in quarters:
                    g = 4 * n + k
                    if g >= 4:
                        act.wait_ge(quarter_used, g - 3)
                    kk = k if n < N_IN else Y_ORDER[k]
                    src = ring[n % MIX_RING][:, kk * 4 * PW:(kk + 1) * 4 * PW]
                    act.activation(w_hi[:, k].rearrange("p c n -> p (c n)"), src, ACT.Copy).then_inc(hi_ready, 1)

            def empty_projection(n):
                act.wait_ge(quarter_used, 4 * n + 4)
                for b in range(2):
                    src = proj_bank(n, b)[:, 0:PW]
                    if order[n] < BLK_V:
                        dst = proj[:, order[n] + b, :]
                    else:
                        c0 = (order[n] - BLK_V) * P
                        dst = v_tok[:, b, c0:c0 + PW]
                    ins = act.activation(dst, src, ACT.Copy)
                ins.then_inc(proj_free, 1)

            def stick_scores(b):
                z = scores[b][:, 0]
                act.wait_ge(aux_full, U_Z + 2 * b + 1)
                act.activation(z[:, :, P:3 * P], aux(U_Z + 2 * b)[:, :].rearrange("p (h k) -> p h k", h=2),
                               ACT.Copy, scale=float(P) ** -0.5).then_inc(aux_free, 1)
                act.wait_ge(aux_full, U_Z + 2 * b + 2)
                act.activation(z[:, :, 0:P], aux(U_Z + 2 * b + 1)[:, 0:2 * P].rearrange("p (h k) -> p h k", h=2),
                               ACT.Copy, scale=float(P) ** -0.5).then_inc(aux_free, 1)

            def stick_exp(pairs):
                for b in pairs:
                    act.wait_ge(z_masked, b + 1)
                    ins = act.activation(scores[b][:, 1], scores[b][:, 0], ACT.Abs)
                ordered(ins)
                for b in pairs:
                    ins = act.activation(scores[b][:, 1], scores[b][:, 1], ACT.Exp, scale=-1.0)
                ordered(ins)

            def stick_log():
                for b in range(HC // 2):
                    act.activation(scores[b][:, 1], scores[b][:, 1], ACT.Ln, bias=1.0).then_inc(ln_ready, 1)

            def stick_weights(b):
                act.wait_ge(logw_ready, b + 1)
                act.activation(scores[b][:, 0], scores[b][:, 1], ACT.Exp).then_inc(w_ready, 1)

            def weights_transposed(h):
                act.wait_ge(aux_full, U_WT + h + 1)
                act.activation(scores[h // 2][:, 1, h % 2, :], aux(U_WT + h)[:, 0:3 * P], ACT.Copy).then_inc(aux_free, 1)

            def attention_out(b):
                act.wait_ge(aux_full, U_PV + b + 1)
                act.activation(proj[:, BLK_Q + 2 * b:BLK_Q + 2 * b + 2, :],
                               aux(U_PV + b)[:, :].rearrange("p (h k) -> p h k", h=2), ACT.Copy).then_inc(aux_free, 1)

            def lru_gates(heads):
                for h in heads:
                    u = U_LRU + h
                    act.wait_ge(aux_full, u + 1)
                    act.activation(proj[:, BLK_XA + h, :], aux(u)[:, 0:SEQ], ACT.Sigmoid,
                                   bias=prm[:, R_BA + h:R_BA + h + 1])
                    act.activation(lru_u[:, h, :], aux(u)[:, SEQ:2 * SEQ], ACT.Sigmoid,
                                   bias=prm[:, R_BX + h:R_BX + h + 1]).then_inc(aux_free, 1)

            def norm_log(uses, dst):
                for j, u in enumerate(uses):
                    act.wait_ge(aux_full, u + 1)
                    act.activation(dst[:, 2 * j:2 * j + 2, :], aux(u)[:, :].rearrange("p (h k) -> p h k", h=2),
                                   ACT.Ln, scale=1.0 / P, bias=c_eps[:, 0:1]).then_inc(aux_free, 1)

            def norm_exp(uses, dst):
                act.wait_ge(aux_free, uses[-1] + 1)
                for j in range(len(uses)):
                    d = dst[:, 2 * j:2 * j + 2, :]
                    act.activation(d, d, ACT.Exp, scale=-0.5).then_inc(rstd_ready, 1)

            def y_split_high(k):
                act.wait_ge(quarter_used, 4 * (N_IN - 1) + k + 1)
                for need, a, b in Y_RUNS[Y_ORDER[k]]:
                    act.wait_ge(y_norm, need)
                    moved = 4 * (k - Y_ORDER[k])
                    ins = act.activation(y_hi[:, a + moved:b + moved, :], proj[:, y_block(a):y_block(a) + b - a, :], ACT.Copy)
                ins.then_inc(y_hi_ready, 1)

            def after_residual(k):
                act.wait_ge(proj_free, N_IN + k + 1)
                if k > 0:
                    act.wait_ge(ssq2_ready, k)
                for t in range(TILES):
                    ins = act.activation(squares[:, t, :], x_acc[:, t, k * PW:(k + 1) * PW], ACT.Square,
                                         accum_out=ssq[:, t, 4 + k:5 + k])
                ins.then_inc(ssq2_ready, 1)

            def transposed_x2(k):
                act.wait_ge(x2T_full, k + 1)
                if k >= 2:
                    act.wait_ge(x2T_used, k - 1)
                for c in range(2):
                    ins = act.activation(x2T[:, k % 2, c, :], bank[AUX + k % 2][:, c * SEQ:(c + 1) * SEQ], ACT.Copy,
                                         scale=prm[:, R_FFN + 2 * k + c:R_FFN + 2 * k + c + 1])
                ins.then_inc(x2T_ready, 1)

            rstd_a, rstd_b = proj[:, BLK_XA:BLK_XA + HA, :], proj[:, BLK_CG:BLK_CG + HB, :]
            rstd_c = proj[:, BLK_K:BLK_K + HC, :]

            for n in range(N_MIX):
                if n == N_IN:
                    split_high(n, range(1, 3))
                    y_split_high(1)
                    empty_projection(n - 1)
                    split_high(n, range(3, 4))
                elif n == 0:
                    for k in range(4):
                        split_high(0, range(k, k + 1))
                        hT_high(k)
                else:
                    split_high(n)
                    if n == S_CG + 1:
                        act.wait_ge(lru_out, 1)
                    if n < N_IN:
                        empty_projection(n - 1)
                if n == 1:
                    parameters()
                    load_table(ACT.Ln)
                if n == 6:
                    norm_log(range(U_QK, U_QK + 4), temp)
                if n == 8:
                    norm_log(range(U_QK + 4, U_Z), temp[:, 8:12])
                    norm_exp(range(U_QK, U_Z), temp)
                if n == 11:
                    stick_scores(0)
                    stick_scores(1)
                    stick_exp(range(0, 2))
                if n == 12:
                    stick_scores(2)
                    stick_exp(range(2, 3))
                    stick_log()
                if n == 13:
                    lru_gates(range(0, 4))
                if n == 14:
                    lru_gates(range(4, HA))
                    stick_weights(0)
                    stick_weights(1)
                if n == 15:
                    stick_weights(2)
                    act.wait_ge(y2_ready, 1)
                    y = proj[:, BLK_XA:BLK_XA + HA, :]
                    ordered(act.activation(lru_a[:, :, :], y, ACT.Exp, scale=-0.5))
                    act.activation(y, y, ACT.Tanh, scale=0.5).then_inc(decay_ready, 1)
                if n == 16:
                    for h in range(HC):
                        weights_transposed(h)
                    act.wait_ge(expm1_ready, 1)
                    act.activation(conv_a[:, :, :], conv_a[:, :, :], ACT.Sqrt).then_inc(root_ready, 1)
                if n == 17:
                    for b in range(HC // 2):
                        attention_out(b)
                    act.wait_ge(proj_free, S_XB)
                    act.activation(proj[:, BLK_GA:BLK_GA + HA, :], proj[:, BLK_GA:BLK_GA + HA, :],
                                   ACT.Gelu_apprx_tanh).then_inc(gelu_ready, 1)
                if n == 19:
                    norm_log(range(U_YC, U_YA), rstd_c)
                    norm_exp(range(U_YC, U_YA), rstd_c)
                if n == 20:
                    norm_log(range(U_YA, U_YB), rstd_a)
                    split_high(N_IN, range(0, 1))
                    norm_log(range(U_YB, U_YB + 1), rstd_b)
                    y_split_high(0)
                    norm_exp(range(U_YA, U_YB), rstd_a)
                    norm_exp(range(U_YB, U_YB + 1), rstd_b)
                if n == N_IN:
                    load_table(ACT.Ln)
                    y_split_high(2)
                    norm_log(range(U_YB + 1, U_END), rstd_b[:, 2:])
                    norm_exp(range(U_YB + 1, U_END), rstd_b[:, 2:])
                    y_split_high(3)
                    load_table(ACT.Sqrt)
                if n > N_IN:
                    after_residual(n - N_IN - 1)
                if n > N_IN + 1:
                    transposed_x2(n - N_IN - 2)
            transposed_x2(N_OUT - 2)
            after_residual(N_OUT - 1)
            transposed_x2(N_OUT - 1)
            act.wait_ge(var_ready, 2)
            act.activation(ssq[:, :, 2:3], ssq[:, :, 1:2], ACT.Sqrt).then_inc(std_ready, 1)
            load_table(ACT.Exp)
            act.wait_ge(sub_ready, 1)
            act.activation(small[:, 0:TILES * NG], small[:, 0:TILES * NG], ACT.Exp).then_inc(e_ready, 1)
            act.wait_ge(sub_ready, 2)
            act.activation(small[:, TILES * NG:2 * TILES * NG], small[:, TILES * NG:2 * TILES * NG], ACT.Exp).then_inc(e_ready, 1)
            load_table(ACT.Silu)

            def item_step(q, k):
                i = q * QI + k
                act.wait_ge(piece_used, i * PARTS + 3)
                if not (isinstance(q, int) and i == 0):
                    act.wait_ge(fold_full, i)
                act.activation(gate_sb[:, :], b_gate[:, :], ACT.Copy).then_inc(gate_out, 1)
                act.wait_ge(fold_full, i + 1)
                if not (isinstance(q, int) and i == 0):
                    act.wait_ge(hid_ready, i)
                act.activation(silu_sb[:, :, :], b_fold[:, 0:P].rearrange("p (f s) -> p f s", f=FC),
                               ACT.Silu).then_inc(silu_ready, 1)
                for h in range(2):
                    act.wait_ge(piece_used, i * PARTS + (5 + h))
                    for n in range(2):
                        ins = act.activation(y_cols(k, h, n), b_down[h][SLOTS * n:SLOTS * (n + 1), 0:DB], ACT.Copy)
                    ins.then_inc(y_out_act, 1)

            def quad(q, n_extra=None):
                act.wait_ge(give_full, q + 1)
                act.activation(give[:, :, :], b_fold[:, 2 * P:4 * P].rearrange("p (t s) -> p t s", t=TILES),
                               ACT.Copy).then_inc(give_ready, 1)
                for k in range(QI):
                    if n_extra is None:
                        item_step(q, k)
                    else:
                        with act.If(n_extra > (q - QUADS) * QI + k):
                            item_step(q, k)

            quad(0)
            with act.Fori(1, QUADS) as q:
                quad(q)
            act.wait_ge(table_ready, 1)
            n_extra = act.value_load(tab[0:1, 0:1], min_val=0, max_val=NX - 1)
            with act.Fori(QUADS, QUADS + XQ) as q:
                with act.If(n_extra > (q - QUADS) * QI):
                    quad(q, n_extra)

        @block.vector
        def _(dve):
            steps = [0]

            def ordered(ins):
                steps[0] += 1
                ins.then_inc(dve_step, 1)
                dve.wait_ge(dve_step, steps[0])

            def token_rstd(round_):
                dve.wait_ge(std_ready, round_)
                r, v, w = ssq[:, :, 2:3], ssq[:, :, 1:2], ssq[:, :, 3:4]
                ordered(dve.reciprocal(r, r))
                ordered(dve.tensor_tensor(w, r, r, ALU.mult))
                ordered(dve.tensor_tensor(w, w, v, ALU.mult))
                ordered(dve.tensor_scalar(w, w, -0.5, 1.5, ALU.mult, ALU.add))
                ins = dve.tensor_tensor(r, r, w, ALU.mult)
                if round_ == 1:
                    ins.then_inc(rstd1_ready, 1)
                    dve.wait_ge(rstd1_ready, 1)
                else:
                    ordered(ins)

            for t in range(TILES):
                dve.wait_ge(x_in[t], 16)
                ins = dve.scalar_tensor_tensor(squares_x[:, t, D // 2:], x_acc[:, t, D // 2:], 1.0, x_acc[:, t, D // 2:],
                                               ALU.mult, ALU.mult, accum_out=ssq[:, t, 5:6])
            ins.then_inc(ssq_ready, 1)
            dve.wait_ge(ssq_ready, 2)
            ordered(dve.tensor_reduce(ssq[:, :, 0:1], ssq[:, :, 4:6], AX, ALU.add))
            dve.tensor_scalar(ssq[:, :, 1:2], ssq[:, :, 0:1], 1.0 / D, EPS, ALU.mult, ALU.add).then_inc(var_ready, 1)
            dve.wait_ge(var_ready, 1)
            token_rstd(1)
            dve.tensor_scalar(h_perm[:, 1].rearrange("p c k -> p k c"),
                              x_acc[:, 1, :].rearrange("p (k c) -> p k c", c=KC), ssq[:, 1, 2:3], None,
                              ALU.mult).then_inc(h1_ready, 1)

            def hT_low(quarter):
                if quarter == 0:
                    dve.wait_ge(gain_in, 16)
                for j in (2 * quarter, 2 * quarter + 1):
                    dve.wait_ge(hT_hi_ready, j + 1)
                    for c in range(2):
                        ins = dve.scalar_tensor_tensor(hT_lo[:, 2 * j + c, :], bank[j][:, c * SEQ:(c + 1) * SEQ],
                                                       gain_mix[:, 2 * j + c:2 * j + c + 1],
                                                       hT_hi[:, 2 * j + c, :].bitcast(F32), ALU.mult, ALU.subtract)
                    ins.then_inc(hT_ready, 1)

            def softplus_lam():
                dve.wait_ge(lam_exp, 1)
                e_, s_, s2 = lru_t[:, 1, :], lru_t[:, 0, :], lru_t[:, 2, :]
                ordered(dve.tensor_scalar(s_, e_, 2.0, None, ALU.add))
                ordered(dve.reciprocal(s_, s_))
                ordered(dve.tensor_tensor(s_, s_, e_, ALU.mult))
                ordered(dve.tensor_tensor(s2, s_, s_, ALU.mult))
                ordered(dve.tensor_scalar(lru_c[:, :], s2, 1.0 / 19, None, ALU.mult))
                for k in range(8, 0, -1):
                    ordered(dve.scalar_tensor_tensor(lru_c[:, :], lru_c[:, :], 1.0 / (2 * k + 1), s2, ALU.add, ALU.mult))
                ordered(dve.scalar_tensor_tensor(lru_c[:, :], lru_c[:, :], 1.0, s_, ALU.add, ALU.mult))
                ordered(dve.tensor_scalar(s2, prm[:, R_LAM:R_LAM + HA], -1.0, 0.0, ALU.mult, ALU.max))
                ordered(dve.scalar_tensor_tensor(lru_c[:, :], lru_c[:, :], 2.0, s2, ALU.mult, ALU.add))
                ordered(dve.tensor_scalar(lru_c[:, :], lru_c[:, :], 2 * LRU_C, None, ALU.mult))

            def split_low(n, quarters=range(4)):
                for k in quarters:
                    g = 4 * n + k
                    dve.wait_ge(hi_ready, g + 1)
                    if g >= 4:
                        dve.wait_ge(quarter_used, g - 3)
                    kk = k if n < N_IN else Y_ORDER[k]
                    src = ring[n % MIX_RING][:, kk * 4 * PW:(kk + 1) * 4 * PW]
                    dve.tensor_tensor(w_lo[:, k].rearrange("p c n -> p (c n)"), src,
                                      w_hi[:, k].rearrange("p c n -> p (c n)").bitcast(F32),
                                      ALU.subtract).then_inc(lo_ready, 1)

            def normalise_qk(pairs):
                for j in pairs:
                    dve.wait_ge(rstd_ready, j + 1)
                    for b in range(2):
                        blk = BLK_Q + 2 * j + b
                        gain = R_Q if blk < BLK_K else R_K
                        ins = dve.scalar_tensor_tensor(proj[:, blk, :], proj[:, blk, :], prm[:, gain:gain + 1],
                                                       temp[:, 2 * j + b, :], ALU.mult, ALU.mult)
                    ins.then_inc(qk_ready, 1)

            def causal_conv(dst, src, taps, tap_col, bias_col, heads, dst0, src0):
                for h in heads:
                    d, s = dst[:, dst0 + h, :], src[:, src0 + h, :]
                    last = tap_col(taps - 1, h)
                    if bias_col is None:
                        ins = dve.tensor_scalar(d, s, prm[:, last:last + 1], None, ALU.mult)
                    else:
                        ins = dve.tensor_scalar(d, s, prm[:, last:last + 1],
                                                prm[:, bias_col + h:bias_col + h + 1], ALU.mult, ALU.add)
                for back in range(1, taps):
                    ordered(ins)
                    for h in heads:
                        d, s = dst[:, dst0 + h, :], src[:, src0 + h, :]
                        w = tap_col(taps - 1 - back, h)
                        ins = dve.scalar_tensor_tensor(d[:, back:], s[:, 0:SEQ - back], prm[:, w:w + 1],
                                                       d[:, back:], ALU.mult, ALU.add)
                return ins

            def conv_a_heads(j):
                dve.wait_ge(proj_free, S_XA + j + 1)
                causal_conv(conv_a, proj, CONV_A, lambda j, h: R_CA + j * HA + h, R_CAB, range(2 * j, 2 * j + 2), 0,
                            BLK_XA).then_inc(conv_ready, 1)

            def stick(b):
                z, t = scores[b][:, 0], scores[b][:, 1]
                dve.wait_ge(ln_ready, b + 1)
                ordered(dve.scalar_tensor_tensor(t, z, 0.0, t, ALU.max, ALU.add))
                for h in range(2):
                    for a, e in ((0, P), (P, 3 * P)):
                        back = t[:, h, a:e][:, ::-1]
                        ins = dve.tensor_tensor_scan(back, back, back, 0.0, ALU.add, ALU.max)
                ordered(ins)
                dve.tensor_tensor(t, z, t, ALU.subtract).then_inc(logw_ready, 1)

            def normalise_y(pairs, done, rstd, first, chunk0):
                for j in range(pairs):
                    dve.wait_ge(rstd_ready, HC + done + j + 1)
                    for b in range(2):
                        blk, c = first + 2 * j + b, chunk0 + 2 * j + b
                        ins = dve.scalar_tensor_tensor(proj[:, blk, :], proj[:, blk, :],
                                                       prm[:, R_MIX + c:R_MIX + c + 1],
                                                       proj[:, rstd + 2 * j + b, :], ALU.mult, ALU.mult)
                    ins.then_inc(y_norm, 1)

            def y_split_low(k):
                dve.wait_ge(y_hi_ready, k + 1)
                for _, a, b in Y_RUNS[Y_ORDER[k]]:
                    place = slice(a + 4 * (k - Y_ORDER[k]), b + 4 * (k - Y_ORDER[k]))
                    ins = dve.tensor_tensor(y_lo[:, place, :], proj[:, y_block(a):y_block(a) + b - a, :],
                                            y_hi[:, place, :].bitcast(F32), ALU.subtract)
                ins.then_inc(y_split, 1)

            def gated_conv(j):
                dve.wait_ge(proj_free, S_BG + 1 + j)
                b = 2 * j
                dve.tensor_tensor(proj[:, BLK_BG + b:BLK_BG + b + 2, :], proj[:, BLK_BG + b:BLK_BG + b + 2, :],
                                  proj[:, BLK_CG + b:BLK_CG + b + 2, :], ALU.mult).then_inc(yb_ready, 1)

            def residual(k):
                dve.wait_ge(quarter_used, 4 * (N_IN + k) + 4)
                if k == 0:
                    dve.wait_ge(x_again, 16 * TILES)
                for t in range(TILES):
                    dst = x_acc[:, t, k * PW:(k + 1) * PW]
                    ins = dve.tensor_tensor(dst, dst, proj_bank(N_IN + k, t)[:, 0:PW], ALU.add)
                ins.then_inc(proj_free, 1)

            y_, w_ = proj[:, BLK_XA:BLK_XA + HA, :], conv_a[:, :, :]

            for n in range(N_MIX):
                if n == N_IN:
                    split_low(n, range(1, 3))
                    y_split_low(1)
                    gated_conv(1)
                    split_low(n, range(3, 4))
                elif n == 0:
                    for k in range(4):
                        split_low(0, range(k, k + 1))
                        hT_low(k)
                else:
                    split_low(n)
                if n == 2:
                    softplus_lam()
                if n == 8:
                    conv_a_heads(0)
                if n == 9:
                    conv_a_heads(1)
                    normalise_qk(range(0, HC // 2))
                if n == 10:
                    normalise_qk(range(HC // 2, HC))
                    conv_a_heads(2)
                if n == 13:
                    stick(0)
                    stick(1)
                if n == 14:
                    stick(2)
                    dve.wait_ge(aux_free, U_LRU + HA)
                    for h in range(HA):
                        ins = dve.tensor_scalar(proj[:, BLK_XA + h, :], proj[:, BLK_XA + h, :],
                                                lru_c[:, h:h + 1], None, ALU.mult)
                    ins.then_inc(y2_ready, 1)
                if n == 15:
                    dve.wait_ge(decay_ready, 1)
                    dve.wait_ge(gated_in, 1)
                    ordered(dve.tensor_tensor(w_, lru_a[:, :, :], lru_a[:, :, :], ALU.mult))
                    dve.scalar_tensor_tensor(w_, w_, 1.0, y_, ALU.add, ALU.mult).then_inc(expm1_ready, 1)
                if n == 17:
                    dve.wait_ge(u_ready, 1)
                    for h in range(HA):
                        ins = dve.tensor_tensor_scan(proj[:, BLK_XA + h, :], lru_a[:, h, :], lru_u[:, h, :], 0.0,
                                                     ALU.mult, ALU.add)
                    ins.then_inc(lru_out, 1)
                if n == 19:
                    dve.wait_ge(cx_ready, 1)
                    ordered(causal_conv(proj, proj, CONV_B, lambda j, h: R_CB + j * HB + h, None, range(HB), BLK_CG,
                                        BLK_XB))
                if n == 20:
                    gated_conv(0)
                    normalise_y(HC // 2, 0, BLK_K, BLK_Q, HA + HB)
                    split_low(N_IN, range(0, 1))
                    y_split_low(0)
                    normalise_y(HA // 2, HC // 2, BLK_XA, BLK_GA, 0)
                if n == N_IN:
                    normalise_y(1, (HC + HA) // 2, BLK_CG, BLK_BG, HA)
                    y_split_low(2)
                    normalise_y(1, (HC + HA) // 2 + 1, BLK_CG + 2, BLK_BG + 2, HA + 2)
                    y_split_low(3)
                if n > N_IN:
                    residual(n - N_IN - 1)
            residual(N_OUT - 1)

            dve.wait_ge(ssq2_ready, N_OUT)
            ordered(dve.tensor_reduce(ssq[:, :, 0:1], ssq[:, :, 4:4 + N_OUT], AX, ALU.add))
            dve.tensor_scalar(ssq[:, :, 1:2], ssq[:, :, 0:1], 1.0 / D, EPS, ALU.mult, ALU.add).then_inc(var_ready, 1)
            dve.wait_ge(var_ready, 2)
            token_rstd(2)
            dve.wait_ge(logitsT_full, 1)
            dve.tensor_copy(logitsT[0:NG + NE, :], bank[AUX + 2][0:NG + NE, 0:SEQ]).then_inc(logitsT_ready, 1)

            TT = TILES
            small_at = [TT * (NG + NG)]

            def take(*shape):
                n = int(np.prod(shape))
                v = small[:, small_at[0]:small_at[0] + n]
                small_at[0] += n
                assert small_at[0] <= small.shape[1]
                if len(shape) == 2:
                    return v.rearrange("p (a b) -> p a b", a=shape[0])
                if len(shape) == 3:
                    return v.rearrange("p (a b c) -> p a b c", a=shape[0], b=shape[1])
                return v

            g_exp = small[:, 0:TT * NG].rearrange("p (t g) -> p t g", t=TT)
            e_exp = small[:, TT * NG:2 * TT * NG].rearrange("p (t g) -> p t g", t=TT)
            lg = take(TT, NG + NE)
            g_one, t4 = take(TT, NG), take(TT, NG)
            g_max, g_mark, pg = take(TT, 1), take(TT, 1), take(TT, 1)
            m1, m2, mark = take(TT, NG), take(TT, NG), take(TT, NG)
            weight1, weight2 = take(TT, NG), take(TT, NG)
            one1, one2, t8 = take(TT, NG, EG), take(TT, NG, EG), take(TT, NG, EG)
            rest, sel = take(TT, NG, EG), take(TT, NG, EG)
            cnt, excl, incl = take(NE), take(NE), take(NE)
            ntab = take(2 + NX + QI)
            lg_g, lg_e = lg[:, :, 0:NG], lg[:, :, NG:].rearrange("p t (g j) -> p t g j", g=NG)

            def over_g(a):
                return a.to_broadcast([P, TT, NG])

            def over_e(a):
                return a.unsqueeze(3).to_broadcast([P, TT, NG, EG])

            desc_g = desc[:, 0:NG].unsqueeze(1).to_broadcast([P, TT, NG])
            desc_e = desc[:, 0:EG].unsqueeze(1).unsqueeze(1).to_broadcast([P, TT, NG, EG])

            dve.wait_ge(logits_full, 1)
            dve.wait_ge(router_in, ROUTER_PARS)
            for t in range(TILES):
                ins = dve.scalar_tensor_tensor(lg[:, t], bank[AUX + 3][:, t * (NG + NE):(t + 1) * (NG + NE)],
                                               ssq[:, t, 2:3], b_rt[:, :], ALU.mult, ALU.add)
            ordered(ins)
            dve.tensor_reduce(g_max, lg_g, AX, ALU.max)
            ordered(dve.tensor_reduce(m1, lg_e, AX, ALU.max))
            dve.tensor_tensor(g_exp, lg_g, over_g(g_max), ALU.subtract).then_inc(sub_ready, 1)
            dve.tensor_tensor(t4, lg_g, over_g(g_max), ALU.is_equal)
            ordered(dve.tensor_tensor(t8, lg_e, over_e(m1), ALU.is_equal))
            dve.tensor_tensor(t4, t4, desc_g, ALU.mult)
            ordered(dve.tensor_tensor(t8, t8, desc_e, ALU.mult))
            dve.tensor_reduce(g_mark, t4, AX, ALU.max)
            ordered(dve.tensor_reduce(mark, t8, AX, ALU.max))
            dve.tensor_tensor(g_one, t4, over_g(g_mark), ALU.is_equal)
            ordered(dve.tensor_tensor(one1, t8, over_e(mark), ALU.is_equal))
            ordered(dve.scalar_tensor_tensor(rest, one1, MASKED, lg_e, ALU.mult, ALU.add))
            ordered(dve.tensor_reduce(m2, rest, AX, ALU.max))
            dve.tensor_tensor(e_exp, m2, m1, ALU.subtract).then_inc(sub_ready, 1)
            ordered(dve.tensor_tensor(t8, rest, over_e(m2), ALU.is_equal))
            ordered(dve.tensor_tensor(t8, t8, desc_e, ALU.mult))
            ordered(dve.tensor_reduce(mark, t8, AX, ALU.max))
            ordered(dve.tensor_tensor(one2, t8, over_e(mark), ALU.is_equal))
            ordered(dve.tensor_tensor(t8, one1, one2, ALU.add))
            dve.tensor_tensor(sel_b[:, :, :].rearrange("p t (g j) -> p t g j", g=NG), t8, over_e(g_one),
                              ALU.mult).then_inc(sel_ready, 1)
            dve.tensor_tensor(sel, t8, over_e(g_one), ALU.mult)
            dve.wait_ge(e_ready, 2)
            dve.tensor_reduce(pg, g_exp, AX, ALU.add)
            ordered(dve.tensor_scalar(weight1, e_exp, 1.0, None, ALU.add))
            dve.reciprocal(pg, pg)
            ordered(dve.reciprocal(weight1, weight1))
            ranks = rank_item[:, :, 0:NE]
            dve.wait_ge(rank_full, 1)
            dve.tensor_copy(cnt, bank[5][:, TT * NE:(TT + 1) * NE])
            ordered(dve.scalar_tensor_tensor(ranks, bank[5][:, 0:TT * NE].rearrange("p (t e) -> p t e", t=TT), 1.0,
                                             sel.rearrange("p t g j -> p t (g j)"), ALU.add, ALU.mult))

            def choose(q, mark):
                r = rank_item[:, :, bass.ds(q * QI, QI)]
                for t in range(TILES):
                    ins = dve.tensor_tensor(chosen[:, t], r[:, t].unsqueeze(2).to_broadcast([P, QI, SLOTS]),
                                            iota_s[:, :].unsqueeze(1).to_broadcast([P, QI, SLOTS]), ALU.is_equal)
                ins.then_inc(chosen_made, 1)
                dve.wait_ge(chosen_made, mark)
                for t in range(TILES):
                    ins = dve.tensor_scalar(pick[:, t], chosen[:, t], ssq[:, t, 2:3], None, ALU.mult)
                ins.then_inc(pick_ready, 1)

            def choose_gates(q):
                g = gate_item[:, :, bass.ds(q * QI, QI)]
                for t in range(TILES):
                    ins = dve.tensor_tensor(pick_gate[:, t], chosen[:, t],
                                            g[:, t].unsqueeze(2).to_broadcast([P, QI, SLOTS]), ALU.mult)
                ins.then_inc(pick_gate_ready, 1)

            choose(0, 1)
            ordered(dve.tensor_tensor(weight1, weight1, over_g(pg), ALU.mult))
            dve.tensor_tensor(weight2, weight1, e_exp, ALU.mult)
            ordered(dve.tensor_tensor(one1, one1, over_e(weight1), ALU.mult))
            ordered(dve.tensor_tensor(one2, one2, over_e(weight2), ALU.mult))
            ordered(dve.tensor_tensor(one1, one1, one2, ALU.add))
            ordered(dve.tensor_tensor(gate_item[:, :, 0:NE].rearrange("p t (g j) -> p t g j", g=NG), over_e(g_one),
                                      one1, ALU.mult))
            choose_gates(0)

            M = NX + QI
            it = iota_e[:, NE:NE + M]
            by_item = it.unsqueeze(2).to_broadcast([P, M, NE])

            def by_expert(a):
                return a.unsqueeze(1).to_broadcast([P, M, NE])

            mt, cr = match[:, :, :], cross[:, :, :]

            def count_further_items():
                ordered(dve.tensor_scalar(incl, cnt, float(SLOTS), None, ALU.is_gt))
                for k in range(2, SEQ // SLOTS):
                    ordered(dve.scalar_tensor_tensor(incl, cnt, float(SLOTS * k), incl, ALU.is_gt, ALU.add))
                ordered(dve.tensor_copy(excl, incl))
                ordered(dve.tensor_tensor_scan(incl, excl, excl, 0.0, ALU.add, ALU.max))
                ordered(dve.tensor_tensor(excl, incl, excl, ALU.subtract))
                dve.tensor_tensor(mt, by_item, by_expert(excl), ALU.is_ge)
                ordered(dve.tensor_tensor(cr, by_item, by_expert(incl), ALU.is_lt))
                ordered(dve.tensor_tensor(mt, mt, cr, ALU.mult))

            def fill_table():
                ordered(dve.tensor_tensor(cr, mt, by_expert(iota_e[:, 0:NE]), ALU.mult))
                dve.tensor_reduce(ntab[:, 2:2 + M], cr, AX, ALU.add)
                ordered(dve.tensor_copy(ntab[:, 0:1], incl[:, NE - 1:NE]))
                ordered(dve.tensor_scalar(ntab[:, 1:2], ntab[:, 0:1], 0.0, float(QUADS - 1), ALU.is_gt, ALU.add))
                for k in range(1, XQ):
                    ordered(dve.scalar_tensor_tensor(ntab[:, 1:2], ntab[:, 0:1], float(QI * k), ntab[:, 1:2],
                                                     ALU.is_gt, ALU.add))
                dve.tensor_copy(tab[:, :], ntab[:, 0:2 + NX]).then_inc(table_ready, 1)

            def rank_further_items(t):
                ordered(dve.tensor_tensor(cr, by_item, by_expert(excl), ALU.subtract))
                ordered(dve.tensor_scalar(cr, cr, -float(SLOTS), -float(SLOTS), ALU.mult, ALU.add))
                ordered(dve.tensor_tensor(cr, cr, by_expert(rank_item[:, t, 0:NE]), ALU.add))
                ordered(dve.tensor_tensor(cr, cr, mt, ALU.mult))
                ordered(dve.tensor_reduce(rank_item[:, t, NE:NE + M], cr, AX, ALU.add))
                ordered(dve.tensor_tensor(cr, mt, by_expert(gate_item[:, t, 0:NE]), ALU.mult))
                ordered(dve.tensor_reduce(gate_item[:, t, NE:NE + M], cr, AX, ALU.add))

            further = [count_further_items, fill_table, lambda: rank_further_items(0), lambda: rank_further_items(1)]

            def gather_out(q):
                for b in range(4):
                    dve.wait_ge(gath_full, q * 4 + (b + 1))
                    if not isinstance(q, int) and b == 0:
                        dve.wait_ge(piece_used, q * PER_QUAD - 2)
                    dve.tensor_tensor(x_exp[:, 4 * b:4 * b + 4, :],
                                      b_gath[b % 2][:, :].rearrange("p (c s) -> p c s", c=4),
                                      gain_ffn[:, 4 * b:4 * b + 4].unsqueeze(2).to_broadcast([P, 4, P]),
                                      ALU.mult).then_inc(gath_out, 1)

            def accumulate(q, h):
                for b in range(4 * h, 4 * h + 4):
                    t, n = out_block(b)
                    dve.wait_ge(comb_full, q * 8 + (b + 1))
                    dst = x_acc[:, t, n * 512:(n + 1) * 512]
                    dve.tensor_tensor(dst, dst, b_comb[b % 2][:, :], ALU.add).then_inc(acc_done, 1)

            def item_step(q, k, further_quad=False):
                i = q * QI + k
                first = isinstance(q, int) and i == 0
                dve.wait_ge(piece_used, i * PARTS + 4)
                if not first:
                    dve.wait_ge(fold_full, i)
                dve.tensor_copy(up_sb[:, :], b_up[:, :]).then_inc(up_out, 1)
                dve.wait_ge(silu_ready, i + 1)
                if not first:
                    dve.wait_ge(piece_used, i * PARTS)
                dve.tensor_tensor(hidT[:, :, :], silu_sb[:, :, :],
                                  b_fold[:, P:2 * P].rearrange("p (f s) -> p f s", f=FC),
                                  ALU.mult).then_inc(hid_ready, 1)
                for h in range(2):
                    dve.wait_ge(piece_used, i * PARTS + (5 + h))
                    for n in range(2, 4):
                        ins = dve.tensor_copy(y_cols(k, h, n), b_down[h][SLOTS * n:SLOTS * (n + 1), 0:DB])
                    ins.then_inc(y_out_dve, 1)
                if k == QI - 1 and not further_quad:
                    accumulate(q, 0)
                    accumulate(q, 1)

            def quad(q, n_extra=None):
                gather_out(q)
                dve.wait_ge(give_full, q + 1)
                choose(q + 1, q + 2)
                choose_gates(q + 1)
                for k in range(QI):
                    if n_extra is None:
                        item_step(q, k)
                        if isinstance(q, int):
                            further[k]()
                    else:
                        with dve.If(n_extra > (q - QUADS) * QI + k):
                            item_step(q, k, True)
                if n_extra is not None:
                    accumulate(q, 0)
                    accumulate(q, 1)

            quad(0)
            with dve.Fori(1, QUADS) as q:
                quad(q)
            n_extra = dve.value_load(tab[0:1, 0:1], min_val=0, max_val=NX - 1)
            with dve.Fori(QUADS, QUADS + XQ) as q:
                with dve.If(n_extra > (q - QUADS) * QI):
                    quad(q, n_extra)

        @block.tensor
        def _(pe):
            def keep_clock(scratch, n):
                for _ in range(n):
                    pe.matmul(scratch[:, 0:P], ident[:, :], ident[:, :], start=True, stop=True)

            pe.wait_ge(consts_ready, 2)
            keep_clock(bank[0], 34)
            for t in reversed(range(TILES)):
                pe.wait_ge((h0_ready, h1_ready)[t], 1)
                for j in range(KC // 2):
                    for c in range(2):
                        ins = pe.transpose(bank[j][:, c * SEQ + t * P:c * SEQ + (t + 1) * P],
                                           h_perm[:, t, 2 * j + c, :], ident[:, :])
                    if t == 0:
                        ins.then_inc(hT_full, 1)

            def piece(n, parity, kind):
                if not (isinstance(n, int) and n < 2):
                    pe.wait_ge(proj_free, n - 1)
                for k in range(4):
                    pe.wait_ge(lo_ready, n * 4 + (k + 1))
                    if isinstance(n, int) and n == 0:
                        pe.wait_ge(hT_ready, 2 * k + 2)
                    if isinstance(n, int) and n == N_IN - 1 and k == 1:
                        yb_sums(0)
                    if isinstance(n, int) and n == N_IN:
                        if k == 1:
                            yb_sums(1)
                        pe.wait_ge(y_split, k + 1)
                    for cc in range(4):
                        c = 4 * k + cc
                        for b in range(2):
                            dst = bank[2 * parity + b][:, 0:PW]
                            hi, lo = w_hi[:, k, cc, :], w_lo[:, k, cc, :]
                            cols = slice(b * P, (b + 1) * P)
                            if kind == "w":
                                trio = [(hi[:, cols], hT_hi[:, c, :]), (hi[:, cols], hT_lo[:, c, :]),
                                        (lo[:, cols], hT_hi[:, c, :])]
                            else:
                                a_hi, a_lo = (y_hi, y_lo) if kind == "y" else (hT_hi, hT_lo)
                                trio = [(a_hi[:, c, cols], hi), (a_hi[:, c, cols], lo), (a_lo[:, c, cols], hi)]
                            for j, (stationary, moving) in enumerate(trio):
                                ins = pe.matmul(dst, stationary, moving, start=(k == 0 and cc == 0 and j == 0),
                                                stop=(k == 3 and cc == 3 and j == 2))
                    ins.then_inc(quarter_used, 1)

            def pieces(first, last, kind):
                with pe.Fori(first, last, 2) as n:
                    piece(n, first % 2, kind)
                    piece(n + 1, (first + 1) % 2, kind)

            def use(u):
                if u >= 4:
                    pe.wait_ge(aux_free, u - 3)
                return aux(u)

            def sums(u, squares):
                for b in range(2):
                    ins = pe.matmul(use(u)[:, b * SEQ:(b + 1) * SEQ], ones[:, :], squares[:, b, :], start=True, stop=True)
                ins.then_inc(aux_full, 1)

            def yb_sums(j):
                pe.wait_ge(y_sq, (HC + HA) // 2 + j + 1)
                sums(U_YB + j, proj[:, BLK_CG + 2 * j:BLK_CG + 2 * j + 2, :])

            piece(0, 0, "w")
            pe.wait_ge(par_in, PARS)
            pe.transpose(aux(U_PRM)[:, 0:P], prm_rows[:, :], ident[:, :]).then_inc(aux_full, 1)
            piece(1, 1, "w")
            def qk_sums(pairs):
                for j in pairs:
                    pe.wait_ge(qk_sq, j + 1)
                    sums(U_QK + j, temp[:, 2 * j:2 * j + 2, :])

            def stick_scores(b):
                u = U_Z + 2 * b
                for h in range(2):
                    q, k = proj[:, BLK_Q + 2 * b + h, :], proj[:, BLK_K + 2 * b + h, :]
                    ins = pe.matmul(use(u)[:, h * SEQ:(h + 1) * SEQ], q[:, P:2 * P], k, start=True, stop=True)
                ins.then_inc(aux_full, 1)
                for h in range(2):
                    q, k = proj[:, BLK_Q + 2 * b + h, :], proj[:, BLK_K + 2 * b + h, :]
                    ins = pe.matmul(use(u + 1)[:, h * P:(h + 1) * P], q[:, 0:P], k[:, 0:P], start=True, stop=True)
                ins.then_inc(aux_full, 1)

            def lru_gates(heads):
                for h in heads:
                    for g in range(2):
                        ins = pe.matmul(use(U_LRU + h)[:, g * SEQ:(g + 1) * SEQ], lru_w[:, g, h, :], conv_a[:, h, :],
                                        start=True, stop=True)
                    ins.then_inc(aux_full, 1)

            pieces(2, 6, "w")
            qk_sums(range(0, 4))
            pieces(6, 8, "w")
            qk_sums(range(4, HC))
            piece(8, 0, "w")
            piece(9, 1, "h")
            piece(10, 0, "h")
            pe.wait_ge(qk_ready, HC)
            stick_scores(0)
            stick_scores(1)
            piece(11, 1, "h")
            stick_scores(2)
            piece(12, 0, "w")
            pe.wait_ge(conv_ready, HA // 2)
            pe.wait_ge(lru_in, 32)
            lru_gates(range(0, 4))
            piece(13, 1, "w")
            lru_gates(range(4, HA))
            pieces(14, 16, "w")
            for h in range(HC):
                w = scores[h // 2][:, 0, h % 2, :]
                pe.wait_ge(w_ready, h // 2 + 1)
                for k in range(3):
                    ins = pe.transpose(use(U_WT + h)[:, k * P:(k + 1) * P], w[:, k * P:(k + 1) * P], ident[:, :])
                ins.then_inc(aux_full, 1)
            piece(16, 0, "w")
            for b in range(HC // 2):
                for hh in range(2):
                    h = 2 * b + hh
                    wT = scores[b][:, 1, hh, :]
                    pe.wait_ge(aux_free, U_WT + h + 1)
                    dst = use(U_PV + b)
                    pe.matmul(dst[:, hh * SEQ:(hh + 1) * SEQ], v_tok[:, 0, h * P:(h + 1) * P], wT[:, 0:SEQ],
                              start=True, stop=False)
                    ins = pe.matmul(dst[:, hh * SEQ + P:(hh + 1) * SEQ], v_tok[:, 1, h * P:(h + 1) * P],
                                    wT[:, SEQ:SEQ + P], start=False, stop=True)
                ins.then_inc(aux_full, 1)
            pieces(17, 19, "w")
            for j in range(HC // 2):
                pe.wait_ge(y_sq, j + 1)
                sums(U_YC + j, proj[:, BLK_K + 2 * j:BLK_K + 2 * j + 2, :])
            piece(19, 1, "w")
            for j in range(HA // 2):
                pe.wait_ge(y_sq, HC // 2 + j + 1)
                sums(U_YA + j, proj[:, BLK_XA + 2 * j:BLK_XA + 2 * j + 2, :])
            piece(20, 0, "w")

            NR = NG + NE
            logits_bank = bank[AUX + 2]

            def transpose_x2(k):
                pe.wait_ge(proj_free, N_IN + k + 1)
                if k == 0:
                    pe.wait_ge(aux_free, U_END)
                if k >= 2:
                    pe.wait_ge(x2T_ready, k - 1)
                for c in range(2):
                    for t in range(TILES):
                        ins = pe.transpose(bank[AUX + k % 2][:, c * SEQ + t * P:c * SEQ + (t + 1) * P],
                                           x_acc[:, t, (2 * k + c) * P:(2 * k + c + 1) * P], ident[:, :])
                ins.then_inc(x2T_full, 1)

            def logits(k):
                pe.wait_ge(x2T_ready, k + 1)
                for c in range(2):
                    ins = pe.matmul(logits_bank[0:NR, 0:SEQ], w_rt[:, 2 * k + c, :], x2T[:, k % 2, c, :],
                                    start=(k == 0 and c == 0), stop=(k == N_OUT - 1 and c == 1))
                ins.then_inc(x2T_used if k < N_OUT - 1 else logitsT_full, 1)

            pe.wait_ge(router_in, ROUTER_PARS)
            for k in range(N_OUT):
                piece(N_IN + k, (N_IN + k) % 2, "y")
                if k >= 1:
                    transpose_x2(k - 1)
                if k >= 2:
                    logits(k - 2)
            transpose_x2(N_OUT - 1)
            logits(N_OUT - 2)
            logits(N_OUT - 1)
            pe.wait_ge(logitsT_ready, 1)
            for t in range(TILES):
                ins = pe.transpose(bank[AUX + 3][:, t * NR:(t + 1) * NR], logitsT[0:NR, t * P:(t + 1) * P],
                                   ident[0:NR, 0:NR])
            ins.then_inc(logits_full, 1)
            keep_clock(bank[0], 20)
            pe.wait_ge(sel_ready, 1)
            pe.matmul(bank[5][:, 0:NE], before[:, :], sel_b[:, 0, :], start=True, stop=True)
            pe.matmul(bank[5][:, NE:2 * NE], ones_b[:, :], sel_b[:, 0, :], start=True, stop=False)
            pe.matmul(bank[5][:, NE:2 * NE], before[:, :], sel_b[:, 1, :], start=False, stop=True)
            pe.matmul(bank[5][:, 2 * NE:3 * NE], ones_b[:, :], sel_b[:, 0, :], start=True, stop=False)
            pe.matmul(bank[5][:, 2 * NE:3 * NE], ones_b[:, :], sel_b[:, 1, :], start=False, stop=True).then_inc(rank_full, 1)

            keep_clock(bank[0], 10)

            def outputs_written(q, k, h):
                pe.wait_ge(y_out_act, q * (2 * QI) + (2 * k + h + 1))
                pe.wait_ge(y_out_dve, q * (2 * QI) + (2 * k + h + 1))

            def combine(q, h):
                for b in range(4 * h, 4 * h + 4):
                    if not (isinstance(q, int) and b < 2):
                        pe.wait_ge(acc_done, q * 8 + (b - 1))
                    t, n = out_block(b)
                    pe.matmul(b_comb[b % 2][:, :], give[:, t, :], y_exp[:, n * 512:(n + 1) * 512],
                              start=True, stop=True).then_inc(comb_full, 1)

            def gather(q, blocks=range(4)):
                if isinstance(q, int):
                    pe.wait_ge(x2_perm_ready, N_OUT)
                pe.wait_ge(pick_ready, q + 1)
                for b in blocks:
                    if not (isinstance(q, int) and b < 2):
                        pe.wait_ge(gath_out, q * 4 + (b - 1))
                    for c in range(4):
                        for t in range(TILES):
                            ins = pe.matmul(b_gath[b % 2][:, c * P:(c + 1) * P], x2_perm[:, t, 4 * b + c, :],
                                            pick[:, t].rearrange("p i s -> p (i s)"), start=(t == 0), stop=(t == 1))
                    ins.then_inc(gath_full, 1)

            def transpose_gates(q):
                pe.wait_ge(pick_gate_ready, q + 1)
                if not isinstance(q, int):
                    pe.wait_ge(give_ready, q)
                    pe.wait_ge(hid_ready, q * QI)
                for t in range(TILES):
                    ins = pe.transpose(b_fold[:, (2 + t) * P:(3 + t) * P],
                                       pick_gate[:, t].rearrange("p i s -> p (i s)"), ident[:, :])
                ins.then_inc(give_full, 1)

            def item_step(q, k, further_quad=False):
                i = q * QI + k
                first = isinstance(q, int) and i == 0
                cols = slice(SLOTS * k, SLOTS * (k + 1))
                for p in range(4):
                    if first and p == 2:
                        gather(q, range(2, 4))
                        transpose_gates(q)
                    weights = ring[place_of(k, p)]
                    pe.wait_ge(piece_in[place_of(k, p)], piece_count(q, k, p))
                    dst = (b_gate, b_up)[p % 2]
                    if p < 2 and not first:
                        pe.wait_ge((gate_out, up_out)[p], i)
                    for cc in range(H):
                        c = (p // 2) * H + cc
                        j = c % 4
                        if k == 0 and p % 2 == 0 and j == 0:
                            pe.wait_ge(gath_out, q * 4 + (c // 4 + 1))
                        ins = pe.matmul(dst[SLOTS * j:SLOTS * (j + 1), :], x_exp[:, c, cols],
                                        weights[:, cc * F:(cc + 1) * F], start=(c < 4), stop=(c >= KC - 4))
                    ins.then_inc(piece_used, 1)
                if k == QI - 1:
                    keep_clock(bank[5], 5)
                pe.wait_ge(gate_out, i + 1)
                pe.wait_ge(up_out, i + 1)
                if not first:
                    pe.wait_ge(hid_ready, i)
                if k == 0:
                    pe.wait_ge(give_ready, q + 1)
                for m, part in enumerate((gate_sb, up_sb)):
                    for f in range(FC):
                        ins = pe.matmul(b_fold[:, m * P + f * SLOTS:m * P + (f + 1) * SLOTS],
                                        part[:, :].rearrange("p (k f) -> p f k", f=FC)[:, f, :], fold[:, :],
                                        start=True, stop=True)
                ins.then_inc(fold_full, 1)
                if k == QI - 1:
                    keep_clock(bank[5], 6)
                pe.wait_ge(hid_ready, i + 1)
                for h in range(2):
                    if not first:
                        pe.wait_ge(y_out_act, q * (2 * QI) + (2 * k + h - 1))
                        pe.wait_ge(y_out_dve, q * (2 * QI) + (2 * k + h - 1))
                    weights = ring[place_of(k, 4 + h)]
                    pe.wait_ge(piece_in[place_of(k, 4 + h)], piece_count(q, k, 4 + h))
                    for f in range(FC):
                        for n in range(4):
                            ins = pe.matmul(b_down[h][SLOTS * n:SLOTS * (n + 1), 0:DB], hidT[:, f, :],
                                            weights[:, f * (D // 2) + n * DB:f * (D // 2) + (n + 1) * DB],
                                            start=(f == 0), stop=(f == FC - 1))
                    ins.then_inc(piece_used, 1)
                if k == QI - 1 and not further_quad:
                    outputs_written(q, k, 0)
                    combine(q, 0)
                if k == QI - 1 or further_quad:
                    outputs_written(q, k, 1)
                if k == QI - 1 and not further_quad:
                    combine(q, 1)

            def quad(q, n_extra=None):
                if isinstance(q, int):
                    gather(q, range(2))
                else:
                    gather(q)
                    transpose_gates(q)
                for k in range(QI):
                    if n_extra is None:
                        item_step(q, k)
                    else:
                        with pe.If(n_extra > (q - QUADS) * QI + k):
                            item_step(q, k, True)
                if n_extra is not None:
                    combine(q, 0)
                    combine(q, 1)

            quad(0)
            with pe.Fori(1, QUADS) as q:
                quad(q)
            pe.wait_ge(table_ready, 1)
            n_extra = pe.value_load(tab[0:1, 0:1], min_val=0, max_val=NX - 1)
            with pe.Fori(QUADS, QUADS + XQ) as q:
                with pe.If(n_extra > (q - QUADS) * QI):
                    quad(q, n_extra)


_INS = ['x', 'norm_mix', 'w_in', 'conv_a_w', 'conv_a_b', 'lru_wa', 'lru_ba', 'lru_wx', 'lru_bx', 'lru_lam',
        'conv_b_w', 'q_norm', 'k_norm', 'mix_norm', 'w_out', 'norm_ffn', 'w_router_group', 'b_router_group',
        'w_router_expert', 'b_router_expert', 'w_gate', 'w_up', 'w_down']


def kernel(**inputs):
    import concourse.bacc as _bacc
    from concourse.bass_utils import run_bass_kernel_spmd as _run

    nc = _bacc.Bacc("TRN2", target_bir_lowering=False, num_devices=1)
    arrays, args = {}, []
    for name in _INS:
        a = np.ascontiguousarray(inputs[name])
        arrays[f"in_{name}"] = a
        args.append(nc.dram_tensor(f"in_{name}", a.shape, mybir.dt.from_np(a.dtype), kind="ExternalInput").ap())
    args.append(nc.dram_tensor("out_0", inputs["x"].shape, F32, kind="ExternalOutput").ap())
    hymba_layer(nc, *args)
    r = _run(nc, [arrays], core_ids=[0])
    return r.results[0]["out_0"]
```
